# Optimizing a Trainium2 kernel written in Bass

```python
import jax, jax.numpy as jnp
from jax import lax
import numpy as np

D_MODEL = 1024
BATCH = 1
SEQ = 2048
DEPTH = 1

N_MIXERS = 2
N_LRU = (DEPTH + N_MIXERS - 1) // N_MIXERS
N_SSD = DEPTH // N_MIXERS
CONV_W = 4
EPS = 1e-6
LRU_WIDTH = D_MODEL
LRU_HEADS = 8
LRU_BLOCK = LRU_WIDTH // LRU_HEADS
LRU_C = 8.0
SSD_D_INNER = 2 * D_MODEL
SSD_HEAD_DIM = 64
SSD_HEADS = SSD_D_INNER // SSD_HEAD_DIM
SSD_GROUPS = 4
SSD_HPG = SSD_HEADS // SSD_GROUPS
SSD_STATE = 128
SSD_CHUNK = 128
SSD_CONV_DIM = SSD_D_INNER + 2 * SSD_GROUPS * SSD_STATE
SSD_IN_DIM = SSD_D_INNER + SSD_CONV_DIM + SSD_HEADS
N_EXPERTS = 16
N_EXPERT_GROUPS = 4
EXPERTS_PER_GROUP = N_EXPERTS // N_EXPERT_GROUPS
TOP_K = 2
D_EXPERT = D_MODEL // 4

kernel_name = "hybrid_rglru_ssd_grouped_moe_adaln"

def rmsnorm(x, g):
    xf = x.astype(jnp.float32)
    y = xf * lax.rsqrt(jnp.mean(xf * xf, axis=-1, keepdims=True) + EPS)
    return (y * g.astype(jnp.float32)).astype(x.dtype)

def modulate(h, shift, scale):
    return h * (1.0 + scale[:, None, :]) + shift[:, None, :]

def causal_dwconv(x, w, b):
    k, ch = w.shape
    y = lax.conv_general_dilated(x, w[:, None, :].astype(x.dtype), window_strides=(1,),
                                 padding=[(k - 1, 0)], dimension_numbers=('NWC', 'WIO', 'NWC'),
                                 feature_group_count=ch)
    return y + b.astype(y.dtype)

def _lin_combine(left, right):
    a_l, b_l = left
    a_r, b_r = right
    return a_l * a_r, a_r * b_l + b_r

def rglru_mixer(h, w_in, conv_w, conv_b, wa, ba, wx, bx, lam, w_out):
    bsz, s, _ = h.shape
    u = h @ w_in
    gate_br, x_br = u[..., :LRU_WIDTH], u[..., LRU_WIDTH:]
    x_br = causal_dwconv(x_br, conv_w, conv_b)
    xb = x_br.astype(jnp.float32).reshape(bsz, s, LRU_HEADS, LRU_BLOCK)
    r = jax.nn.sigmoid(jnp.einsum('bshi,hij->bshj', xb, wa.astype(jnp.float32)) + ba.astype(jnp.float32).reshape(LRU_HEADS, LRU_BLOCK))
    i = jax.nn.sigmoid(jnp.einsum('bshi,hij->bshj', xb, wx.astype(jnp.float32)) + bx.astype(jnp.float32).reshape(LRU_HEADS, LRU_BLOCK))
    log_a = -LRU_C * r * jax.nn.softplus(-lam.astype(jnp.float32)).reshape(LRU_HEADS, LRU_BLOCK)
    a = jnp.exp(log_a)
    b = jnp.sqrt(-jnp.expm1(2.0 * log_a)) * (i * xb)
    _, hs = lax.associative_scan(_lin_combine, (a, b), axis=1)
    y = hs.reshape(bsz, s, LRU_WIDTH).astype(h.dtype) * jax.nn.gelu(gate_br, approximate=True)
    return y @ w_out

def ssd_mixer(h, w_in, conv_w, conv_b, dt_bias, a_log, d_skip, norm_g, w_out):
    bsz, s, _ = h.shape
    f32 = jnp.float32
    nc, L, G, E, P, N = s // SSD_CHUNK, SSD_CHUNK, SSD_GROUPS, SSD_HPG, SSD_HEAD_DIM, SSD_STATE
    proj = h @ w_in
    z = proj[..., :SSD_D_INNER]
    xbc = proj[..., SSD_D_INNER:SSD_D_INNER + SSD_CONV_DIM]
    dt = proj[..., SSD_D_INNER + SSD_CONV_DIM:]
    xbc = jax.nn.silu(causal_dwconv(xbc, conv_w, conv_b))
    xs = xbc[..., :SSD_D_INNER].astype(f32)
    Bm = xbc[..., SSD_D_INNER:SSD_D_INNER + G * N].astype(f32)
    Cm = xbc[..., SSD_D_INNER + G * N:].astype(f32)
    dt = jax.nn.softplus(dt.astype(f32) + dt_bias.astype(f32))
    A = -jnp.exp(a_log.astype(f32))
    xh = xs.reshape(bsz, s, SSD_HEADS, P)
    X = (xh * dt[..., None]).reshape(bsz, nc, L, G, E, P)
    dA = (dt * A).reshape(bsz, nc, L, G, E)
    Bc = Bm.reshape(bsz, nc, L, G, N)
    Cc = Cm.reshape(bsz, nc, L, G, N)
    Acs = jnp.cumsum(dA, axis=2)
    Acs_t = jnp.moveaxis(Acs, 2, -1)
    diff = Acs_t[..., :, None] - Acs_t[..., None, :]
    causal = jnp.tril(jnp.ones((L, L), dtype=bool))
    Lmat = jnp.exp(jnp.where(causal, diff, -jnp.inf))
    CB = jnp.einsum('bclgn,bcsgn->bcgls', Cc, Bc)
    y_diag = jnp.einsum('bcgels,bcsgep->bclgep', CB[:, :, :, None] * Lmat, X)
    decay_states = jnp.exp(Acs[:, :, -1:] - Acs)
    states = jnp.einsum('bclgn,bclge,bclgep->bcgepn', Bc, decay_states, X)
    chunk_decay = jnp.exp(Acs[:, :, -1])

    def step(carry, inp):
        st, dec = inp
        return carry * dec[..., None, None] + st, carry

    init = jnp.zeros((bsz, G, E, P, N), f32)
    _, prev = lax.scan(step, init, (jnp.moveaxis(states, 1, 0), jnp.moveaxis(chunk_decay, 1, 0)))
    prev = jnp.moveaxis(prev, 0, 1)
    y_off = jnp.einsum('bclgn,bcgepn,bclge->bclgep', Cc, prev, jnp.exp(Acs))
    y = (y_diag + y_off).reshape(bsz, s, SSD_HEADS, P) + d_skip.astype(f32)[:, None] * xh
    y = y.reshape(bsz, s, SSD_D_INNER) * jax.nn.silu(z.astype(f32))
    yg = y.reshape(bsz, s, G, SSD_D_INNER // G)
    yg = yg * lax.rsqrt(jnp.mean(yg * yg, axis=-1, keepdims=True) + EPS)
    y = yg.reshape(bsz, s, SSD_D_INNER) * norm_g.astype(f32)
    return y.astype(h.dtype) @ w_out

def grouped_moe(h, router_w, router_b, w_gate, w_up, w_down):
    bsz, s, _ = h.shape
    logits = h.astype(jnp.float32) @ router_w.astype(jnp.float32) + router_b.astype(jnp.float32)
    probs = jax.nn.softmax(logits, axis=-1)
    pg = probs.reshape(bsz, s, N_EXPERT_GROUPS, EXPERTS_PER_GROUP)
    group_score = lax.top_k(pg, TOP_K)[0].sum(-1)
    best = jnp.argmax(group_score, axis=-1)
    in_group = (jnp.arange(N_EXPERTS) // EXPERTS_PER_GROUP)[None, None, :] == best[..., None]
    masked = jnp.where(in_group, probs, -jnp.inf)
    top_vals, top_idx = lax.top_k(masked, TOP_K)
    top_w = top_vals / jnp.sum(top_vals, axis=-1, keepdims=True)
    gates = jnp.sum(jax.nn.one_hot(top_idx, N_EXPERTS, dtype=jnp.float32) * top_w[..., None], axis=-2)
    g = jnp.einsum('bsd,edf->bsef', h, w_gate)
    u = jnp.einsum('bsd,edf->bsef', h, w_up)
    act = jax.nn.silu(g) * u * gates.astype(g.dtype)[..., None]
    out = jnp.einsum('bsef,efd->bsd', act, w_down)
    return out.astype(h.dtype)

def setup_inputs(seed: int = 0) -> dict:
    key = jax.random.key(seed)
    ks = jax.random.split(key, 40)
    f32 = jnp.float32
    nrm = lambda k, shape, sc: jax.random.normal(k, shape, f32) * sc
    D = D_MODEL
    a0 = jax.random.uniform(ks[12], (N_LRU, LRU_WIDTH), f32, 0.9, 0.999)
    dt0 = jnp.exp(jax.random.uniform(ks[20], (N_SSD, SSD_HEADS), f32, np.log(1e-3), np.log(1e-1)))
    return {
        'x': nrm(ks[0], (BATCH, SEQ, D), 1.0),
        'c': nrm(ks[1], (BATCH, D), 1.0),
        'ada_w': nrm(ks[2], (DEPTH, D, 6 * D), 0.5 * D ** -0.5),
        'ada_b': nrm(ks[3], (DEPTH, 6 * D), 0.02),
        'norm1_g': 1.0 + nrm(ks[4], (DEPTH, D), 0.05),
        'norm2_g': 1.0 + nrm(ks[5], (DEPTH, D), 0.05),
        'lru_w_in': nrm(ks[6], (N_LRU, D, 2 * LRU_WIDTH), D ** -0.5),
        'lru_conv_w': nrm(ks[7], (N_LRU, CONV_W, LRU_WIDTH), CONV_W ** -0.5),
        'lru_conv_b': nrm(ks[8], (N_LRU, LRU_WIDTH), 0.02),
        'lru_wa': nrm(ks[9], (N_LRU, LRU_HEADS, LRU_BLOCK, LRU_BLOCK), LRU_BLOCK ** -0.5),
        'lru_ba': nrm(ks[10], (N_LRU, LRU_WIDTH), 0.02),
        'lru_wx': nrm(ks[11], (N_LRU, LRU_HEADS, LRU_BLOCK, LRU_BLOCK), LRU_BLOCK ** -0.5),
        'lru_bx': nrm(ks[13], (N_LRU, LRU_WIDTH), 0.02),
        'lru_lambda': jnp.log(a0) - jnp.log1p(-a0),
        'lru_w_out': nrm(ks[14], (N_LRU, LRU_WIDTH, D), LRU_WIDTH ** -0.5),
        'ssd_w_in': nrm(ks[15], (N_SSD, D, SSD_IN_DIM), D ** -0.5),
        'ssd_conv_w': nrm(ks[16], (N_SSD, CONV_W, SSD_CONV_DIM), CONV_W ** -0.5),
        'ssd_conv_b': nrm(ks[17], (N_SSD, SSD_CONV_DIM), 0.02),
        'ssd_dt_bias': dt0 + jnp.log(-jnp.expm1(-dt0)),
        'ssd_a_log': jnp.log(jax.random.uniform(ks[18], (N_SSD, SSD_HEADS), f32, 1.0, 16.0)),
        'ssd_d': 1.0 + nrm(ks[19], (N_SSD, SSD_HEADS), 0.1),
        'ssd_norm_g': 1.0 + nrm(ks[21], (N_SSD, SSD_D_INNER), 0.05),
        'ssd_w_out': nrm(ks[22], (N_SSD, SSD_D_INNER, D), SSD_D_INNER ** -0.5),
        'router_w': nrm(ks[23], (D, N_EXPERTS), D ** -0.5),
        'router_b': nrm(ks[24], (N_EXPERTS,), 0.01),
        'moe_w_gate': nrm(ks[25], (DEPTH, N_EXPERTS, D, D_EXPERT), D ** -0.5),
        'moe_w_up': nrm(ks[26], (DEPTH, N_EXPERTS, D, D_EXPERT), D ** -0.5),
        'moe_w_down': nrm(ks[27], (DEPTH, N_EXPERTS, D_EXPERT, D), D_EXPERT ** -0.5),
        'final_norm_g': 1.0 + nrm(ks[28], (D,), 0.05),
    }

def reference(x, c, ada_w, ada_b, norm1_g, norm2_g,
              lru_w_in, lru_conv_w, lru_conv_b, lru_wa, lru_ba, lru_wx, lru_bx, lru_lambda, lru_w_out,
              ssd_w_in, ssd_conv_w, ssd_conv_b, ssd_dt_bias, ssd_a_log, ssd_d, ssd_norm_g, ssd_w_out,
              router_w, router_b, moe_w_gate, moe_w_up, moe_w_down, final_norm_g):
    cond = jax.nn.silu(c)
    for i in range(DEPTH):
        mod = cond @ ada_w[i] + ada_b[i]
        sh1, sc1, g1, sh2, sc2, g2 = jnp.split(mod, 6, axis=-1)
        hn = modulate(rmsnorm(x, norm1_g[i]), sh1, sc1)
        j = i // N_MIXERS
        if i % N_MIXERS == 0:
            y = rglru_mixer(hn, lru_w_in[j], lru_conv_w[j], lru_conv_b[j], lru_wa[j], lru_ba[j],
                            lru_wx[j], lru_bx[j], lru_lambda[j], lru_w_out[j])
        else:
            y = ssd_mixer(hn, ssd_w_in[j], ssd_conv_w[j], ssd_conv_b[j], ssd_dt_bias[j], ssd_a_log[j],
                          ssd_d[j], ssd_norm_g[j], ssd_w_out[j])
        x = x + g1[:, None, :] * y
        hn = modulate(rmsnorm(x, norm2_g[i]), sh2, sc2)
        x = x + g2[:, None, :] * grouped_moe(hn, router_w, router_b, moe_w_gate[i], moe_w_up[i], moe_w_down[i])
    return rmsnorm(x, final_norm_g)


_drawn_inputs = setup_inputs


def setup_inputs(seed=0):
    import zlib

    import numpy as np

    out = dict(_drawn_inputs(seed))
    spreads = {}
    factors = {'lru_conv_b': 3.21, 'lru_ba': 33.713, 'lru_bx': 21.62, 'router_b': 3.142}
    for name, (base, spread) in spreads.items():
        noise = np.random.default_rng([zlib.crc32(name.encode()), seed]).standard_normal(out[name].shape)
        drawn = base * np.exp(spread * noise) if base else spread * noise
        out[name] = __import__('jax').numpy.asarray(drawn.astype(out[name].dtype))
    for name, factor in factors.items():
        out[name] = (out[name] * factor).astype(out[name].dtype)
    return out
```

```python
import concourse.bass as bass
from concourse import mybir
from contextlib import ExitStack

F32 = mybir.dt.float32
F32R = mybir.dt.float32r
I32 = mybir.dt.int32
ALU = mybir.AluOpType
ACT = mybir.ActivationFunctionType
AX = mybir.AxisListType
ds = bass.ds

P = 128
D = 1024
S = 2048
KD = D // P
NT = S // P
NB = 512
EPS = 1e-6
LRU_C = 8.0
CONV = 4
HALF = S // 2
E = 16
G = 4
PER = E // G
FE = 256
TOPK = 2
MAXB = S * TOPK // P + E
LEAD = 3
WE = KD * 2 * FE + FE // P * D


def at_least(it, k):
    return not isinstance(it, int) or it >= k


def pipelined(eng, n, ramp, stages):
    def step(s):
        for stage, lag in stages:
            if 0 <= s - lag < n:
                stage(s - lag, (s - lag) % 2)
    for s in range(ramp):
        step(s)
    with eng.Fori(0, (n - ramp) // 2) as i:
        for u in range(2):
            for stage, lag in stages:
                stage(2 * i + (ramp + u - lag), (u - lag) % 2)
    for s in range(n, n + max(lag for _, lag in stages)):
        step(s)


def norm_and_transpose(nc, sem, cst, io, hT_hi, hT_lo, cond):
    ctx = ExitStack()
    with ctx:
        sb = lambda n, s, d=F32: ctx.enter_context(nc.sbuf_tensor(n, s, d))
        ps = lambda n, s: ctx.enter_context(nc.psum_tensor(n, s, F32))
        ada = sb("n_ada", [P, 2, KD, NB])
        acc = sb("n_acc", [P, 2, NB])
        brow = sb("n_brow", [P, 2, D])
        gain = sb("n_gain", [P, D])
        ct = sb("n_c", [P, KD])
        cth = sb("n_cth", [P, KD])
        xt = sb("n_x", [P, 2, D])
        junk = acc[:].rearrange("p a b -> p (a b)")
        hn = sb("n_hn", [P, 2, D])
        ssq = sb("n_ssq", [P, 2])
        std = sb("n_std", [P, 2])
        rstd = sb("n_rstd", [P, 2])
        pm = [ps("n_pm0", [P, NB]), ps("n_pm1", [P, NB])]
        pt = [ps("n_pt0", [P, D]), ps("n_pt1", [P, D])]

        c_in, rows_in = sem("c_in"), sem("rows_in")
        ada_in = [sem("ada_in0"), sem("ada_in1")]
        x_in = [sem("x_in0"), sem("x_in1")]
        cth_ready, cond_ready = sem("cth_ready"), sem("cond_ready")
        acc_step, summed, row_ready = sem("acc_step"), sem("summed"), sem("row_ready")
        ssq_ready, std_ready, rstd_ready = sem("ssq_ready"), sem("std_ready"), sem("rstd_ready")
        scaled, shifted, turned = sem("scaled"), sem("shifted"), sem("turned")
        hi_ready, lo_ready = sem("hi_ready"), sem("lo_ready")

        ada_v = io["ada_w"][0].rearrange("(p k) n -> p k n", k=KD)
        NCH = 2 * D // NB
        block = ctx.enter_context(nc.Block())

        @block.sync
        def _(sp):
            sp.dma_start(ct[:], io["c"][0].rearrange("(p k) -> p k", k=KD)).then_inc(c_in, 16)
            for n in range(2):
                sp.dma_start(ada[:, n], ada_v[:, :, n * NB:(n + 1) * NB]).then_inc(ada_in[n], 16)
            sp.dma_start(brow[:], io["ada_b"][0, 0:2 * D].partition_broadcast(P)
                         .rearrange("p (a n) -> p a n", a=2)).then_inc(rows_in, 16)
            sp.dma_start(gain[:], io["norm1_g"][0].partition_broadcast(P)).then_inc(rows_in, 16)
            for n in range(2, NCH):
                sp.wait_ge(acc_step, KD * (n - 1))
                sp.dma_start(ada[:, n % 2], ada_v[:, :, n * NB:(n + 1) * NB]).then_inc(ada_in[n % 2], 16)

            def load(it, u):
                if at_least(it, 2):
                    sp.wait_ge(scaled, it - 1)
                sp.dma_start(xt[:, u], io["x"][0, ds(it * P, P), :]).then_inc(x_in[u], 16)
            pipelined(sp, NT, 2, [(load, 0)])

        @block.scalar
        def _(act):
            act.wait_ge(c_in, 16)
            nc.scalar.activation(cth[:], ct[:], ACT.Tanh, scale=0.5).then_inc(cth_ready, 1)

            def squares(it, u):
                act.wait_ge(x_in[u], it * 8 + 16 - u * 8)
                if at_least(it, 2):
                    act.wait_ge(rstd_ready, it - 1)
                nc.scalar.activation(junk, xt[:, u], ACT.Square, accum_out=ssq[:, u:u + 1]).then_inc(ssq_ready, 1)
                act.wait_ge(ssq_ready, it + 1)
                nc.scalar.activation(std[:, u:u + 1], ssq[:, u:u + 1], ACT.Sqrt, scale=1.0 / D,
                                     bias=cst["eps"][:]).then_inc(std_ready, 1)

            def high(it, u):
                act.wait_ge(turned, it + 1)
                act.nop(nofuse=True)
                nc.scalar.activation(hT_hi[:, :, ds(it * P, P)], pt[u][:].rearrange("p (k n) -> p k n", k=KD),
                                     ACT.Copy).then_inc(hi_ready, 1)
            act.wait_ge(row_ready, NCH)
            pipelined(act, NT, 4, [(squares, 0), (high, 2)])

        @block.vector
        def _(dve):
            dve.wait_ge(cth_ready, 1)
            nc.vector.scalar_tensor_tensor(cond[:], cth[:], 1.0, ct[:], ALU.add, ALU.mult).then_inc(cond_ready, 1)
            dve.wait_ge(cond_ready, 1)
            nc.vector.tensor_scalar(cond[:], cond[:], 0.5, None, ALU.mult).then_inc(cond_ready, 1)
            dve.wait_ge(cond_ready, 2)
            dve.wait_ge(rows_in, 32)
            for n in range(NCH):
                a = acc[:, n % 2, :]
                dve.wait_ge(ada_in[n % 2], 16 * (n // 2 + 1))
                if n >= 2:
                    dve.wait_ge(summed, n - 1)
                nc.vector.tensor_scalar(a, ada[:, n % 2, 0, :], cond[:, 0:1], None, ALU.mult).then_inc(acc_step, 1)
                for k in range(1, KD):
                    dve.wait_ge(acc_step, KD * n + k)
                    nc.vector.scalar_tensor_tensor(a, ada[:, n % 2, k, :], cond[:, k:k + 1], a,
                                                   ALU.mult, ALU.add).then_inc(acc_step, 1)
            for n in range(NCH):
                row, cols = n * NB // D, ds(n * NB % D, NB)
                dve.wait_ge(summed, n + 1)
                if row == 0:
                    nc.vector.tensor_tensor(brow[:, 0, cols], pm[n % 2][:], brow[:, 0, cols], ALU.add).then_inc(row_ready, 1)
                else:
                    nc.vector.tensor_tensor(brow[:, 1, cols], pm[n % 2][:], brow[:, 1, cols], ALU.add).then_inc(cond_ready, 1)
                    dve.wait_ge(cond_ready, 1 + n)
                    nc.vector.scalar_tensor_tensor(brow[:, 1, cols], brow[:, 1, cols], 1.0, gain[:, cols],
                                                   ALU.add, ALU.mult).then_inc(row_ready, 1)
            dve.wait_ge(row_ready, NCH)

            def scale(it, u):
                dve.wait_ge(std_ready, it + 1)
                if at_least(it, 2):
                    dve.wait_ge(turned, it - 1)
                nc.vector.reciprocal(rstd[:, u:u + 1], std[:, u:u + 1]).then_inc(rstd_ready, 1)
                dve.wait_ge(rstd_ready, it + 1)
                nc.vector.scalar_tensor_tensor(hn[:, u], xt[:, u], rstd[:, u:u + 1], brow[:, 1], ALU.mult,
                                               ALU.mult).then_inc(scaled, 1)

            def low(it, u):
                dve.wait_ge(hi_ready, it + 1)
                nc.vector.tensor_tensor(hT_lo[:, :, ds(it * P, P)], pt[u][:].rearrange("p (k n) -> p k n", k=KD),
                                        hT_hi[:, :, ds(it * P, P)].bitcast(F32), ALU.subtract).then_inc(lo_ready, 1)
            pipelined(dve, NT, 4, [(scale, 0), (low, 2)])

        @block.gpsimd
        def _(pool):
            pool.wait_ge(row_ready, NCH)

            def shift(it, u):
                pool.wait_ge(scaled, it + 1)
                nc.gpsimd.tensor_tensor(hn[:, u], hn[:, u], brow[:, 0], ALU.add).then_inc(shifted, 1)
            pipelined(pool, NT, 2, [(shift, 0)])

        @block.tensor
        def _(pe):
            for n in range(NCH):
                pe.wait_ge(acc_step, KD * (n + 1))
                if n >= 2:
                    pe.wait_ge(row_ready, n - 1)
                nc.tensor.matmul(pm[n % 2][:], cst["ones"][:], acc[:, n % 2, :], start=True, stop=True).then_inc(summed, 1)

            def turn(it, u):
                pe.wait_ge(shifted, it + 1)
                if at_least(it, 2):
                    pe.wait_ge(lo_ready, it - 1)
                for k in range(KD):
                    last = nc.tensor.transpose(pt[u][:, k * P:(k + 1) * P], hn[:, u, k * P:(k + 1) * P], cst["ident"][:])
                last.then_inc(turned, 1)
            pipelined(pe, NT, 2, [(turn, 0)])


def lru(nc, sem, cst, io, hT_hi, hT_lo, cond, y_dram, mod_dram):
    ctx = ExitStack()
    with ctx:
        sb = lambda n, s, d=F32: ctx.enter_context(nc.sbuf_tensor(n, s, d))
        ps = lambda n, s: ctx.enter_context(nc.psum_tensor(n, s, F32))
        raw = {"x": sb("raw_x", [P, KD, P]), "g": sb("raw_g", [P, KD, P])}
        whi = {"x": sb("wx_hi", [P, KD, P], F32R), "g": sb("wg_hi", [P, KD, P], F32R)}
        wlo = {"x": sb("wx_lo", [P, KD, P], F32R), "g": sb("wg_lo", [P, KD, P], F32R)}
        gw = sb("gate_w", [P, 2, P])
        cw = sb("conv_w", [P, KD, CONV])
        cb = sb("conv_b", [P, KD])
        gb = sb("gate_b", [P, 2, KD])
        lam = sb("lam", [P, KD])
        dec = sb("decay", [P, 2, KD])
        sp_t = sb("sp_t", [P, 6, KD])
        xu = sb("xu", [P, 2, CONV - 1 + NB])
        zero = sb("zero3", [P, CONV - 1])
        XB, TR, TI, A, T, M, GE = [sb(n, [P, HALF]) for n in ("XB", "TR", "TI", "A", "T", "M", "GE")]
        carry = sb("carry", [P, 1])
        stg = sb("stg", [P, 2, KD // 2, NB])
        mtmp = sb("mtmp", [P, NB])
        macc = sb("macc", [P, NB])
        px = [ps("px0", [P, NB]), ps("px1", [P, NB])]
        pg = [ps("pg0", [P, NB]), ps("pg1", [P, NB])]
        pr, pi = ps("pr", [P, NB]), ps("pi", [P, NB])

        raw_in = {"x": sem("raw_x_in"), "g": sem("raw_g_in")}
        hi_done = {"x": sem("wx_hi_done"), "g": sem("wg_hi_done")}
        lo_done = {"x": sem("wx_lo_done"), "g": sem("wg_lo_done")}
        vec_in, vec_ready, gw_in = sem("vec_in"), sem("vec_ready"), sem("gw_in")
        x_mm, g_mm, gate_mm = sem("x_mm"), sem("g_mm"), sem("gate_mm")
        xu_ready, halo_ready, tap0, tap1, tap2, conv = [sem(n) for n in
                                                       ("xu_ready", "halo_ready", "tap0", "tap1", "tap2", "conv")]
        tr_ready, ti_ready, a_ready, t_ready, sq_ready, m_ready = [sem(n) for n in
                                                       ("tr_ready", "ti_ready", "a_ready", "t_ready", "sq_ready", "m_ready")]
        root_ready, ix_ready, b_ready, scan_ready, carried, gelu, y_ready, y_out = [sem(n) for n in
                          ("root_ready", "ix_ready", "b_ready", "scan_ready", "carried", "gelu", "y_ready", "y_out")]
        s_a, s_b = sem("sp_a"), sem("sp_b")
        stg_in = [sem("stg_in0"), sem("stg_in1")]
        mt, ma, mo = sem("mod_tmp"), sem("mod_acc"), sem("mod_out")
        zeroed = sem("zeroed")

        w_v = io["lru_w_in"][0].rearrange("(k p) n -> p k n", p=P)
        OFF = {"g": 0, "x": D}
        y_v = y_dram.rearrange("t p j n -> p j t n")
        NH = HALF // NB
        TH = HALF // P
        block = ctx.enter_context(nc.Block())

        def channels(eng, body):
            body(0, False)
            with eng.Fori(1, KD - 1) as j:
                body(j, False)
            body(KD - 1, True)

        @block.sync
        def _(sp):
            col = lambda a: a.rearrange("(j p) -> p j", p=P)
            sp.dma_start(raw["x"][:], w_v[:, :, D:D + P]).then_inc(raw_in["x"], 16)
            with nc.allow_non_contiguous_dma(reason="small vectors by channel"):
                sp.dma_start(lam[:], col(io["lru_lambda"][0]), allow_slow_non_contiguous=True).then_inc(vec_in, 16)
                sp.dma_start(cb[:], col(io["lru_conv_b"][0]), allow_slow_non_contiguous=True).then_inc(vec_in, 16)
                sp.dma_start(gb[:, 0], col(io["lru_ba"][0]), allow_slow_non_contiguous=True).then_inc(vec_in, 16)
                sp.dma_start(gb[:, 1], col(io["lru_bx"][0]), allow_slow_non_contiguous=True).then_inc(vec_in, 16)
                for w in range(CONV):
                    sp.dma_start(cw[:, :, w], col(io["lru_conv_w"][0, w]), allow_slow_non_contiguous=True).then_inc(vec_in, 16)

            def body(j, last):
                if at_least(j, 1):
                    sp.wait_ge(lo_done["g"], j)
                sp.dma_start(raw["g"][:], w_v[:, :, ds(j * P, P)]).then_inc(raw_in["g"], 16)
                if at_least(j, 1):
                    sp.wait_ge(gate_mm, j * 4)
                sp.dma_start(gw[:, 0], io["lru_wa"][0, ds(j, 1)].rearrange("o i q -> (o i) q")).then_inc(gw_in, 16)
                sp.dma_start(gw[:, 1], io["lru_wx"][0, ds(j, 1)].rearrange("o i q -> (o i) q")).then_inc(gw_in, 16)
                if not last:
                    sp.wait_ge(lo_done["x"], j + 1)
                    sp.dma_start(raw["x"][:], w_v[:, :, ds(j * P + (D + P), P)]).then_inc(raw_in["x"], 16)
                for h in range(2):
                    sp.wait_ge(y_ready, 2 * j + h + 1)
                    sp.dma_start(y_v[:, ds(j, 1), h * TH:(h + 1) * TH, :].rearrange("p o t n -> p (o t) n"),
                                 M[:].rearrange("p (t n) -> p t n", n=P)).then_inc(y_out, 16)
            channels(sp, body)
            sp.wait_ge(y_out, 16 * 2 * KD)

        @block.scalar
        def _(act):
            act.wait_ge(vec_in, 16 * (4 + CONV))
            nc.scalar.activation(sp_t[:, 0], lam[:], ACT.Abs).then_inc(s_a, 1)
            act.wait_ge(s_a, 1)
            nc.scalar.activation(sp_t[:, 1], sp_t[:, 0], ACT.Exp, scale=-1.0).then_inc(s_a, 1)
            act.wait_ge(s_b, 1)
            nc.scalar.activation(sp_t[:, 3], sp_t[:, 2], ACT.Ln).then_inc(s_a, 1)
            act.wait_ge(raw_in["x"], 16)
            nc.scalar.activation(whi["x"][:], raw["x"][:], ACT.Copy).then_inc(hi_done["x"], 1)
            act.wait_ge(zeroed, 1)
            nc.scalar.activation(xu[:, 0, 0:CONV - 1], zero[:], ACT.Copy).then_inc(halo_ready, 1)
            act.wait_ge(vec_ready, 1)

            def body(j, last):
                for h in range(2):
                    hh = 2 * j + h
                    for n in range(NH):
                        c = hh * NH + n
                        act.wait_ge(x_mm, c + 1)
                        if at_least(j, 1) or c >= 2:
                            act.wait_ge(conv, c - 1)
                        nc.scalar.activation(xu[:, n, CONV - 1:], px[n][:], ACT.Copy).then_inc(xu_ready, 1)
                        act.wait_ge(xu_ready, c + 1)
                        act.wait_ge(halo_ready, c + 1)
                        if n == 0 and (at_least(j, 1) or h):
                            act.wait_ge(ix_ready, hh)
                        act.nop(nofuse=True)
                        nc.scalar.activation(XB[:, n * NB:(n + 1) * NB], xu[:, n, 0:NB], ACT.Identity,
                                             scale=cw[:, ds(j, 1), 0], bias=cb[:, ds(j, 1)]).then_inc(tap0, 1)
                        if at_least(j, 1) or c >= 1:
                            act.wait_ge(conv, c)
                        tail = zero[:] if h == 1 and n == NH - 1 else xu[:, n, NB:]
                        if not (last and h == 1 and n == NH - 1):
                            nc.scalar.activation(xu[:, 1 - n, 0:CONV - 1], tail, ACT.Copy).then_inc(halo_ready, 1)
                        if h == 0 and n == 0:
                            act.wait_ge(raw_in["g"], 16 * (j + 1))
                            if at_least(j, 1):
                                act.wait_ge(g_mm, 4 * j)
                            nc.scalar.activation(whi["g"][:], raw["g"][:], ACT.Copy).then_inc(hi_done["g"], 1)
                        if h == 1 and n == NH - 1 and not last:
                            act.wait_ge(raw_in["x"], 16 * (j + 2))
                            nc.scalar.activation(whi["x"][:], raw["x"][:], ACT.Copy).then_inc(hi_done["x"], 1)
                    for n in range(NH):
                        c = hh * NH + n
                        act.wait_ge(gate_mm, c + 1)
                        if n == 0 and (at_least(j, 1) or h):
                            act.wait_ge(b_ready, hh)
                        act.nop(nofuse=True)
                        nc.scalar.activation(TR[:, n * NB:(n + 1) * NB], pr[:], ACT.Tanh, scale=0.5,
                                             bias=gb[:, 0, ds(j, 1)]).then_inc(tr_ready, 1)
                        act.nop(nofuse=True)
                        nc.scalar.activation(TI[:, n * NB:(n + 1) * NB], pi[:], ACT.Tanh, scale=0.5,
                                             bias=gb[:, 1, ds(j, 1)]).then_inc(ti_ready, 1)
                    act.wait_ge(tr_ready, (hh + 1) * NH)
                    if at_least(j, 1) or h:
                        act.wait_ge(scan_ready, hh)
                        act.wait_ge(y_out, 16 * hh)
                    act.nop(nofuse=True)
                    nc.scalar.activation(T[:], TR[:], ACT.Tanh, scale=dec[:, 0, ds(j, 1)], bias=dec[:, 0, ds(j, 1)])\
                        .then_inc(t_ready, 1)
                    act.nop(nofuse=True)
                    nc.scalar.activation(A[:], TR[:], ACT.Exp, scale=dec[:, 1, ds(j, 1)], bias=dec[:, 1, ds(j, 1)])\
                        .then_inc(a_ready, 1)
                    act.wait_ge(a_ready, hh + 1)
                    nc.scalar.activation(M[:], A[:], ACT.Square).then_inc(sq_ready, 1)
                    act.wait_ge(m_ready, hh + 1)
                    nc.scalar.activation(M[:], T[:], ACT.Sqrt, scale=0.25).then_inc(root_ready, 1)
                    for n in range(NH):
                        act.wait_ge(g_mm, hh * NH + n + 1)
                        if n == 0 and (at_least(j, 1) or h):
                            act.wait_ge(y_ready, hh)
                        nc.scalar.activation(GE[:, n * NB:(n + 1) * NB], pg[n][:], ACT.Gelu_apprx_tanh).then_inc(gelu, 1)
            channels(act, body)

        @block.vector
        def _(dve):
            nc.vector.memset(zero[:], 0.0).then_inc(zeroed, 1)
            dve.wait_ge(s_a, 2)
            nc.vector.tensor_scalar(sp_t[:, 2], sp_t[:, 1], 1.0, None, ALU.add).then_inc(s_b, 1)
            dve.wait_ge(s_b, 1)
            nc.vector.tensor_scalar(sp_t[:, 4], sp_t[:, 2], -1.0, None, ALU.add).then_inc(s_b, 1)
            dve.wait_ge(s_b, 2)
            nc.vector.tensor_scalar(sp_t[:, 5], sp_t[:, 4], 0.0, None, ALU.is_equal).then_inc(s_b, 1)
            dve.wait_ge(s_b, 3)
            dve.wait_ge(s_a, 3)
            nc.vector.tensor_tensor(sp_t[:, 3], sp_t[:, 3], sp_t[:, 5], ALU.add).then_inc(s_b, 1)
            nc.vector.tensor_tensor(sp_t[:, 4], sp_t[:, 4], sp_t[:, 5], ALU.add).then_inc(s_b, 1)
            dve.wait_ge(s_b, 5)
            nc.vector.tensor_tensor(sp_t[:, 3], sp_t[:, 3], sp_t[:, 1], ALU.mult).then_inc(s_b, 1)
            nc.vector.reciprocal(sp_t[:, 5], sp_t[:, 4]).then_inc(s_b, 1)
            dve.wait_ge(s_b, 7)
            nc.vector.tensor_tensor(sp_t[:, 3], sp_t[:, 3], sp_t[:, 5], ALU.mult).then_inc(s_b, 1)
            nc.vector.tensor_scalar(sp_t[:, 0], lam[:], -1.0, 0.0, ALU.mult, ALU.max).then_inc(s_b, 1)
            dve.wait_ge(s_b, 9)
            nc.vector.tensor_tensor(sp_t[:, 3], sp_t[:, 3], sp_t[:, 0], ALU.add).then_inc(s_b, 1)
            dve.wait_ge(s_b, 10)
            nc.vector.tensor_scalar(dec[:, 0], sp_t[:, 3], LRU_C / 2, None, ALU.mult).then_inc(s_b, 1)
            nc.vector.tensor_scalar(dec[:, 1], sp_t[:, 3], -LRU_C / 2, None, ALU.mult).then_inc(s_b, 1)
            nc.vector.tensor_scalar(gb[:], gb[:], 0.5, None, ALU.mult).then_inc(s_b, 1)
            dve.wait_ge(s_b, 13)
            nc.vector.memset(carry[:], 0.0).then_inc(vec_ready, 1)
            dve.wait_ge(hi_done["x"], 1)
            nc.vector.tensor_tensor(wlo["x"][:], raw["x"][:], whi["x"][:].bitcast(F32), ALU.subtract).then_inc(lo_done["x"], 1)

            def body(j, last):
                for h in range(2):
                    hh = 2 * j + h
                    for n in range(NH):
                        c = hh * NH + n
                        xb = XB[:, n * NB:(n + 1) * NB]
                        dve.wait_ge(tap0, c + 1)
                        for w, before, done in ((1, None, tap1), (2, tap1, tap2), (3, tap2, conv)):
                            if before is not None:
                                dve.wait_ge(before, c + 1)
                            nc.vector.scalar_tensor_tensor(xb, xu[:, n, w:w + NB], cw[:, ds(j, 1), w], xb,
                                                           ALU.mult, ALU.add).then_inc(done, 1)
                        if h == 0 and n == 0:
                            dve.wait_ge(hi_done["g"], j + 1)
                            nc.vector.tensor_tensor(wlo["g"][:], raw["g"][:], whi["g"][:].bitcast(F32), ALU.subtract)\
                                .then_inc(lo_done["g"], 1)
                        if h == 1 and n == NH - 1 and not last:
                            dve.wait_ge(hi_done["x"], j + 2)
                            nc.vector.tensor_tensor(wlo["x"][:], raw["x"][:], whi["x"][:].bitcast(F32), ALU.subtract)\
                                .then_inc(lo_done["x"], 1)
                    dve.wait_ge(ti_ready, (hh + 1) * NH)
                    dve.wait_ge(conv, (hh + 1) * NH)
                    nc.vector.scalar_tensor_tensor(TI[:], TI[:], 1.0, XB[:], ALU.add, ALU.mult).then_inc(ix_ready, 1)
                    dve.wait_ge(sq_ready, hh + 1)
                    nc.vector.scalar_tensor_tensor(T[:], M[:], 1.0, T[:], ALU.add, ALU.mult).then_inc(m_ready, 1)
                    dve.wait_ge(root_ready, hh + 1)
                    dve.wait_ge(ix_ready, hh + 1)
                    nc.vector.tensor_tensor(TI[:], TI[:], M[:], ALU.mult).then_inc(b_ready, 1)
                    dve.wait_ge(b_ready, hh + 1)
                    if at_least(j, 1) or h:
                        dve.wait_ge(carried, hh)
                    nc.vector.tensor_tensor_scan(M[:], A[:], TI[:], 0.0 if h == 0 else carry[:], ALU.mult, ALU.add)\
                        .then_inc(scan_ready, 1)
                    dve.wait_ge(scan_ready, hh + 1)
                    nc.vector.tensor_copy(carry[:], M[:, HALF - 1:HALF]).then_inc(carried, 1)
                    dve.wait_ge(carried, hh + 1)
                    dve.wait_ge(gelu, (hh + 1) * NH)
                    nc.vector.tensor_tensor(M[:], M[:], GE[:], ALU.mult).then_inc(y_ready, 1)
            channels(dve, body)

        @block.gpsimd
        def _(pool):
            ada_v = io["ada_w"][0].rearrange("(p k) n -> p k n", k=KD)
            KH = KD // 2
            NM = 4 * D // NB
            def load(m, q):
                pool.dma_start(stg[:, q], ada_v[:, q * KH:(q + 1) * KH, ds(m * NB + 2 * D, NB)]).then_inc(stg_in[q], 16)
            load(0, 0)
            load(0, 1)
            def body(m, last):
                for k in range(KD):
                    q = k // KH
                    if k % KH == 0:
                        pool.wait_ge(stg_in[q], 16 * (m + 1))
                    if k == 0:
                        if at_least(m, 1):
                            pool.wait_ge(mo, 16 * m)
                        pool.nop(nofuse=True)
                        nc.gpsimd.tensor_scalar(macc[:], stg[:, q, k % KH], cond[:, k:k + 1], 0.0, ALU.mult, ALU.add).then_inc(ma, 1)
                        continue
                    pool.wait_ge(ma, m * KD + k)
                    pool.nop(nofuse=True)
                    nc.gpsimd.tensor_scalar(mtmp[:], stg[:, q, k % KH], cond[:, k:k + 1], 0.0, ALU.mult, ALU.add).then_inc(mt, 1)
                    pool.wait_ge(mt, m * (KD - 1) + k)
                    nc.gpsimd.tensor_tensor(macc[:], macc[:], mtmp[:], ALU.add).then_inc(ma, 1)
                    if k % KH == KH - 1:
                        pool.wait_ge(ma, m * KD + k + 1)
                        if not last:
                            load(m + 1, q)
                pool.dma_start(mod_dram[:, ds(m * NB, NB)], macc[:]).then_inc(mo, 16)
            body(0, False)
            with pool.Fori(1, NM - 1) as m:
                body(m, False)
            body(NM - 1, True)
            pool.wait_ge(mo, 16 * NM)

        @block.tensor
        def _(pe):
            def project(br, dst, tok):
                for k in range(KD):
                    cols = slice(tok, tok + NB)
                    nc.tensor.matmul(dst[:], whi[br][:, k], hT_hi[:, k, cols], start=(k == 0), stop=False)
                    nc.tensor.matmul(dst[:], whi[br][:, k], hT_lo[:, k, cols], start=False, stop=False)
                    last = nc.tensor.matmul(dst[:], wlo[br][:, k], hT_hi[:, k, cols], start=False, stop=(k == KD - 1))
                return last

            def body(j, last):
                def gates(h, n):
                    c = (2 * j + h) * NH + n
                    if h == 0 and n == 0:
                        pe.wait_ge(gw_in, 32 * (j + 1))
                    pe.wait_ge(conv, c + 1)
                    if at_least(j, 1) or c >= 1:
                        pe.wait_ge(ti_ready, c)
                    nc.tensor.matmul(pr[:], gw[:, 0], XB[:, n * NB:(n + 1) * NB], start=True, stop=True)
                    nc.tensor.matmul(pi[:], gw[:, 1], XB[:, n * NB:(n + 1) * NB], start=True, stop=True).then_inc(gate_mm, 1)

                for h in range(2):
                    hh = 2 * j + h
                    if h == 0:
                        pe.wait_ge(lo_done["x"], j + 1)
                    for n in range(NH):
                        if at_least(j, 1) or h:
                            pe.wait_ge(xu_ready, hh * NH + n - 1)
                        project("x", px[n], (h * NH + n) * NB).then_inc(x_mm, 1)
                    gates(h, 0)
                    if h == 0:
                        pe.wait_ge(lo_done["g"], j + 1)
                    for n in range(NH):
                        if at_least(j, 1) or h:
                            pe.wait_ge(gelu, hh * NH + n - 1)
                        project("g", pg[n], (h * NH + n) * NB).then_inc(g_mm, 1)
                        if n == 0:
                            gates(h, 1)
            channels(pe, body)


def out_and_norm(nc, sem, cst, io, x2, y_dram, mod_dram, hn2_dram, g2row, logits):
    ctx = ExitStack()
    with ctx:
        sb = lambda n, s, d=F32: ctx.enter_context(nc.sbuf_tensor(n, s, d))
        ps = lambda n, s: ctx.enter_context(nc.psum_tensor(n, s, F32))
        macc = x2[:, 0:4, :].rearrange("p t n -> p (t n)")
        g1row, sh2, sc2 = sb("g1row", [P, D]), sb("sh2", [P, D]), sb("sc2", [P, D])
        gain = sb("b_gain", [P, D])
        rw = sb("router_w", [P, KD, E])
        rb = sb("router_b", [P, E])
        wr = sb("b_wraw", [P, 2, D])
        wo_hi, wo_lo = sb("wo_hi", [P, KD, D], F32R), sb("wo_lo", [P, KD, D], F32R)
        yt, xr = sb("b_yt", [P, 2, D]), sb("b_xr", [P, 2, D])
        yh = [sb(f"b_yh{u}", [P, D], F32R) for u in range(2)]
        yl = [sb(f"b_yl{u}", [P, D], F32R) for u in range(2)]
        hn = sb("b_hn", [P, 2, D])
        hT = sb("b_hT", [P, D])
        ssq, std, rstd = sb("b_ssq", [P, 2]), sb("b_std", [P, 2]), sb("b_rstd", [P, 2])
        po = [ps("po0", [P, D]), ps("po1", [P, D])]
        pt = ps("b_pt", [P, D])
        pl = ps("pl", [P, NB])
        junk = pt[:]

        rows_in, macc_in, rsum, rows = sem("b_rows_in"), sem("macc_in"), sem("b_rsum"), sem("b_rows")
        wr_in = [sem("wr_in0"), sem("wr_in1")]
        wo_h, wo_l = sem("wo_h"), sem("wo_l")
        y_in = [sem("by_in0"), sem("by_in1")]
        x_in = [sem("bx_in0"), sem("bx_in1")]
        yhi, ylo, mm, gated, resid = sem("b_yhi"), sem("b_ylo"), sem("b_mm"), sem("b_gated"), sem("b_resid")
        sqd, stdd, rec, scaled, shifted = sem("b_sq"), sem("b_std_s"), sem("b_rec"), sem("b_scaled"), sem("b_shifted")
        turned, hT_ready, routed, logit = sem("b_turned"), sem("b_hT_s"), sem("b_routed"), sem("b_logit")
        stored = [sem("b_stored0"), sem("b_stored1")]
        half_sum = sem("b_sc")
        w_v = io["lru_w_out"][0].rearrange("(k p) n -> k p n", p=P)
        y_v = y_dram.rearrange("t p j n -> t p (j n)")
        NR = 4 * D // NB
        dst = [g1row, sh2, sc2, g2row]
        block = ctx.enter_context(nc.Block())

        @block.sync
        def _(sp):
            sp.dma_start(macc, mod_dram).then_inc(macc_in, 16)
            for q in range(4):
                sp.dma_start(dst[q][:], io["ada_b"][0, (2 + q) * D:(3 + q) * D].partition_broadcast(P)).then_inc(rows_in, 16)
            sp.dma_start(gain[:], io["norm2_g"][0].partition_broadcast(P)).then_inc(rows_in, 16)
            sp.dma_start(rw[:], io["router_w"].rearrange("(k p) e -> p k e", p=P)).then_inc(rows_in, 16)
            sp.dma_start(rb[:], io["router_b"].partition_broadcast(P)).then_inc(rows_in, 16)
            for k in range(KD):
                if k >= 2:
                    sp.wait_ge(wo_l, k - 1)
                sp.dma_start(wr[:, k % 2], w_v[k]).then_inc(wr_in[k % 2], 16)

            def load(it, u):
                if at_least(it, 2):
                    sp.wait_ge(ylo, it - 1)
                    sp.wait_ge(resid, it - 1)
                sp.dma_start(yt[:, u], y_v[ds(it, 1)].rearrange("o p n -> (o p) n")).then_inc(y_in[u], 16)
                sp.dma_start(xr[:, u], io["x"][0, ds(it * P, P), :]).then_inc(x_in[u], 16)

            def store(it, u):
                sp.wait_ge(shifted, it + 1)
                sp.dma_start(hn2_dram[ds(it * P, P), :], hn[:, u]).then_inc(stored[u], 16)
            pipelined(sp, NT, 6, [(load, 0), (store, 4)])
            for u in range(2):
                sp.wait_ge(stored[u], 16 * NT // 2)

        @block.scalar
        def _(act):
            for k in range(KD):
                act.wait_ge(wr_in[k % 2], 16 * (k // 2 + 1))
                nc.scalar.activation(wo_hi[:, k], wr[:, k % 2], ACT.Copy).then_inc(wo_h, 1)

            def high(it, u):
                act.wait_ge(y_in[u], it * 8 + 16 - u * 8)
                if at_least(it, 2):
                    act.wait_ge(mm, it - 1)
                nc.scalar.activation(yh[u][:], yt[:, u], ACT.Copy).then_inc(yhi, 1)

            def squares(it, u):
                act.wait_ge(resid, it + 1)
                if at_least(it, 2):
                    act.wait_ge(rec, it - 1)
                act.nop(nofuse=True)
                nc.scalar.activation(hn[:, u], x2[:, ds(it, 1)].rearrange("p o n -> p (o n)"), ACT.Square,
                                     accum_out=ssq[:, u:u + 1]).then_inc(sqd, 1)
                act.wait_ge(sqd, it + 1)
                nc.scalar.activation(std[:, u:u + 1], ssq[:, u:u + 1], ACT.Sqrt, scale=1.0 / D,
                                     bias=cst["eps"][:]).then_inc(stdd, 1)

            def squares_free(it, u):
                if at_least(it, 2):
                    act.wait_ge(turned, it - 1)
                    act.wait_ge(stored[u], it * 8 - u * 8)
                squares(it, u)

            def evacuate(it, u):
                act.wait_ge(turned, it + 1)
                if at_least(it, 1):
                    act.wait_ge(routed, it)
                nc.scalar.activation(hT[:], pt[:], ACT.Copy).then_inc(hT_ready, 1)
            pipelined(act, NT, 6, [(high, 0), (squares_free, 2), (evacuate, 4)])

        @block.vector
        def _(dve):
            dve.wait_ge(rows_in, 16 * 7)
            for n in range(NR):
                q, cols = n * NB // D, ds(n * NB % D, NB)
                dve.wait_ge(rsum, n + 1)
                nc.vector.tensor_tensor(dst[q][:, cols], po[n % 2][:, 0:NB], dst[q][:, cols], ALU.add).then_inc(rows, 1)
                if n == 3 * D // NB - 1:
                    dve.wait_ge(rows, n + 1)
                    nc.vector.scalar_tensor_tensor(sc2[:], sc2[:], 1.0, gain[:], ALU.add, ALU.mult).then_inc(half_sum, 1)
            dve.wait_ge(rows, NR)
            dve.wait_ge(half_sum, 1)
            for k in range(KD):
                dve.wait_ge(wo_h, k + 1)
                nc.vector.tensor_tensor(wo_lo[:, k], wr[:, k % 2], wo_hi[:, k].bitcast(F32), ALU.subtract).then_inc(wo_l, 1)

            def low(it, u):
                dve.wait_ge(yhi, it + 1)
                if at_least(it, 2):
                    dve.wait_ge(mm, it - 1)
                nc.vector.tensor_tensor(yl[u][:], yt[:, u], yh[u][:].bitcast(F32), ALU.subtract).then_inc(ylo, 1)

            def gate(it, u):
                dve.wait_ge(mm, it + 1)
                nc.vector.tensor_tensor(x2[:, ds(it, 1)].rearrange("p o n -> p (o n)"), po[u][:], g1row[:],
                                        ALU.mult).then_inc(gated, 1)

            def norm(it, u):
                dve.wait_ge(stdd, it + 1)
                nc.vector.reciprocal(rstd[:, u:u + 1], std[:, u:u + 1]).then_inc(rec, 1)
                dve.wait_ge(rec, it + 1)
                nc.vector.scalar_tensor_tensor(hn[:, u], x2[:, ds(it, 1)].rearrange("p o n -> p (o n)"),
                                               rstd[:, u:u + 1], sc2[:], ALU.mult, ALU.mult).then_inc(scaled, 1)

            def bias(it, u):
                dve.wait_ge(routed, it + 1)
                nc.vector.tensor_tensor(logits[:, ds(it, 1)].rearrange("p o n -> p (o n)"), pl[:, 0:E], rb[:],
                                        ALU.add).then_inc(logit, 1)
            pipelined(dve, NT, 6, [(low, 0), (gate, 1), (norm, 2), (bias, 4)])

        @block.gpsimd
        def _(pool):
            def add_x(it, u):
                pool.wait_ge(gated, it + 1)
                pool.wait_ge(x_in[u], it * 8 + 16 - u * 8)
                x2t = x2[:, ds(it, 1)].rearrange("p o n -> p (o n)")
                nc.gpsimd.tensor_tensor(x2t, x2t, xr[:, u], ALU.add).then_inc(resid, 1)

            def shift(it, u):
                pool.wait_ge(scaled, it + 1)
                nc.gpsimd.tensor_tensor(hn[:, u], hn[:, u], sh2[:], ALU.add).then_inc(shifted, 1)
            pipelined(pool, NT, 4, [(add_x, 0), (shift, 1)])

        @block.tensor
        def _(pe):
            pe.wait_ge(macc_in, 16)
            for n in range(NR):
                if n >= 2:
                    pe.wait_ge(rows, n - 1)
                nc.tensor.matmul(po[n % 2][:, 0:NB], cst["ones"][:], macc[:, n * NB:(n + 1) * NB],
                                 start=True, stop=True).then_inc(rsum, 1)
            pe.wait_ge(wo_l, KD)
            pe.wait_ge(rows, NR)

            def main(it, u, half):
                if half == 0:
                    pe.wait_ge(ylo, it + 1)
                    if at_least(it, 2):
                        pe.wait_ge(gated, it - 1)
                cols = slice(half * NB, (half + 1) * NB)
                for k in range(KD):
                    tok = slice(k * P, (k + 1) * P)
                    nc.tensor.matmul(po[u][:, cols], yh[u][:, tok], wo_hi[:, k, cols], start=(k == 0), stop=False)
                    nc.tensor.matmul(po[u][:, cols], yh[u][:, tok], wo_lo[:, k, cols], start=False, stop=False)
                    last = nc.tensor.matmul(po[u][:, cols], yl[u][:, tok], wo_hi[:, k, cols], start=False, stop=(k == KD - 1))
                if half == 1:
                    last.then_inc(mm, 1)

            def turn(it, u):
                pe.wait_ge(shifted, it + 1)
                if at_least(it, 1):
                    pe.wait_ge(hT_ready, it)
                for k in range(KD):
                    last = nc.tensor.transpose(pt[:, k * P:(k + 1) * P], hn[:, u, k * P:(k + 1) * P], cst["ident"][:])
                last.then_inc(turned, 1)

            def route(it, u):
                pe.wait_ge(hT_ready, it + 1)
                if at_least(it, 1):
                    pe.wait_ge(logit, it)
                for k in range(KD):
                    last = nc.tensor.matmul(pl[:, 0:E], hT[:, k * P:(k + 1) * P], rw[:, k], start=(k == 0), stop=(k == KD - 1))
                last.then_inc(routed, 1)
            pipelined(pe, NT, 4, [(lambda it, u: main(it, u, 0), 0), (turn, 3),
                                  (lambda it, u: main(it, u, 1), 0), (route, 3)])


def dispatch(nc, sem, cst, logits, tab):
    ctx = ExitStack()
    with ctx:
        sb = lambda n, s, d=F32: ctx.enter_context(nc.sbuf_tensor(n, s, d))
        ps = lambda n, s: ctx.enter_context(nc.psum_tensor(n, s, F32))
        prob, work, work2, oh1, oh2, mask = [sb(n, [P, NT, E]) for n in ("prob", "work", "work2", "oh1", "oh2", "mask")]
        mx, m1, m2, vm = [sb(n, [P, NT]) for n in ("d_mx", "d_m1", "d_m2", "d_vm")]
        gs, gq = sb("d_gs", [P, NT, G]), sb("d_gq", [P, NT, G])
        gates = sb("d_gates", [P, TOPK, NT])
        below = sb("below", [P, P])
        slot_no, block_no = sb("slot_no", [P, P]), sb("block_no", [P, MAXB])
        rank_w, thresh = sb("rank_w", [P, E]), sb("thresh", [P, E])
        cnt, nblk, ends, start, ones_e = [sb(n, [P, E]) for n in ("cnt", "nblk", "ends", "start", "ones_e")]
        cmp = sb("cmp", [P, E, E])
        cmpb = sb("cmpb", [P, MAXB, E])
        eb, par = sb("eb", [P, MAXB]), sb("par", [P, MAXB])
        pari = sb("pari", [P, MAXB], I32)
        posf = sb("posf", [P, TOPK, NT])
        ri, bi = sb("ri", [P, TOPK * NT], I32), sb("bi", [P, TOPK * NT], I32)
        rf, bf = sb("rf", [P, TOPK * NT]), sb("bf", [P, TOPK * NT])
        tok2 = sb("tok2", [P, TOPK * NT])
        pick = [sb(f"pick{u}", [P, P]) for u in range(2)]
        place = sb("place", [P, 2, 2, MAXB])
        prank, pcnt, pslot = ps("prank", [P, NB]), ps("pcnt", [P, NB]), ps("pslot", [P, NB])

        consts, dve_done, exp_in, exp_out = sem("d_consts"), sem("d_step"), sem("exp_in"), sem("exp_out")
        mask_ready, ranked, picked, slotted = sem("mask_ready"), sem("ranked"), sem("picked"), sem("slotted")
        block = ctx.enter_context(nc.Block())

        @block.gpsimd
        def _(pool):
            nc.gpsimd.memset(below[:], 1.0).then_inc(consts, 1)
            nc.gpsimd.memset(ones_e[:], 1.0).then_inc(consts, 1)
            pool.wait_ge(consts, 2)
            nc.gpsimd.affine_select(out=below[:], in_=below[:], compare_op=ALU.is_gt, fill=0.0, base=0,
                                    pattern=[[1, P]], channel_multiplier=-1).then_inc(consts, 1)
            io_ = lambda t, pat, base, cm: nc.gpsimd.iota(t, pat, base=base, channel_multiplier=cm,
                                                          allow_small_or_imprecise_dtypes=True).then_inc(consts, 1)
            io_(slot_no[:], [[1, P]], 0, 0)
            io_(block_no[:], [[1, MAXB]], 0, 0)
            io_(rank_w[:], [[-1, E]], E, 0)
            io_(thresh[:], [[P, E]], 0, 0)
            io_(tok2[:], [[0, TOPK], [P, NT]], 0, 1)

        @block.scalar
        def _(act):
            act.wait_ge(exp_in, 1)
            nc.scalar.activation(prob[:], work[:], ACT.Exp).then_inc(exp_out, 1)

        @block.vector
        def _(dve):
            n = [0]
            v = nc.vector

            def done(ins):
                n[0] += 1
                ins.then_inc(dve_done, 1)
                dve.wait_ge(dve_done, n[0])
            wide = lambda a, k: a.unsqueeze(2).to_broadcast([a.shape[0], a.shape[1], k])
            row = lambda a, k: a.unsqueeze(1).to_broadcast([P, k, a.shape[-1]])

            done(v.tensor_reduce(mx[:], logits[:], AX.X, ALU.max))
            v.tensor_tensor(work[:], logits[:], wide(mx[:], E), ALU.subtract).then_inc(exp_in, 1)
            dve.wait_ge(exp_out, 1)
            done(v.tensor_reduce(mx[:], prob[:], AX.X, ALU.add))
            done(v.reciprocal(vm[:], mx[:]))
            done(v.tensor_tensor(prob[:], prob[:], wide(vm[:], E), ALU.mult))
            q = prob[:].rearrange("p t (g m) -> p t g m", m=PER)
            done(v.tensor_tensor(gs[:], q[:, :, :, 0], q[:, :, :, 1], ALU.add))
            for a in range(PER):
                for b in range(a + 1, PER):
                    if (a, b) != (0, 1):
                        done(v.tensor_tensor(gq[:], q[:, :, :, a], q[:, :, :, b], ALU.add))
                        done(v.tensor_tensor(gs[:], gs[:], gq[:], ALU.max))
            dve.wait_ge(consts, 8)

            def first_of(out, vals, top, k):
                done(v.tensor_reduce(top, vals, AX.X, ALU.max))
                done(v.tensor_tensor(out, vals, wide(top, k), ALU.is_equal))
                done(v.tensor_tensor(out, out, row(rank_w[:, 0:k], NT), ALU.mult))
                done(v.tensor_reduce(vm[:], out, AX.X, ALU.max))
                done(v.tensor_tensor(out, out, wide(vm[:], k), ALU.is_equal))
            first_of(gq[:], gs[:], mx[:], G)
            inb = gq[:].rearrange("p t g -> p (t g)")
            w3 = work[:].rearrange("p t (g m) -> p (t g) m", m=PER)
            p3 = prob[:].rearrange("p t (g m) -> p (t g) m", m=PER)
            done(v.tensor_tensor(w3, p3, wide(inb, PER), ALU.mult))
            done(v.tensor_scalar(gq[:], gq[:], -1.0, None, ALU.add))
            done(v.tensor_tensor(w3, w3, wide(inb, PER), ALU.add))
            first_of(oh1[:], work[:], m1[:], E)
            done(v.scalar_tensor_tensor(work2[:], oh1[:], -4.0, work[:], ALU.mult, ALU.add))
            first_of(oh2[:], work2[:], m2[:], E)
            v.tensor_tensor(mask[:], oh1[:], oh2[:], ALU.add).then_inc(mask_ready, 1)
            done(v.tensor_tensor(mx[:], m1[:], m2[:], ALU.add))
            done(v.reciprocal(vm[:], mx[:]))
            done(v.tensor_tensor(gates[:, 0], m1[:], vm[:], ALU.mult))
            done(v.tensor_tensor(gates[:, 1], m2[:], vm[:], ALU.mult))
            done(v.memset(thresh[:, 0:1], -1.0))
            dve.wait_ge(ranked, 1)
            done(v.tensor_copy(cnt[:], pcnt[:, 0:E]))
            done(v.tensor_tensor(cmp[:], wide(cnt[:], E), row(thresh[:], E), ALU.is_gt))
            done(v.tensor_reduce(nblk[:], cmp[:], AX.X, ALU.add))
            done(v.tensor_tensor_scan(ends[:], ones_e[:], nblk[:], 0.0, ALU.mult, ALU.add))
            done(v.tensor_tensor(start[:], ends[:], nblk[:], ALU.subtract))
            done(v.tensor_scalar(start[:], start[:], float(P), None, ALU.mult))
            done(v.tensor_copy(tab["ends"][:], ends[:]))
            done(v.tensor_scalar(nblk[:, 0:1], ends[:, E - 1:E], -float(LEAD), None, ALU.add))
            done(v.tensor_copy(tab["blocks_less"][:], nblk[:, 0:1]))
            done(v.tensor_scalar(nblk[:, 0:1], ends[:, E - 1:E], -1.0, float(MAXB + 1), ALU.mult, ALU.add))
            done(v.tensor_copy(tab["unused"][:], nblk[:, 0:1]))
            pr = prank[:, 0:NT * E].rearrange("p (t e) -> p t e", e=E)
            done(v.tensor_tensor(work[:], pr, row(start[:], NT), ALU.add))
            for c, oh in enumerate((oh1, oh2)):
                done(v.tensor_tensor(work2[:], work[:], oh[:], ALU.mult))
                done(v.tensor_reduce(posf[:, c], work2[:], AX.X, ALU.add))
            pos_i = tab["pos"][:].rearrange("p c t -> p (c t)")
            done(v.tensor_copy(pos_i, posf[:].rearrange("p c t -> p (c t)")))
            done(v.tensor_scalar(ri[:], pos_i, P - 1, None, ALU.bitwise_and))
            done(v.tensor_scalar(bi[:], pos_i, P.bit_length() - 1, None, ALU.logical_shift_right))
            done(v.tensor_copy(rf[:], ri[:]))
            done(v.tensor_copy(bf[:], bi[:]))
            done(v.tensor_tensor(cmpb[:], wide(block_no[:], E), row(ends[:], MAXB), ALU.is_ge))
            done(v.tensor_reduce(eb[:], cmpb[:], AX.X, ALU.add))
            done(v.tensor_copy(pari[:], eb[:]))
            done(v.tensor_scalar(pari[:], pari[:], 1, None, ALU.bitwise_and))
            done(v.tensor_copy(par[:], pari[:]))
            done(v.tensor_scalar(par[:], par[:], float(WE), None, ALU.mult))
            done(v.tensor_copy(tab["woff"][:], par[:]))
            done(v.tensor_scalar(eb[:], eb[:], 1.0, None, ALU.add))
            done(v.tensor_copy(tab["expert1"][:], eb[:]))
            gate2 = gates[:].rearrange("p c t -> p (c t)")

            def factors(it, u):
                if at_least(it, 2):
                    dve.wait_ge(slotted, it - 1)
                v.tensor_scalar(pick[u][:], slot_no[:], rf[:, ds(it, 1)], None, ALU.is_equal).then_inc(picked, 1)
                v.tensor_scalar(place[:, u, 0], block_no[:], bf[:, ds(it, 1)], tok2[:, ds(it, 1)],
                                ALU.is_equal, ALU.mult).then_inc(picked, 1)
                v.tensor_scalar(place[:, u, 1], block_no[:], bf[:, ds(it, 1)], gate2[:, ds(it, 1)],
                                ALU.is_equal, ALU.mult).then_inc(picked, 1)
            pipelined(dve, TOPK * NT, 2, [(factors, 0)])
            dve.wait_ge(slotted, TOPK * NT)
            done(v.tensor_copy(tab["slot_token"][:], pslot[:, 0:MAXB]))
            done(v.tensor_scalar(tab["slot_gate"][:], pslot[:, MAXB:2 * MAXB], 0.5, None, ALU.mult))

        @block.tensor
        def _(pe):
            pe.wait_ge(consts, 8)
            pe.wait_ge(mask_ready, 1)
            m2d = mask[:].rearrange("p t e -> p (t e)")
            nc.tensor.matmul(prank[:, 0:NT * E], below[:], m2d, start=True, stop=False)
            for t in range(NT - 1):
                nc.tensor.matmul(prank[:, (t + 1) * E:NT * E].rearrange("p (t e) -> p t e", e=E), cst["ones"][:],
                                 mask[:, t:t + 1, :].to_broadcast([P, NT - 1 - t, E]), start=False, stop=(t == NT - 2))
            for t in range(NT):
                last = nc.tensor.matmul(pcnt[:, 0:E], cst["ones"][:], mask[:, t, :], start=(t == 0), stop=(t == NT - 1))
            last.then_inc(ranked, 1)

            def slots(it, u, first, last):
                pe.wait_ge(picked, it * 3 + 3)
                nc.tensor.matmul(pslot[:, 0:2 * MAXB], pick[u][:], place[:, u].rearrange("p a b -> p (a b)"),
                                 start=first, stop=last).then_inc(slotted, 1)
            N = TOPK * NT
            for it in range(2):
                slots(it, it, it == 0, False)
            with pe.Fori(1, N // 2 - 1) as i:
                for u in range(2):
                    slots(2 * i + u, u, False, False)
            for it in range(N - 2, N):
                slots(it, it % 2, False, it == N - 1)


def experts(nc, sem, cst, io, tab, hn2_dram, yslot_dram, g2row):
    ctx = ExitStack()
    with ctx:
        sb = lambda n, s, d=F32: ctx.enter_context(nc.sbuf_tensor(n, s, d))
        ps = lambda n, s: ctx.enter_context(nc.psum_tensor(n, s, F32))
        w = sb("e_w", [P, 2 * WE])
        xg, xT = sb("e_xg", [P, D]), sb("e_xT", [P, D])
        th, tmp, av, aT = sb("e_th", [P, FE]), sb("e_tmp", [P, FE]), sb("e_av", [P, FE]), sb("e_aT", [P, FE])
        ysb = sb("e_y", [P, D])
        idx = sb("e_idx", [P, 1], I32)
        gu, tp, pa, pd = ps("e_gu", [P, NB]), ps("e_tp", [P, D]), ps("e_pa", [P, NB]), ps("e_pd", [P, D])

        wl = [sem("wl0"), sem("wl1")]
        idx_ready, zeroed, filled = sem("idx_ready"), sem("e_zeroed"), sem("e_filled")
        zrow = sb("e_zero", [P, D])
        w_ready, gathered, turned, xT_ready = sem("w_ready"), sem("gathered"), sem("e_turned"), sem("xT_ready")
        gu_mm, th_ready, tmp_ready, av_ready = sem("gu_mm"), sem("th_ready"), sem("tmp_ready"), sem("av_ready")
        av_turned, aT_ready, d_mm, y_ready, y_out = sem("av_turned"), sem("aT_ready"), sem("d_mm"), sem("ey_ready"), sem("ey_out")
        KF = FE // P
        block = ctx.enter_context(nc.Block())
        blocks_less = lambda eng: eng.value_load(tab["blocks_less"][0:1, 0:1], min_val=E - LEAD, max_val=MAXB - LEAD)

        @block.sync
        def _(sp):
            def load(e, u):
                gu_w = w[:, u * WE:u * WE + KD * 2 * FE].rearrange("p (k a f) -> p k a f", k=KD, a=2)
                src = lambda t: io[t][0, ds(e, 1)].rearrange("o (k p) f -> p (o k) f", p=P)
                sp.dma_start(gu_w[:, :, 0], src("moe_w_gate")).then_inc(wl[u], 16)
                sp.dma_start(gu_w[:, :, 1], src("moe_w_up")).then_inc(wl[u], 16)
                sp.dma_start(w[:, u * WE + KD * 2 * FE:(u + 1) * WE].rearrange("p (k n) -> p k n", k=KF),
                             src("moe_w_down")).then_inc(wl[u], 16)
            load(0, 0)
            load(1, 1)
            sp.wait_ge(zeroed, 1)
            used = sp.value_load(tab["ends"][0:1, E - 1:E], min_val=E, max_val=MAXB)
            unused = sp.value_load(tab["unused"][0:1, 0:1], min_val=1, max_val=MAXB + 1)
            with sp.Fori(used, MAXB + 1) as b:
                sp.dma_start(yslot_dram[ds(b * P, P), :], zrow[:]).then_inc(filled, 16)
            sp.wait_ge(wl[0], 48)
            sp.sem_inc(w_ready, 1)
            with sp.Fori(0, (E - 2) // 2) as i:
                for u in range(2):
                    sp.wait_ge(wl[1 - u], (i + 1 + u) * 48)
                    sp.sem_inc(w_ready, 1)
                    last = sp.value_load(tab["ends"][0:1, ds(2 * i + u, 1)], min_val=1, max_val=MAXB)
                    sp.wait_ge(d_mm, last)
                    load(2 * i + u + 2, u)
            sp.wait_ge(wl[1], E // 2 * 48)
            sp.sem_inc(w_ready, 1)
            sp.wait_ge(filled, unused * 16)
            sp.nop(nofuse=True)

        @block.gpsimd
        def _(pool):
            nless = blocks_less(pool)

            def gather(b, first=False):
                if not first:
                    pool.wait_ge(turned, b)
                pool.nop(nofuse=True)
                nc.gpsimd.tensor_copy(idx[:], tab["slot_token"][:, ds(b, 1)]).then_inc(idx_ready, 1)
                pool.wait_ge(idx_ready, b + 1)
                pool.nop(nofuse=True)
                pool.indirect_dma_start(xg[:], None, hn2_dram, bass.IndirectOffsetOnAxis(ap=idx[:], axis=0))\
                    .then_inc(gathered, 16)

            def store(b):
                pool.wait_ge(y_ready, b + 1)
                pool.dma_start(yslot_dram[ds(b * P, P), :], ysb[:]).then_inc(y_out, 16)
            gather(0, True)
            gather(1)
            gather(2)
            with pool.Fori(0, nless) as i:
                gather(i + LEAD)
                store(i)
            for k in range(LEAD):
                store(nless + k)
            pool.wait_ge(y_out, (nless + LEAD) * 16)

        @block.scalar
        def _(act):
            nless = blocks_less(act)

            def tanh(b):
                act.wait_ge(gu_mm, b + 1)
                nc.scalar.activation(th[:], gu[:, 0:FE], ACT.Tanh, scale=0.5).then_inc(th_ready, 1)

            def evacuate(b):
                act.wait_ge(turned, b + 1)
                nc.scalar.activation(xT[:], tp[:], ACT.Copy).then_inc(xT_ready, 1)
            evacuate(0)
            with act.Fori(0, nless + (LEAD - 1)) as b:
                tanh(b)
                evacuate(b + 1)
            tanh(nless + (LEAD - 1))

        @block.vector
        def _(dve):
            nc.vector.memset(zrow[:], 0.0).then_inc(zeroed, 1)
            nless = blocks_less(dve)

            def act_product(b):
                dve.wait_ge(th_ready, b + 1)
                nc.vector.scalar_tensor_tensor(tmp[:], th[:], 1.0, gu[:, 0:FE], ALU.add, ALU.mult).then_inc(tmp_ready, 1)
                dve.wait_ge(tmp_ready, b + 1)
                nc.vector.tensor_tensor(av[:], tmp[:], gu[:, FE:2 * FE], ALU.mult).then_inc(av_ready, 1)

            def evacuate(b):
                dve.wait_ge(av_turned, b + 1)
                nc.vector.tensor_copy(aT[:], pa[:, 0:FE]).then_inc(aT_ready, 1)

            def y_scaled(b, first=False):
                dve.wait_ge(d_mm, b + 1)
                if not first:
                    dve.wait_ge(y_out, b * 16)
                nc.vector.scalar_tensor_tensor(ysb[:], pd[:], tab["slot_gate"][:, ds(b, 1)], g2row[:],
                                               ALU.mult, ALU.mult).then_inc(y_ready, 1)
            act_product(0)
            evacuate(0)
            act_product(1)
            y_scaled(0, True)
            evacuate(1)
            act_product(2)
            with dve.Fori(0, nless) as i:
                y_scaled(i + 1)
                evacuate(i + 2)
                act_product(i + 3)
            y_scaled(nless + 1)
            evacuate(nless + 2)
            y_scaled(nless + 2)

        @block.tensor
        def _(pe):
            nless = blocks_less(pe)

            def turn(b):
                pe.wait_ge(gathered, (b + 1) * 16)
                for k in range(KD):
                    last = nc.tensor.transpose(tp[:, k * P:(k + 1) * P], xg[:, k * P:(k + 1) * P], cst["ident"][:])
                last.then_inc(turned, 1)

            def gate_up(b, first=False):
                e1 = pe.value_load(tab["expert1"][0:1, ds(b, 1)], min_val=1, max_val=E)
                off = pe.value_load(tab["woff"][0:1, ds(b, 1)], min_val=0, max_val=WE)
                pe.wait_ge(w_ready, e1)
                pe.wait_ge(xT_ready, b + 1)
                if not first:
                    pe.wait_ge(av_ready, b)
                for k in range(KD):
                    last = nc.tensor.matmul(gu[:], xT[:, k * P:(k + 1) * P], w[:, ds(off + k * 2 * FE, 2 * FE)],
                                            start=(k == 0), stop=(k == KD - 1))
                last.then_inc(gu_mm, 1)

            def turn_act(b):
                pe.wait_ge(av_ready, b + 1)
                for k in range(KF):
                    last = nc.tensor.transpose(pa[:, k * P:(k + 1) * P], av[:, k * P:(k + 1) * P], cst["ident"][:])
                last.then_inc(av_turned, 1)

            def down(b, first=False):
                off = pe.value_load(tab["woff"][0:1, ds(b, 1)], min_val=0, max_val=WE)
                pe.wait_ge(aT_ready, b + 1)
                if not first:
                    pe.wait_ge(y_ready, b)
                for half in range(D // NB):
                    for k in range(KF):
                        last = nc.tensor.matmul(pd[:, half * NB:(half + 1) * NB], aT[:, k * P:(k + 1) * P],
                                                w[:, ds(off + (KD * 2 * FE + k * D + half * NB), NB)],
                                                start=(k == 0), stop=(k == KF - 1))
                last.then_inc(d_mm, 1)
            turn(0)
            gate_up(0, True)
            turn(1)
            gate_up(1)
            turn_act(0)
            turn(2)
            down(0, True)
            with pe.Fori(0, nless) as i:
                gate_up(i + 2)
                turn_act(i + 1)
                turn(i + 3)
                down(i + 1)
            gate_up(nless + 2)
            turn_act(nless + 1)
            down(nless + 1)
            turn_act(nless + 2)
            down(nless + 2)


def combine(nc, sem, cst, io, tab, x2, yslot_dram, out):
    ctx = ExitStack()
    with ctx:
        sb = lambda n, s, d=F32: ctx.enter_context(nc.sbuf_tensor(n, s, d))
        ps = lambda n, s: ctx.enter_context(nc.psum_tensor(n, s, F32))
        ya, yb, ob = sb("f_ya", [P, 2, D]), sb("f_yb", [P, 2, D]), sb("f_ob", [P, 2, D])
        fg = sb("f_g", [P, D])
        ssq, std, rstd = sb("f_ssq", [P, 2]), sb("f_std", [P, 2]), sb("f_rstd", [P, 2])
        junk = ps("f_junk", [P, D])
        idx = [sb(f"f_idx{u}", [P, TOPK], I32) for u in range(2)]
        fg_in, idx_ready = sem("f_in"), sem("f_idx_ready")
        ya_in, yb_in, stored = [[sem(f"f_{n}{u}") for u in range(2)] for n in ("ya", "yb", "st")]
        pair, summed, sqd, stdd, rec, normed = [sem("f_" + n) for n in ("pair", "summed", "sqd", "stdd", "rec", "normed")]
        block = ctx.enter_context(nc.Block())
        tile = lambda it: x2[:, ds(it, 1)].rearrange("p o n -> p (o n)")

        @block.gpsimd
        def _(pool):
            def gather(it, u):
                if at_least(it, 2):
                    pool.wait_ge(summed, it - 1)
                pool.nop(nofuse=True)
                nc.gpsimd.tensor_copy(idx[u][:].rearrange("p (c o) -> p c o", o=1), tab["pos"][:, :, ds(it, 1)])\
                    .then_inc(idx_ready, 1)
                pool.wait_ge(idx_ready, it + 1)
                pool.nop(nofuse=True)
                for c, (buf, s) in enumerate(((ya, ya_in), (yb, yb_in))):
                    pool.indirect_dma_start(buf[:, u], None, yslot_dram,
                                            bass.IndirectOffsetOnAxis(ap=idx[u][:, c:c + 1], axis=0)).then_inc(s[u], 16)
            pipelined(pool, NT, 2, [(gather, 0)])

        @block.sync
        def _(sp):
            sp.dma_start(fg[:], io["final_norm_g"].partition_broadcast(P)).then_inc(fg_in, 16)

            def store(it, u):
                sp.wait_ge(normed, it + 1)
                sp.dma_start(out[0, ds(it * P, P), :], ob[:, u]).then_inc(stored[u], 16)
            pipelined(sp, NT, 2, [(store, 0)])
            for u in range(2):
                sp.wait_ge(stored[u], NT // 2 * 16)

        @block.scalar
        def _(act):
            def squares(it, u):
                act.wait_ge(summed, it + 1)
                if at_least(it, 2):
                    act.wait_ge(rec, it - 1)
                act.nop(nofuse=True)
                nc.scalar.activation(junk[:], tile(it), ACT.Square, accum_out=ssq[:, u:u + 1]).then_inc(sqd, 1)
                act.wait_ge(sqd, it + 1)
                nc.scalar.activation(std[:, u:u + 1], ssq[:, u:u + 1], ACT.Sqrt, scale=1.0 / D,
                                     bias=cst["eps"][:]).then_inc(stdd, 1)
            pipelined(act, NT, 2, [(squares, 0)])

        @block.vector
        def _(dve):
            def add(it, u):
                dve.wait_ge(ya_in[u], it * 8 + 16 - u * 8)
                dve.wait_ge(yb_in[u], it * 8 + 16 - u * 8)
                nc.vector.tensor_tensor(ya[:, u], ya[:, u], yb[:, u], ALU.add).then_inc(pair, 1)
                dve.wait_ge(pair, it + 1)
                nc.vector.tensor_tensor(tile(it), tile(it), ya[:, u], ALU.add).then_inc(summed, 1)

            def norm(it, u):
                dve.wait_ge(stdd, it + 1)
                nc.vector.reciprocal(rstd[:, u:u + 1], std[:, u:u + 1]).then_inc(rec, 1)
                dve.wait_ge(rec, it + 1)
                if at_least(it, 2):
                    dve.wait_ge(stored[u], it * 8 - u * 8)
                nc.vector.scalar_tensor_tensor(ob[:, u], tile(it), rstd[:, u:u + 1], fg[:], ALU.mult, ALU.mult)\
                    .then_inc(normed, 1)
            dve.wait_ge(fg_in, 16)
            pipelined(dve, NT, 4, [(add, 0), (norm, 1)])


def build(nc, io, out):
    ctx = ExitStack()
    with ctx:
        sb = lambda n, s, d=F32: ctx.enter_context(nc.sbuf_tensor(n, s, d))
        sem = lambda n: ctx.enter_context(nc.semaphore(n))
        cst = {"ident": sb("ident", [P, P]), "ones": sb("ones", [P, P]), "eps": sb("eps", [P, 1])}
        cond = sb("cond", [P, KD])
        y_dram = nc.dram_tensor("y_scratch", (NT, P, KD, P), F32, kind="Internal").ap()
        mod_dram = nc.dram_tensor("mod_scratch", (P, 4 * D), F32, kind="Internal").ap()
        hn2_dram = nc.dram_tensor("hn2_scratch", (S, D), F32, kind="Internal").ap()
        made, cleared = sem("const_made"), sem("ident_cleared")
        with nc.Block() as block:
            @block.gpsimd
            def _(pool):
                nc.gpsimd.memset(cst["ident"][:], 0.0).then_inc(cleared, 1)
                nc.gpsimd.memset(cst["ones"][:], 1.0).then_inc(made, 1)
                nc.gpsimd.memset(cst["eps"][:], EPS).then_inc(made, 1)
                pool.wait_ge(cleared, 1)
                nc.gpsimd.affine_select(out=cst["ident"][:], in_=cst["ident"][:], compare_op=ALU.not_equal, fill=1.0,
                                        base=0, pattern=[[-1, P]], channel_multiplier=1).then_inc(made, 1)
                pool.wait_ge(made, 3)
        with nc.sbuf_tensor("hT_hi", [P, KD, S], F32R) as hT_hi, nc.sbuf_tensor("hT_lo", [P, KD, S], F32R) as hT_lo:
            norm_and_transpose(nc, sem, cst, io, hT_hi, hT_lo, cond)
            lru(nc, sem, cst, io, hT_hi, hT_lo, cond, y_dram, mod_dram)
        x2 = sb("x2", [P, NT, D])
        g2row = sb("g2row", [P, D])
        logits = sb("logits", [P, NT, E])
        out_and_norm(nc, sem, cst, io, x2, y_dram, mod_dram, hn2_dram, g2row, logits)
        tab = {"blocks_less": sb("t_blocks_less", [P, 1], I32), "unused": sb("t_unused", [P, 1], I32), "ends": sb("t_ends", [P, E], I32), "pos": sb("t_pos", [P, TOPK, NT], I32),
               "expert1": sb("t_expert1", [P, MAXB], I32), "woff": sb("t_woff", [P, MAXB], I32),
               "slot_token": sb("t_slot_token", [P, MAXB], I32), "slot_gate": sb("t_slot_gate", [P, MAXB])}
        yslot_dram = nc.dram_tensor("yslot_scratch", ((MAXB + 1) * P, D), F32, kind="Internal").ap()
        dispatch(nc, sem, cst, logits, tab)
        experts(nc, sem, cst, io, tab, hn2_dram, yslot_dram, g2row)
        combine(nc, sem, cst, io, tab, x2, yslot_dram, out)


_INS = ["x", "c", "ada_w", "ada_b", "norm1_g", "norm2_g", "lru_w_in", "lru_conv_w", "lru_conv_b", "lru_wa", "lru_ba",
        "lru_wx", "lru_bx", "lru_lambda", "lru_w_out", "router_w", "router_b", "moe_w_gate", "moe_w_up", "moe_w_down",
        "final_norm_g"]


def kernel(**inputs):
    import numpy as _np
    import concourse.bacc as _bacc
    from concourse import mybir as _mybir
    from concourse.bass_utils import run_bass_kernel_spmd as _run

    nc = _bacc.Bacc("TRN2", target_bir_lowering=False, num_devices=1)
    arrays, io = {}, {}
    for name in _INS:
        a = _np.ascontiguousarray(inputs[name])
        arrays[f"in_{name}_dram"] = a
        io[name] = nc.dram_tensor(f"in_{name}_dram", a.shape, _mybir.dt.from_np(a.dtype), kind="ExternalInput").ap()
    out = nc.dram_tensor("out_0_dram", (1, S, D), _mybir.dt.float32, kind="ExternalOutput").ap()
    build(nc, io, out)
    r = _run(nc, [arrays], core_ids=[0])
    return r.results[0]["out_0_dram"]
```

```python
import concourse.bass as bass
from concourse import mybir
from contextlib import ExitStack

F32 = mybir.dt.float32
F32R = mybir.dt.float32r
I32 = mybir.dt.int32
ALU = mybir.AluOpType
ACT = mybir.ActivationFunctionType
AX = mybir.AxisListType
ds = bass.ds

P = 128
D = 1024
S = 2048
KD = D // P
NT = S // P
NB = 512
EPS = 1e-6
LRU_C = 8.0
CONV = 4
HALF = S // 2
E = 16
G = 4
PER = E // G
FE = 256
TOPK = 2
MAXB = S * TOPK // P + E
LEAD = 3
WE = KD * 2 * FE + FE // P * D


def at_least(it, k):
    return not isinstance(it, int) or it >= k


def pipelined(eng, n, ramp, stages):
    def step(s):
        for stage, lag in stages:
            if 0 <= s - lag < n:
                stage(s - lag, (s - lag) % 2)
    for s in range(ramp):
        step(s)
    with eng.Fori(0, (n - ramp) // 2) as i:
        for u in range(2):
            for stage, lag in stages:
                stage(2 * i + (ramp + u - lag), (u - lag) % 2)
    for s in range(n, n + max(lag for _, lag in stages)):
        step(s)


def norm_and_transpose(nc, sem, cst, io, hT_hi, hT_lo, cond):
    ctx = ExitStack()
    with ctx:
        sb = lambda n, s, d=F32: ctx.enter_context(nc.sbuf_tensor(n, s, d))
        ps = lambda n, s: ctx.enter_context(nc.psum_tensor(n, s, F32))
        ada = sb("n_ada", [P, 2, KD, NB])
        acc = sb("n_acc", [P, 2, NB])
        brow = sb("n_brow", [P, 2, D])
        gain = sb("n_gain", [P, D])
        ct = sb("n_c", [P, KD])
        cth = sb("n_cth", [P, KD])
        xt = sb("n_x", [P, 2, D])
        junk = acc[:].rearrange("p a b -> p (a b)")
        hn = sb("n_hn", [P, 2, D])
        ssq = sb("n_ssq", [P, 2])
        std = sb("n_std", [P, 2])
        rstd = sb("n_rstd", [P, 2])
        pm = [ps("n_pm0", [P, NB]), ps("n_pm1", [P, NB])]
        pt = [ps("n_pt0", [P, D]), ps("n_pt1", [P, D])]

        c_in, rows_in = sem("c_in"), sem("rows_in")
        ada_in = [sem("ada_in0"), sem("ada_in1")]
        x_in = [sem("x_in0"), sem("x_in1")]
        cth_ready, cond_ready = sem("cth_ready"), sem("cond_ready")
        acc_step, summed, row_ready = sem("acc_step"), sem("summed"), sem("row_ready")
        ssq_ready, std_ready, rstd_ready = sem("ssq_ready"), sem("std_ready"), sem("rstd_ready")
        scaled, shifted, turned = sem("scaled"), sem("shifted"), sem("turned")
        hi_ready, lo_ready = sem("hi_ready"), sem("lo_ready")

        ada_v = io["ada_w"][0].rearrange("(p k) n -> p k n", k=KD)
        NCH = 2 * D // NB
        block = ctx.enter_context(nc.Block())

        @block.sync
        def _(sp):
            sp.dma_start(ct[:], io["c"][0].rearrange("(p k) -> p k", k=KD)).then_inc(c_in, 16)
            for n in range(2):
                sp.dma_start(ada[:, n], ada_v[:, :, n * NB:(n + 1) * NB]).then_inc(ada_in[n], 16)
            sp.dma_start(brow[:], io["ada_b"][0, 0:2 * D].partition_broadcast(P)
                         .rearrange("p (a n) -> p a n", a=2)).then_inc(rows_in, 16)
            sp.dma_start(gain[:], io["norm1_g"][0].partition_broadcast(P)).then_inc(rows_in, 16)
            for n in range(2, NCH):
                sp.wait_ge(acc_step, KD * (n - 1))
                sp.dma_start(ada[:, n % 2], ada_v[:, :, n * NB:(n + 1) * NB]).then_inc(ada_in[n % 2], 16)

            def load(it, u):
                if at_least(it, 2):
                    sp.wait_ge(scaled, it - 1)
                sp.dma_start(xt[:, u], io["x"][0, ds(it * P, P), :]).then_inc(x_in[u], 16)
            pipelined(sp, NT, 2, [(load, 0)])

        @block.scalar
        def _(act):
            act.wait_ge(c_in, 16)
            nc.scalar.activation(cth[:], ct[:], ACT.Tanh, scale=0.5).then_inc(cth_ready, 1)

            def squares(it, u):
                act.wait_ge(x_in[u], it * 8 + 16 - u * 8)
                if at_least(it, 2):
                    act.wait_ge(rstd_ready, it - 1)
                nc.scalar.activation(junk, xt[:, u], ACT.Square, accum_out=ssq[:, u:u + 1]).then_inc(ssq_ready, 1)
                act.wait_ge(ssq_ready, it + 1)
                nc.scalar.activation(std[:, u:u + 1], ssq[:, u:u + 1], ACT.Sqrt, scale=1.0 / D,
                                     bias=cst["eps"][:]).then_inc(std_ready, 1)

            def high(it, u):
                act.wait_ge(turned, it + 1)
                act.nop(nofuse=True)
                nc.scalar.activation(hT_hi[:, :, ds(it * P, P)], pt[u][:].rearrange("p (k n) -> p k n", k=KD),
                                     ACT.Copy).then_inc(hi_ready, 1)
            act.wait_ge(row_ready, NCH)
            pipelined(act, NT, 4, [(squares, 0), (high, 2)])

        @block.vector
        def _(dve):
            dve.wait_ge(cth_ready, 1)
            nc.vector.scalar_tensor_tensor(cond[:], cth[:], 1.0, ct[:], ALU.add, ALU.mult).then_inc(cond_ready, 1)
            dve.wait_ge(cond_ready, 1)
            nc.vector.tensor_scalar(cond[:], cond[:], 0.5, None, ALU.mult).then_inc(cond_ready, 1)
            dve.wait_ge(cond_ready, 2)
            dve.wait_ge(rows_in, 32)
            for n in range(NCH):
                a = acc[:, n % 2, :]
                dve.wait_ge(ada_in[n % 2], 16 * (n // 2 + 1))
                if n >= 2:
                    dve.wait_ge(summed, n - 1)
                nc.vector.tensor_scalar(a, ada[:, n % 2, 0, :], cond[:, 0:1], None, ALU.mult).then_inc(acc_step, 1)
                for k in range(1, KD):
                    dve.wait_ge(acc_step, KD * n + k)
                    nc.vector.scalar_tensor_tensor(a, ada[:, n % 2, k, :], cond[:, k:k + 1], a,
                                                   ALU.mult, ALU.add).then_inc(acc_step, 1)
            for n in range(NCH):
                row, cols = n * NB // D, ds(n * NB % D, NB)
                dve.wait_ge(summed, n + 1)
                if row == 0:
                    nc.vector.tensor_tensor(brow[:, 0, cols], pm[n % 2][:], brow[:, 0, cols], ALU.add).then_inc(row_ready, 1)
                else:
                    nc.vector.tensor_tensor(brow[:, 1, cols], pm[n % 2][:], brow[:, 1, cols], ALU.add).then_inc(cond_ready, 1)
                    dve.wait_ge(cond_ready, 1 + n)
                    nc.vector.scalar_tensor_tensor(brow[:, 1, cols], brow[:, 1, cols], 1.0, gain[:, cols],
                                                   ALU.add, ALU.mult).then_inc(row_ready, 1)
            dve.wait_ge(row_ready, NCH)

            def scale(it, u):
                dve.wait_ge(std_ready, it + 1)
                if at_least(it, 2):
                    dve.wait_ge(turned, it - 1)
                nc.vector.reciprocal(rstd[:, u:u + 1], std[:, u:u + 1]).then_inc(rstd_ready, 1)
                dve.wait_ge(rstd_ready, it + 1)
                nc.vector.scalar_tensor_tensor(hn[:, u], xt[:, u], rstd[:, u:u + 1], brow[:, 1], ALU.mult,
                                               ALU.mult).then_inc(scaled, 1)

            def low(it, u):
                dve.wait_ge(hi_ready, it + 1)
                nc.vector.tensor_tensor(hT_lo[:, :, ds(it * P, P)], pt[u][:].rearrange("p (k n) -> p k n", k=KD),
                                        hT_hi[:, :, ds(it * P, P)].bitcast(F32), ALU.subtract).then_inc(lo_ready, 1)
            pipelined(dve, NT, 4, [(scale, 0), (low, 2)])

        @block.gpsimd
        def _(pool):
            pool.wait_ge(row_ready, NCH)

            def shift(it, u):
                pool.wait_ge(scaled, it + 1)
                nc.gpsimd.tensor_tensor(hn[:, u], hn[:, u], brow[:, 0], ALU.add).then_inc(shifted, 1)
            pipelined(pool, NT, 2, [(shift, 0)])

        @block.tensor
        def _(pe):
            for n in range(NCH):
                pe.wait_ge(acc_step, KD * (n + 1))
                if n >= 2:
                    pe.wait_ge(row_ready, n - 1)
                nc.tensor.matmul(pm[n % 2][:], cst["ones"][:], acc[:, n % 2, :], start=True, stop=True).then_inc(summed, 1)

            def turn(it, u):
                pe.wait_ge(shifted, it + 1)
                if at_least(it, 2):
                    pe.wait_ge(lo_ready, it - 1)
                for k in range(KD):
                    last = nc.tensor.transpose(pt[u][:, k * P:(k + 1) * P], hn[:, u, k * P:(k + 1) * P], cst["ident"][:])
                last.then_inc(turned, 1)
            pipelined(pe, NT, 2, [(turn, 0)])


def lru(nc, sem, cst, io, hT_hi, hT_lo, cond, y_dram, mod_dram):
    ctx = ExitStack()
    with ctx:
        sb = lambda n, s, d=F32: ctx.enter_context(nc.sbuf_tensor(n, s, d))
        ps = lambda n, s: ctx.enter_context(nc.psum_tensor(n, s, F32))
        raw = {"x": sb("raw_x", [P, KD, P]), "g": sb("raw_g", [P, KD, P])}
        whi = {"x": sb("wx_hi", [P, KD, P], F32R), "g": sb("wg_hi", [P, KD, P], F32R)}
        wlo = {"x": sb("wx_lo", [P, KD, P], F32R), "g": sb("wg_lo", [P, KD, P], F32R)}
        gw = sb("gate_w", [P, 2, P])
        cw = sb("conv_w", [P, KD, CONV])
        cb = sb("conv_b", [P, KD])
        gb = sb("gate_b", [P, 2, KD])
        lam = sb("lam", [P, KD])
        dec = sb("decay", [P, 2, KD])
        sp_t = sb("sp_t", [P, 6, KD])
        xu = sb("xu", [P, 2, CONV - 1 + NB])
        zero = sb("zero3", [P, CONV - 1])
        XB, TR, TI, A, T, M, GE = [sb(n, [P, HALF]) for n in ("XB", "TR", "TI", "A", "T", "M", "GE")]
        carry = sb("carry", [P, 1])
        stg = sb("stg", [P, 2, KD // 2, NB])
        mtmp = sb("mtmp", [P, NB])
        macc = sb("macc", [P, NB])
        px = [ps("px0", [P, NB]), ps("px1", [P, NB])]
        pg = [ps("pg0", [P, NB]), ps("pg1", [P, NB])]
        pr, pi = ps("pr", [P, NB]), ps("pi", [P, NB])

        raw_in = {"x": sem("raw_x_in"), "g": sem("raw_g_in")}
        hi_done = {"x": sem("wx_hi_done"), "g": sem("wg_hi_done")}
        lo_done = {"x": sem("wx_lo_done"), "g": sem("wg_lo_done")}
        vec_in, vec_ready, gw_in = sem("vec_in"), sem("vec_ready"), sem("gw_in")
        x_mm, g_mm, gate_mm = sem("x_mm"), sem("g_mm"), sem("gate_mm")
        xu_ready, halo_ready, tap0, tap1, tap2, conv = [sem(n) for n in
                                                       ("xu_ready", "halo_ready", "tap0", "tap1", "tap2", "conv")]
        tr_ready, ti_ready, a_ready, t_ready, sq_ready, m_ready = [sem(n) for n in
                                                       ("tr_ready", "ti_ready", "a_ready", "t_ready", "sq_ready", "m_ready")]
        root_ready, ix_ready, b_ready, scan_ready, carried, gelu, y_ready, y_out = [sem(n) for n in
                          ("root_ready", "ix_ready", "b_ready", "scan_ready", "carried", "gelu", "y_ready", "y_out")]
        s_a, s_b = sem("sp_a"), sem("sp_b")
        stg_in = [sem("stg_in0"), sem("stg_in1")]
        mt, ma, mo = sem("mod_tmp"), sem("mod_acc"), sem("mod_out")
        zeroed = sem("zeroed")

        w_v = io["lru_w_in"][0].rearrange("(k p) n -> p k n", p=P)
        OFF = {"g": 0, "x": D}
        y_v = y_dram.rearrange("t p j n -> p j t n")
        NH = HALF // NB
        TH = HALF // P
        block = ctx.enter_context(nc.Block())

        def channels(eng, body):
            body(0, False)
            with eng.Fori(1, KD - 1) as j:
                body(j, False)
            body(KD - 1, True)

        @block.sync
        def _(sp):
            col = lambda a: a.rearrange("(j p) -> p j", p=P)
            sp.dma_start(raw["x"][:], w_v[:, :, D:D + P]).then_inc(raw_in["x"], 16)
            with nc.allow_non_contiguous_dma(reason="small vectors by channel"):
                sp.dma_start(lam[:], col(io["lru_lambda"][0]), allow_slow_non_contiguous=True).then_inc(vec_in, 16)
                sp.dma_start(cb[:], col(io["lru_conv_b"][0]), allow_slow_non_contiguous=True).then_inc(vec_in, 16)
                sp.dma_start(gb[:, 0], col(io["lru_ba"][0]), allow_slow_non_contiguous=True).then_inc(vec_in, 16)
                sp.dma_start(gb[:, 1], col(io["lru_bx"][0]), allow_slow_non_contiguous=True).then_inc(vec_in, 16)
                for w in range(CONV):
                    sp.dma_start(cw[:, :, w], col(io["lru_conv_w"][0, w]), allow_slow_non_contiguous=True).then_inc(vec_in, 16)

            def body(j, last):
                if at_least(j, 1):
                    sp.wait_ge(lo_done["g"], j)
                sp.dma_start(raw["g"][:], w_v[:, :, ds(j * P, P)]).then_inc(raw_in["g"], 16)
                if at_least(j, 1):
                    sp.wait_ge(gate_mm, j * 4)
                sp.dma_start(gw[:, 0], io["lru_wa"][0, ds(j, 1)].rearrange("o i q -> (o i) q")).then_inc(gw_in, 16)
                sp.dma_start(gw[:, 1], io["lru_wx"][0, ds(j, 1)].rearrange("o i q -> (o i) q")).then_inc(gw_in, 16)
                if not last:
                    sp.wait_ge(lo_done["x"], j + 1)
                    sp.dma_start(raw["x"][:], w_v[:, :, ds(j * P + (D + P), P)]).then_inc(raw_in["x"], 16)
                for h in range(2):
                    sp.wait_ge(y_ready, 2 * j + h + 1)
                    sp.dma_start(y_v[:, ds(j, 1), h * TH:(h + 1) * TH, :].rearrange("p o t n -> p (o t) n"),
                                 M[:].rearrange("p (t n) -> p t n", n=P)).then_inc(y_out, 16)
            channels(sp, body)
            sp.wait_ge(y_out, 16 * 2 * KD)

        @block.scalar
        def _(act):
            act.wait_ge(vec_in, 16 * (4 + CONV))
            nc.scalar.activation(sp_t[:, 0], lam[:], ACT.Abs).then_inc(s_a, 1)
            act.wait_ge(s_a, 1)
            nc.scalar.activation(sp_t[:, 1], sp_t[:, 0], ACT.Exp, scale=-1.0).then_inc(s_a, 1)
            act.wait_ge(s_b, 1)
            nc.scalar.activation(sp_t[:, 3], sp_t[:, 2], ACT.Ln).then_inc(s_a, 1)
            act.wait_ge(raw_in["x"], 16)
            nc.scalar.activation(whi["x"][:], raw["x"][:], ACT.Copy).then_inc(hi_done["x"], 1)
            act.wait_ge(zeroed, 1)
            nc.scalar.activation(xu[:, 0, 0:CONV - 1], zero[:], ACT.Copy).then_inc(halo_ready, 1)
            act.wait_ge(vec_ready, 1)

            def body(j, last):
                for h in range(2):
                    hh = 2 * j + h
                    for n in range(NH):
                        c = hh * NH + n
                        act.wait_ge(x_mm, c + 1)
                        if at_least(j, 1) or c >= 2:
                            act.wait_ge(conv, c - 1)
                        nc.scalar.activation(xu[:, n, CONV - 1:], px[n][:], ACT.Copy).then_inc(xu_ready, 1)
                        act.wait_ge(xu_ready, c + 1)
                        act.wait_ge(halo_ready, c + 1)
                        if n == 0 and (at_least(j, 1) or h):
                            act.wait_ge(ix_ready, hh)
                        act.nop(nofuse=True)
                        nc.scalar.activation(XB[:, n * NB:(n + 1) * NB], xu[:, n, 0:NB], ACT.Identity,
                                             scale=cw[:, ds(j, 1), 0], bias=cb[:, ds(j, 1)]).then_inc(tap0, 1)
                        if at_least(j, 1) or c >= 1:
                            act.wait_ge(conv, c)
                        tail = zero[:] if h == 1 and n == NH - 1 else xu[:, n, NB:]
                        if not (last and h == 1 and n == NH - 1):
                            nc.scalar.activation(xu[:, 1 - n, 0:CONV - 1], tail, ACT.Copy).then_inc(halo_ready, 1)
                        if h == 0 and n == 0:
                            act.wait_ge(raw_in["g"], 16 * (j + 1))
                            if at_least(j, 1):
                                act.wait_ge(g_mm, 4 * j)
                            nc.scalar.activation(whi["g"][:], raw["g"][:], ACT.Copy).then_inc(hi_done["g"], 1)
                        if h == 1 and n == NH - 1 and not last:
                            act.wait_ge(raw_in["x"], 16 * (j + 2))
                            nc.scalar.activation(whi["x"][:], raw["x"][:], ACT.Copy).then_inc(hi_done["x"], 1)
                    for n in range(NH):
                        c = hh * NH + n
                        act.wait_ge(gate_mm, c + 1)
                        if n == 0 and (at_least(j, 1) or h):
                            act.wait_ge(b_ready, hh)
                        act.nop(nofuse=True)
                        nc.scalar.activation(TR[:, n * NB:(n + 1) * NB], pr[:], ACT.Tanh, scale=0.5,
                                             bias=gb[:, 0, ds(j, 1)]).then_inc(tr_ready, 1)
                        act.nop(nofuse=True)
                        nc.scalar.activation(TI[:, n * NB:(n + 1) * NB], pi[:], ACT.Tanh, scale=0.5,
                                             bias=gb[:, 1, ds(j, 1)]).then_inc(ti_ready, 1)
                    act.wait_ge(tr_ready, (hh + 1) * NH)
                    if at_least(j, 1) or h:
                        act.wait_ge(scan_ready, hh)
                        act.wait_ge(y_out, 16 * hh)
                    act.nop(nofuse=True)
                    nc.scalar.activation(T[:], TR[:], ACT.Tanh, scale=dec[:, 0, ds(j, 1)], bias=dec[:, 0, ds(j, 1)])\
                        .then_inc(t_ready, 1)
                    act.nop(nofuse=True)
                    nc.scalar.activation(A[:], TR[:], ACT.Exp, scale=dec[:, 1, ds(j, 1)], bias=dec[:, 1, ds(j, 1)])\
                        .then_inc(a_ready, 1)
                    act.wait_ge(a_ready, hh + 1)
                    nc.scalar.activation(M[:], A[:], ACT.Square).then_inc(sq_ready, 1)
                    act.wait_ge(m_ready, hh + 1)
                    nc.scalar.activation(M[:], T[:], ACT.Sqrt, scale=0.25).then_inc(root_ready, 1)
                    for n in range(NH):
                        act.wait_ge(g_mm, hh * NH + n + 1)
                        if n == 0 and (at_least(j, 1) or h):
                            act.wait_ge(y_ready, hh)
                        nc.scalar.activation(GE[:, n * NB:(n + 1) * NB], pg[n][:], ACT.Gelu_apprx_tanh).then_inc(gelu, 1)
            channels(act, body)

        @block.vector
        def _(dve):
            nc.vector.memset(zero[:], 0.0).then_inc(zeroed, 1)
            dve.wait_ge(s_a, 2)
            nc.vector.tensor_scalar(sp_t[:, 2], sp_t[:, 1], 1.0, None, ALU.add).then_inc(s_b, 1)
            dve.wait_ge(s_b, 1)
            nc.vector.tensor_scalar(sp_t[:, 4], sp_t[:, 2], -1.0, None, ALU.add).then_inc(s_b, 1)
            dve.wait_ge(s_b, 2)
            nc.vector.tensor_scalar(sp_t[:, 5], sp_t[:, 4], 0.0, None, ALU.is_equal).then_inc(s_b, 1)
            dve.wait_ge(s_b, 3)
            dve.wait_ge(s_a, 3)
            nc.vector.tensor_tensor(sp_t[:, 3], sp_t[:, 3], sp_t[:, 5], ALU.add).then_inc(s_b, 1)
            nc.vector.tensor_tensor(sp_t[:, 4], sp_t[:, 4], sp_t[:, 5], ALU.add).then_inc(s_b, 1)
            dve.wait_ge(s_b, 5)
            nc.vector.tensor_tensor(sp_t[:, 3], sp_t[:, 3], sp_t[:, 1], ALU.mult).then_inc(s_b, 1)
            nc.vector.reciprocal(sp_t[:, 5], sp_t[:, 4]).then_inc(s_b, 1)
            dve.wait_ge(s_b, 7)
            nc.vector.tensor_tensor(sp_t[:, 3], sp_t[:, 3], sp_t[:, 5], ALU.mult).then_inc(s_b, 1)
            nc.vector.tensor_scalar(sp_t[:, 0], lam[:], -1.0, 0.0, ALU.mult, ALU.max).then_inc(s_b, 1)
            dve.wait_ge(s_b, 9)
            nc.vector.tensor_tensor(sp_t[:, 3], sp_t[:, 3], sp_t[:, 0], ALU.add).then_inc(s_b, 1)
            dve.wait_ge(s_b, 10)
            nc.vector.tensor_scalar(dec[:, 0], sp_t[:, 3], LRU_C / 2, None, ALU.mult).then_inc(s_b, 1)
            nc.vector.tensor_scalar(dec[:, 1], sp_t[:, 3], -LRU_C / 2, None, ALU.mult).then_inc(s_b, 1)
            nc.vector.tensor_scalar(gb[:], gb[:], 0.5, None, ALU.mult).then_inc(s_b, 1)
            dve.wait_ge(s_b, 13)
            nc.vector.memset(carry[:], 0.0).then_inc(vec_ready, 1)
            dve.wait_ge(hi_done["x"], 1)
            nc.vector.tensor_tensor(wlo["x"][:], raw["x"][:], whi["x"][:].bitcast(F32), ALU.subtract).then_inc(lo_done["x"], 1)

            def body(j, last):
                for h in range(2):
                    hh = 2 * j + h
                    for n in range(NH):
                        c = hh * NH + n
                        xb = XB[:, n * NB:(n + 1) * NB]
                        dve.wait_ge(tap0, c + 1)
                        for w, before, done in ((1, None, tap1), (2, tap1, tap2), (3, tap2, conv)):
                            if before is not None:
                                dve.wait_ge(before, c + 1)
                            nc.vector.scalar_tensor_tensor(xb, xu[:, n, w:w + NB], cw[:, ds(j, 1), w], xb,
                                                           ALU.mult, ALU.add).then_inc(done, 1)
                        if h == 0 and n == 0:
                            dve.wait_ge(hi_done["g"], j + 1)
                            nc.vector.tensor_tensor(wlo["g"][:], raw["g"][:], whi["g"][:].bitcast(F32), ALU.subtract)\
                                .then_inc(lo_done["g"], 1)
                        if h == 1 and n == NH - 1 and not last:
                            dve.wait_ge(hi_done["x"], j + 2)
                            nc.vector.tensor_tensor(wlo["x"][:], raw["x"][:], whi["x"][:].bitcast(F32), ALU.subtract)\
                                .then_inc(lo_done["x"], 1)
                    dve.wait_ge(ti_ready, (hh + 1) * NH)
                    dve.wait_ge(conv, (hh + 1) * NH)
                    nc.vector.scalar_tensor_tensor(TI[:], TI[:], 1.0, XB[:], ALU.add, ALU.mult).then_inc(ix_ready, 1)
                    dve.wait_ge(sq_ready, hh + 1)
                    nc.vector.scalar_tensor_tensor(T[:], M[:], 1.0, T[:], ALU.add, ALU.mult).then_inc(m_ready, 1)
                    dve.wait_ge(root_ready, hh + 1)
                    dve.wait_ge(ix_ready, hh + 1)
                    nc.vector.tensor_tensor(TI[:], TI[:], M[:], ALU.mult).then_inc(b_ready, 1)
                    dve.wait_ge(b_ready, hh + 1)
                    if at_least(j, 1) or h:
                        dve.wait_ge(carried, hh)
                    nc.vector.tensor_tensor_scan(M[:], A[:], TI[:], 0.0 if h == 0 else carry[:], ALU.mult, ALU.add)\
                        .then_inc(scan_ready, 1)
                    dve.wait_ge(scan_ready, hh + 1)
                    nc.vector.tensor_copy(carry[:], M[:, HALF - 1:HALF]).then_inc(carried, 1)
                    dve.wait_ge(carried, hh + 1)
                    dve.wait_ge(gelu, (hh + 1) * NH)
                    nc.vector.tensor_tensor(M[:], M[:], GE[:], ALU.mult).then_inc(y_ready, 1)
            channels(dve, body)

        @block.gpsimd
        def _(pool):
            ada_v = io["ada_w"][0].rearrange("(p k) n -> p k n", k=KD)
            KH = KD // 2
            NM = 4 * D // NB
            def load(m, q):
                pool.dma_start(stg[:, q], ada_v[:, q * KH:(q + 1) * KH, ds(m * NB + 2 * D, NB)]).then_inc(stg_in[q], 16)
            load(0, 0)
            load(0, 1)
            def body(m, last):
                for k in range(KD):
                    q = k // KH
                    if k % KH == 0:
                        pool.wait_ge(stg_in[q], 16 * (m + 1))
                    if k == 0:
                        if at_least(m, 1):
                            pool.wait_ge(mo, 16 * m)
                        pool.nop(nofuse=True)
                        nc.gpsimd.tensor_scalar(macc[:], stg[:, q, k % KH], cond[:, k:k + 1], 0.0, ALU.mult, ALU.add).then_inc(ma, 1)
                        continue
                    pool.wait_ge(ma, m * KD + k)
                    pool.nop(nofuse=True)
                    nc.gpsimd.tensor_scalar(mtmp[:], stg[:, q, k % KH], cond[:, k:k + 1], 0.0, ALU.mult, ALU.add).then_inc(mt, 1)
                    pool.wait_ge(mt, m * (KD - 1) + k)
                    nc.gpsimd.tensor_tensor(macc[:], macc[:], mtmp[:], ALU.add).then_inc(ma, 1)
                    if k % KH == KH - 1:
                        pool.wait_ge(ma, m * KD + k + 1)
                        if not last:
                            load(m + 1, q)
                pool.dma_start(mod_dram[:, ds(m * NB, NB)], macc[:]).then_inc(mo, 16)
            body(0, False)
            with pool.Fori(1, NM - 1) as m:
                body(m, False)
            body(NM - 1, True)
            pool.wait_ge(mo, 16 * NM)

        @block.tensor
        def _(pe):
            def project(br, dst, tok):
                for k in range(KD):
                    cols = slice(tok, tok + NB)
                    nc.tensor.matmul(dst[:], whi[br][:, k], hT_hi[:, k, cols], start=(k == 0), stop=False)
                    nc.tensor.matmul(dst[:], whi[br][:, k], hT_lo[:, k, cols], start=False, stop=False)
                    last = nc.tensor.matmul(dst[:], wlo[br][:, k], hT_hi[:, k, cols], start=False, stop=(k == KD - 1))
                return last

            def body(j, last):
                def gates(h, n):
                    c = (2 * j + h) * NH + n
                    if h == 0 and n == 0:
                        pe.wait_ge(gw_in, 32 * (j + 1))
                    pe.wait_ge(conv, c + 1)
                    if at_least(j, 1) or c >= 1:
                        pe.wait_ge(ti_ready, c)
                    nc.tensor.matmul(pr[:], gw[:, 0], XB[:, n * NB:(n + 1) * NB], start=True, stop=True)
                    nc.tensor.matmul(pi[:], gw[:, 1], XB[:, n * NB:(n + 1) * NB], start=True, stop=True).then_inc(gate_mm, 1)

                for h in range(2):
                    hh = 2 * j + h
                    if h == 0:
                        pe.wait_ge(lo_done["x"], j + 1)
                    for n in range(NH):
                        if at_least(j, 1) or h:
                            pe.wait_ge(xu_ready, hh * NH + n - 1)
                        project("x", px[n], (h * NH + n) * NB).then_inc(x_mm, 1)
                    gates(h, 0)
                    if h == 0:
                        pe.wait_ge(lo_done["g"], j + 1)
                    for n in range(NH):
                        if at_least(j, 1) or h:
                            pe.wait_ge(gelu, hh * NH + n - 1)
                        project("g", pg[n], (h * NH + n) * NB).then_inc(g_mm, 1)
                        if n == 0:
                            gates(h, 1)
            channels(pe, body)


def out_and_norm(nc, sem, cst, io, x2, y_dram, mod_dram, hn2_dram, g2row, logits):
    ctx = ExitStack()
    with ctx:
        sb = lambda n, s, d=F32: ctx.enter_context(nc.sbuf_tensor(n, s, d))
        ps = lambda n, s: ctx.enter_context(nc.psum_tensor(n, s, F32))
        macc = x2[:, 0:4, :].rearrange("p t n -> p (t n)")
        g1row, sh2, sc2 = sb("g1row", [P, D]), sb("sh2", [P, D]), sb("sc2", [P, D])
        gain = sb("b_gain", [P, D])
        rw = sb("router_w", [P, KD, E])
        rb = sb("router_b", [P, E])
        wr = sb("b_wraw", [P, 2, D])
        wo_hi, wo_lo = sb("wo_hi", [P, KD, D], F32R), sb("wo_lo", [P, KD, D], F32R)
        yt, xr = sb("b_yt", [P, 2, D]), sb("b_xr", [P, 2, D])
        yh = [sb(f"b_yh{u}", [P, D], F32R) for u in range(2)]
        yl = [sb(f"b_yl{u}", [P, D], F32R) for u in range(2)]
        hn = sb("b_hn", [P, 2, D])
        hT = sb("b_hT", [P, D])
        ssq, std, rstd = sb("b_ssq", [P, 2]), sb("b_std", [P, 2]), sb("b_rstd", [P, 2])
        po = [ps("po0", [P, D]), ps("po1", [P, D])]
        pt = ps("b_pt", [P, D])
        pl = ps("pl", [P, NB])
        junk = pt[:]

        rows_in, macc_in, rsum, rows = sem("b_rows_in"), sem("macc_in"), sem("b_rsum"), sem("b_rows")
        wr_in = [sem("wr_in0"), sem("wr_in1")]
        wo_h, wo_l = sem("wo_h"), sem("wo_l")
        y_in = [sem("by_in0"), sem("by_in1")]
        x_in = [sem("bx_in0"), sem("bx_in1")]
        yhi, ylo, mm, gated, resid = sem("b_yhi"), sem("b_ylo"), sem("b_mm"), sem("b_gated"), sem("b_resid")
        sqd, stdd, rec, scaled, shifted = sem("b_sq"), sem("b_std_s"), sem("b_rec"), sem("b_scaled"), sem("b_shifted")
        turned, hT_ready, routed, logit = sem("b_turned"), sem("b_hT_s"), sem("b_routed"), sem("b_logit")
        stored = [sem("b_stored0"), sem("b_stored1")]
        half_sum = sem("b_sc")
        w_v = io["lru_w_out"][0].rearrange("(k p) n -> k p n", p=P)
        y_v = y_dram.rearrange("t p j n -> t p (j n)")
        NR = 4 * D // NB
        dst = [g1row, sh2, sc2, g2row]
        block = ctx.enter_context(nc.Block())

        @block.sync
        def _(sp):
            sp.dma_start(macc, mod_dram).then_inc(macc_in, 16)
            for q in range(4):
                sp.dma_start(dst[q][:], io["ada_b"][0, (2 + q) * D:(3 + q) * D].partition_broadcast(P)).then_inc(rows_in, 16)
            sp.dma_start(gain[:], io["norm2_g"][0].partition_broadcast(P)).then_inc(rows_in, 16)
            sp.dma_start(rw[:], io["router_w"].rearrange("(k p) e -> p k e", p=P)).then_inc(rows_in, 16)
            sp.dma_start(rb[:], io["router_b"].partition_broadcast(P)).then_inc(rows_in, 16)
            for k in range(KD):
                if k >= 2:
                    sp.wait_ge(wo_l, k - 1)
                sp.dma_start(wr[:, k % 2], w_v[k]).then_inc(wr_in[k % 2], 16)

            def load(it, u):
                if at_least(it, 2):
                    sp.wait_ge(ylo, it - 1)
                    sp.wait_ge(resid, it - 1)
                sp.dma_start(yt[:, u], y_v[ds(it, 1)].rearrange("o p n -> (o p) n")).then_inc(y_in[u], 16)
                sp.dma_start(xr[:, u], io["x"][0, ds(it * P, P), :]).then_inc(x_in[u], 16)

            def store(it, u):
                sp.wait_ge(shifted, it + 1)
                sp.dma_start(hn2_dram[ds(it * P, P), :], hn[:, u]).then_inc(stored[u], 16)
            pipelined(sp, NT, 6, [(load, 0), (store, 4)])
            for u in range(2):
                sp.wait_ge(stored[u], 16 * NT // 2)

        @block.scalar
        def _(act):
            for k in range(KD):
                act.wait_ge(wr_in[k % 2], 16 * (k // 2 + 1))
                nc.scalar.activation(wo_hi[:, k], wr[:, k % 2], ACT.Copy).then_inc(wo_h, 1)

            def high(it, u):
                act.wait_ge(y_in[u], it * 8 + 16 - u * 8)
                if at_least(it, 2):
                    act.wait_ge(mm, it - 1)
                nc.scalar.activation(yh[u][:], yt[:, u], ACT.Copy).then_inc(yhi, 1)

            def squares(it, u):
                act.wait_ge(resid, it + 1)
                if at_least(it, 2):
                    act.wait_ge(rec, it - 1)
                act.nop(nofuse=True)
                nc.scalar.activation(hn[:, u], x2[:, ds(it, 1)].rearrange("p o n -> p (o n)"), ACT.Square,
                                     accum_out=ssq[:, u:u + 1]).then_inc(sqd, 1)
                act.wait_ge(sqd, it + 1)
                nc.scalar.activation(std[:, u:u + 1], ssq[:, u:u + 1], ACT.Sqrt, scale=1.0 / D,
                                     bias=cst["eps"][:]).then_inc(stdd, 1)

            def squares_free(it, u):
                if at_least(it, 2):
                    act.wait_ge(turned, it - 1)
                    act.wait_ge(stored[u], it * 8 - u * 8)
                squares(it, u)

            def evacuate(it, u):
                act.wait_ge(turned, it + 1)
                if at_least(it, 1):
                    act.wait_ge(routed, it)
                nc.scalar.activation(hT[:], pt[:], ACT.Copy).then_inc(hT_ready, 1)
            pipelined(act, NT, 6, [(high, 0), (squares_free, 2), (evacuate, 4)])

        @block.vector
        def _(dve):
            dve.wait_ge(rows_in, 16 * 7)
            for n in range(NR):
                q, cols = n * NB // D, ds(n * NB % D, NB)
                dve.wait_ge(rsum, n + 1)
                nc.vector.tensor_tensor(dst[q][:, cols], po[n % 2][:, 0:NB], dst[q][:, cols], ALU.add).then_inc(rows, 1)
                if n == 3 * D // NB - 1:
                    dve.wait_ge(rows, n + 1)
                    nc.vector.scalar_tensor_tensor(sc2[:], sc2[:], 1.0, gain[:], ALU.add, ALU.mult).then_inc(half_sum, 1)
            dve.wait_ge(rows, NR)
            dve.wait_ge(half_sum, 1)
            for k in range(KD):
                dve.wait_ge(wo_h, k + 1)
                nc.vector.tensor_tensor(wo_lo[:, k], wr[:, k % 2], wo_hi[:, k].bitcast(F32), ALU.subtract).then_inc(wo_l, 1)

            def low(it, u):
                dve.wait_ge(yhi, it + 1)
                if at_least(it, 2):
                    dve.wait_ge(mm, it - 1)
                nc.vector.tensor_tensor(yl[u][:], yt[:, u], yh[u][:].bitcast(F32), ALU.subtract).then_inc(ylo, 1)

            def gate(it, u):
                dve.wait_ge(mm, it + 1)
                nc.vector.tensor_tensor(x2[:, ds(it, 1)].rearrange("p o n -> p (o n)"), po[u][:], g1row[:],
                                        ALU.mult).then_inc(gated, 1)

            def norm(it, u):
                dve.wait_ge(stdd, it + 1)
                nc.vector.reciprocal(rstd[:, u:u + 1], std[:, u:u + 1]).then_inc(rec, 1)
                dve.wait_ge(rec, it + 1)
                nc.vector.scalar_tensor_tensor(hn[:, u], x2[:, ds(it, 1)].rearrange("p o n -> p (o n)"),
                                               rstd[:, u:u + 1], sc2[:], ALU.mult, ALU.mult).then_inc(scaled, 1)

            def bias(it, u):
                dve.wait_ge(routed, it + 1)
                nc.vector.tensor_tensor(logits[:, ds(it, 1)].rearrange("p o n -> p (o n)"), pl[:, 0:E], rb[:],
                                        ALU.add).then_inc(logit, 1)
            pipelined(dve, NT, 6, [(low, 0), (gate, 1), (norm, 2), (bias, 4)])

        @block.gpsimd
        def _(pool):
            def add_x(it, u):
                pool.wait_ge(gated, it + 1)
                pool.wait_ge(x_in[u], it * 8 + 16 - u * 8)
                x2t = x2[:, ds(it, 1)].rearrange("p o n -> p (o n)")
                nc.gpsimd.tensor_tensor(x2t, x2t, xr[:, u], ALU.add).then_inc(resid, 1)

            def shift(it, u):
                pool.wait_ge(scaled, it + 1)
                nc.gpsimd.tensor_tensor(hn[:, u], hn[:, u], sh2[:], ALU.add).then_inc(shifted, 1)
            pipelined(pool, NT, 4, [(add_x, 0), (shift, 1)])

        @block.tensor
        def _(pe):
            pe.wait_ge(macc_in, 16)
            for n in range(NR):
                if n >= 2:
                    pe.wait_ge(rows, n - 1)
                nc.tensor.matmul(po[n % 2][:, 0:NB], cst["ones"][:], macc[:, n * NB:(n + 1) * NB],
                                 start=True, stop=True).then_inc(rsum, 1)
            pe.wait_ge(wo_l, KD)
            pe.wait_ge(rows, NR)

            def main(it, u, half):
                if half == 0:
                    pe.wait_ge(ylo, it + 1)
                    if at_least(it, 2):
                        pe.wait_ge(gated, it - 1)
                cols = slice(half * NB, (half + 1) * NB)
                for k in range(KD):
                    tok = slice(k * P, (k + 1) * P)
                    nc.tensor.matmul(po[u][:, cols], yh[u][:, tok], wo_hi[:, k, cols], start=(k == 0), stop=False)
                    nc.tensor.matmul(po[u][:, cols], yh[u][:, tok], wo_lo[:, k, cols], start=False, stop=False)
                    last = nc.tensor.matmul(po[u][:, cols], yl[u][:, tok], wo_hi[:, k, cols], start=False, stop=(k == KD - 1))
                if half == 1:
                    last.then_inc(mm, 1)

            def turn(it, u):
                pe.wait_ge(shifted, it + 1)
                if at_least(it, 1):
                    pe.wait_ge(hT_ready, it)
                for k in range(KD):
                    last = nc.tensor.transpose(pt[:, k * P:(k + 1) * P], hn[:, u, k * P:(k + 1) * P], cst["ident"][:])
                last.then_inc(turned, 1)

            def route(it, u):
                pe.wait_ge(hT_ready, it + 1)
                if at_least(it, 1):
                    pe.wait_ge(logit, it)
                for k in range(KD):
                    last = nc.tensor.matmul(pl[:, 0:E], hT[:, k * P:(k + 1) * P], rw[:, k], start=(k == 0), stop=(k == KD - 1))
                last.then_inc(routed, 1)
            pipelined(pe, NT, 4, [(lambda it, u: main(it, u, 0), 0), (turn, 3),
                                  (lambda it, u: main(it, u, 1), 0), (route, 3)])


DOWN = KD * 2 * FE
NQ = 4
QW = WE // NQ
QLOADS = (2, 2, 3, 2)


def load_quarter(sp, io, w, e, q):
    raw, arrived = w["raw"][:, q % 2, :], w["in"][q]
    KQ = QW // (2 * FE)
    src = lambda t: io[t][0, ds(e, 1)].rearrange("o (k p) f -> p (o k) f", p=P)
    if q < 3:
        ks = slice(q * KQ, min((q + 1) * KQ, KD))
        nk = ks.stop - ks.start
        dst = raw[:, 0:nk * 2 * FE].rearrange("p (k a f) -> p k a f", k=nk, a=2)
        sp.dma_start(dst[:, :, 0], src("moe_w_gate")[:, ks]).then_inc(arrived, 16)
        sp.dma_start(dst[:, :, 1], src("moe_w_up")[:, ks]).then_inc(arrived, 16)
    down = src("moe_w_down")
    if q == 2:
        sp.dma_start(raw[:, nk * 2 * FE:], down[:, 0, 0:QW - nk * 2 * FE]).then_inc(arrived, 16)
    if q == 3:
        sp.dma_start(raw[:, 0:NB], down[:, 0, NB:D]).then_inc(arrived, 16)
        sp.dma_start(raw[:, NB:], down[:, 1]).then_inc(arrived, 16)


def dispatch(nc, sem, cst, io, logits, tab, w):
    ctx = ExitStack()
    with ctx:
        sb = lambda n, s, d=F32: ctx.enter_context(nc.sbuf_tensor(n, s, d))
        ps = lambda n, s: ctx.enter_context(nc.psum_tensor(n, s, F32))
        prob, work, work2, oh1, oh2, mask = [sb(n, [P, NT, E]) for n in ("prob", "work", "work2", "oh1", "oh2", "mask")]
        mx, m1, m2, vm = [sb(n, [P, NT]) for n in ("d_mx", "d_m1", "d_m2", "d_vm")]
        gs, gq = sb("d_gs", [P, NT, G]), sb("d_gq", [P, NT, G])
        gates = sb("d_gates", [P, TOPK, NT])
        below = sb("below", [P, P])
        slot_no, block_no = sb("slot_no", [P, P]), sb("block_no", [P, MAXB])
        rank_w, thresh = sb("rank_w", [P, E]), sb("thresh", [P, E])
        cnt, nblk, ends, start, ones_e = [sb(n, [P, E]) for n in ("cnt", "nblk", "ends", "start", "ones_e")]
        begin, second, flag = sb("begin", [P, E]), sb("second", [P, E]), sb("d_flag", [P, MAXB])
        cmp = sb("cmp", [P, E, E])
        cmpb = sb("cmpb", [P, MAXB, E])
        eb, par = sb("eb", [P, MAXB]), sb("par", [P, MAXB])
        pari = sb("pari", [P, MAXB], I32)
        posf = sb("posf", [P, TOPK, NT])
        ri, bi = sb("ri", [P, TOPK * NT], I32), sb("bi", [P, TOPK * NT], I32)
        rf, bf = sb("rf", [P, TOPK * NT]), sb("bf", [P, TOPK * NT])
        tok2 = sb("tok2", [P, TOPK * NT])
        pick = [sb(f"pick{u}", [P, P]) for u in range(2)]
        place = sb("place", [P, 2, 2, MAXB])
        prank, pcnt, pslot = ps("prank", [P, NB]), ps("pcnt", [P, NB]), ps("pslot", [P, NB])

        consts, dve_done, exp_in, exp_out = sem("d_consts"), sem("d_step"), sem("exp_in"), sem("exp_out")
        mask_ready, ranked, picked, slotted = sem("mask_ready"), sem("ranked"), sem("picked"), sem("slotted")
        block = ctx.enter_context(nc.Block())

        @block.gpsimd
        def _(pool):
            nc.gpsimd.memset(below[:], 1.0).then_inc(consts, 1)
            nc.gpsimd.memset(ones_e[:], 1.0).then_inc(consts, 1)
            pool.wait_ge(consts, 2)
            nc.gpsimd.affine_select(out=below[:], in_=below[:], compare_op=ALU.is_gt, fill=0.0, base=0,
                                    pattern=[[1, P]], channel_multiplier=-1).then_inc(consts, 1)
            io_ = lambda t, pat, base, cm: nc.gpsimd.iota(t, pat, base=base, channel_multiplier=cm,
                                                          allow_small_or_imprecise_dtypes=True).then_inc(consts, 1)
            io_(slot_no[:], [[1, P]], 0, 0)
            io_(block_no[:], [[1, MAXB]], 0, 0)
            io_(rank_w[:], [[-1, E]], E, 0)
            io_(thresh[:], [[P, E]], 0, 0)
            io_(tok2[:], [[0, TOPK], [P, NT]], 0, 1)
            for q in range(NQ):
                cols = slice(q * QW, (q + 1) * QW)
                pool.wait_ge(w["hi_done"], q + 1)
                nc.gpsimd.tensor_tensor(w["lo"][:, cols], w["raw"][:, q % 2], w["hi"][:, cols].bitcast(F32),
                                        ALU.subtract).then_inc(w["lo_done"], 1)

        @block.sync
        def _(sp):
            for q in range(NQ):
                if q >= 2:
                    sp.wait_ge(w["lo_done"], q - 1)
                load_quarter(sp, io, w, 0, q)

        @block.scalar
        def _(act):
            act.wait_ge(exp_in, 1)
            nc.scalar.activation(prob[:], work[:], ACT.Exp).then_inc(exp_out, 1)
            for q in range(NQ):
                cols = slice(q * QW, (q + 1) * QW)
                act.wait_ge(w["in"][q], 16 * QLOADS[q])
                nc.scalar.activation(w["hi"][:, cols], w["raw"][:, q % 2], ACT.Copy).then_inc(w["hi_done"], 1)

        @block.vector
        def _(dve):
            n = [0]
            v = nc.vector

            def done(ins):
                n[0] += 1
                ins.then_inc(dve_done, 1)
                dve.wait_ge(dve_done, n[0])
            wide = lambda a, k: a.unsqueeze(2).to_broadcast([a.shape[0], a.shape[1], k])
            row = lambda a, k: a.unsqueeze(1).to_broadcast([P, k, a.shape[-1]])

            done(v.tensor_reduce(mx[:], logits[:], AX.X, ALU.max))
            v.tensor_tensor(work[:], logits[:], wide(mx[:], E), ALU.subtract).then_inc(exp_in, 1)
            dve.wait_ge(exp_out, 1)
            done(v.tensor_reduce(mx[:], prob[:], AX.X, ALU.add))
            done(v.reciprocal(vm[:], mx[:]))
            done(v.tensor_tensor(prob[:], prob[:], wide(vm[:], E), ALU.mult))
            q = prob[:].rearrange("p t (g m) -> p t g m", m=PER)
            done(v.tensor_tensor(gs[:], q[:, :, :, 0], q[:, :, :, 1], ALU.add))
            for a in range(PER):
                for b in range(a + 1, PER):
                    if (a, b) != (0, 1):
                        done(v.tensor_tensor(gq[:], q[:, :, :, a], q[:, :, :, b], ALU.add))
                        done(v.tensor_tensor(gs[:], gs[:], gq[:], ALU.max))
            dve.wait_ge(consts, 8)

            def first_of(out, vals, top, k):
                done(v.tensor_reduce(top, vals, AX.X, ALU.max))
                done(v.tensor_tensor(out, vals, wide(top, k), ALU.is_equal))
                done(v.tensor_tensor(out, out, row(rank_w[:, 0:k], NT), ALU.mult))
                done(v.tensor_reduce(vm[:], out, AX.X, ALU.max))
                done(v.tensor_tensor(out, out, wide(vm[:], k), ALU.is_equal))
            first_of(gq[:], gs[:], mx[:], G)
            inb = gq[:].rearrange("p t g -> p (t g)")
            w3 = work[:].rearrange("p t (g m) -> p (t g) m", m=PER)
            p3 = prob[:].rearrange("p t (g m) -> p (t g) m", m=PER)
            done(v.tensor_tensor(w3, p3, wide(inb, PER), ALU.mult))
            done(v.tensor_scalar(gq[:], gq[:], -1.0, None, ALU.add))
            done(v.tensor_tensor(w3, w3, wide(inb, PER), ALU.add))
            first_of(oh1[:], work[:], m1[:], E)
            done(v.scalar_tensor_tensor(work2[:], oh1[:], -4.0, work[:], ALU.mult, ALU.add))
            first_of(oh2[:], work2[:], m2[:], E)
            v.tensor_tensor(mask[:], oh1[:], oh2[:], ALU.add).then_inc(mask_ready, 1)
            done(v.tensor_tensor(mx[:], m1[:], m2[:], ALU.add))
            done(v.reciprocal(vm[:], mx[:]))
            done(v.tensor_tensor(gates[:, 0], m1[:], vm[:], ALU.mult))
            done(v.tensor_tensor(gates[:, 1], m2[:], vm[:], ALU.mult))
            done(v.memset(thresh[:, 0:1], -1.0))
            dve.wait_ge(ranked, 1)
            done(v.tensor_copy(cnt[:], pcnt[:, 0:E]))
            done(v.tensor_tensor(cmp[:], wide(cnt[:], E), row(thresh[:], E), ALU.is_gt))
            done(v.tensor_reduce(nblk[:], cmp[:], AX.X, ALU.add))
            done(v.tensor_tensor_scan(ends[:], ones_e[:], nblk[:], 0.0, ALU.mult, ALU.add))
            done(v.tensor_tensor(start[:], ends[:], nblk[:], ALU.subtract))
            done(v.tensor_copy(begin[:], start[:]))
            done(v.tensor_scalar(second[:], nblk[:], 1.0, None, ALU.is_gt))
            done(v.tensor_tensor(second[:], second[:], begin[:], ALU.add))
            done(v.tensor_scalar(start[:], start[:], float(P), None, ALU.mult))
            done(v.tensor_copy(tab["ends"][:], ends[:]))
            done(v.tensor_scalar(nblk[:, 0:1], ends[:, E - 1:E], -float(LEAD), None, ALU.add))
            done(v.tensor_copy(tab["blocks_less"][:], nblk[:, 0:1]))
            done(v.tensor_scalar(nblk[:, 0:1], ends[:, E - 1:E], -1.0, float(MAXB + 1), ALU.mult, ALU.add))
            done(v.tensor_copy(tab["unused"][:], nblk[:, 0:1]))
            pr = prank[:, 0:NT * E].rearrange("p (t e) -> p t e", e=E)
            done(v.tensor_tensor(work[:], pr, row(start[:], NT), ALU.add))
            for c, oh in enumerate((oh1, oh2)):
                done(v.tensor_tensor(work2[:], work[:], oh[:], ALU.mult))
                done(v.tensor_reduce(posf[:, c], work2[:], AX.X, ALU.add))
            pos_i = tab["pos"][:].rearrange("p c t -> p (c t)")
            done(v.tensor_copy(pos_i, posf[:].rearrange("p c t -> p (c t)")))
            done(v.tensor_scalar(ri[:], pos_i, P - 1, None, ALU.bitwise_and))
            done(v.tensor_scalar(bi[:], pos_i, P.bit_length() - 1, None, ALU.logical_shift_right))
            done(v.tensor_copy(rf[:], ri[:]))
            done(v.tensor_copy(bf[:], bi[:]))
            done(v.tensor_tensor(cmpb[:], wide(block_no[:], E), row(ends[:], MAXB), ALU.is_ge))
            done(v.tensor_reduce(eb[:], cmpb[:], AX.X, ALU.add))
            done(v.tensor_copy(pari[:], eb[:]))
            done(v.tensor_copy(tab["expert"][:], eb[:]))
            done(v.tensor_scalar(pari[:], pari[:], 1, None, ALU.bitwise_and))
            done(v.tensor_copy(par[:], pari[:]))
            done(v.tensor_scalar(par[:], par[:], float(WE), None, ALU.mult))
            done(v.tensor_copy(tab["woff"][:], par[:]))
            done(v.tensor_scalar(par[:], par[:], -1.0, float(WE), ALU.mult, ALU.add))
            done(v.tensor_copy(tab["woff_next"][:], par[:]))
            done(v.tensor_tensor(cmpb[:], wide(block_no[:], E), row(begin[:], MAXB), ALU.is_equal))
            done(v.tensor_reduce(par[:], cmpb[:], AX.X, ALU.add))
            done(v.tensor_scalar(flag[:], eb[:], float(E - 1), None, ALU.is_lt))
            done(v.tensor_tensor(par[:], par[:], flag[:], ALU.mult))
            done(v.tensor_copy(tab["split0"][:], par[:]))
            done(v.tensor_tensor(cmpb[:], wide(block_no[:], E), row(second[:], MAXB), ALU.is_equal))
            done(v.tensor_reduce(par[:], cmpb[:], AX.X, ALU.add))
            done(v.tensor_tensor(par[:], par[:], flag[:], ALU.mult))
            done(v.tensor_copy(tab["split1"][:], par[:]))
            done(v.tensor_tensor(cmpb[:], wide(block_no[:], E), row(begin[:], MAXB), ALU.is_ge))
            done(v.tensor_tensor(cmpb[:], cmpb[:], row(begin[:], MAXB), ALU.mult))
            done(v.tensor_reduce(par[:], cmpb[:], AX.X, ALU.max))
            done(v.tensor_scalar(par[:], par[:], 1.0, None, ALU.max))
            done(v.tensor_copy(tab["before"][:], par[:]))
            done(v.tensor_scalar(eb[:], eb[:], 1.0, None, ALU.add))
            done(v.tensor_copy(tab["expert1"][:], eb[:]))
            gate2 = gates[:].rearrange("p c t -> p (c t)")

            def factors(it, u):
                if at_least(it, 2):
                    dve.wait_ge(slotted, it - 1)
                v.tensor_scalar(pick[u][:], slot_no[:], rf[:, ds(it, 1)], None, ALU.is_equal).then_inc(picked, 1)
                v.tensor_scalar(place[:, u, 0], block_no[:], bf[:, ds(it, 1)], tok2[:, ds(it, 1)],
                                ALU.is_equal, ALU.mult).then_inc(picked, 1)
                v.tensor_scalar(place[:, u, 1], block_no[:], bf[:, ds(it, 1)], gate2[:, ds(it, 1)],
                                ALU.is_equal, ALU.mult).then_inc(picked, 1)
            pipelined(dve, TOPK * NT, 2, [(factors, 0)])
            dve.wait_ge(slotted, TOPK * NT)
            done(v.tensor_copy(tab["slot_token"][:], pslot[:, 0:MAXB]))
            done(v.tensor_scalar(tab["slot_gate"][:], pslot[:, MAXB:2 * MAXB], 0.5, None, ALU.mult))

        @block.tensor
        def _(pe):
            pe.wait_ge(consts, 8)
            pe.wait_ge(mask_ready, 1)
            m2d = mask[:].rearrange("p t e -> p (t e)")
            nc.tensor.matmul(prank[:, 0:NT * E], below[:], m2d, start=True, stop=False)
            for t in range(NT - 1):
                nc.tensor.matmul(prank[:, (t + 1) * E:NT * E].rearrange("p (t e) -> p t e", e=E), cst["ones"][:],
                                 mask[:, t:t + 1, :].to_broadcast([P, NT - 1 - t, E]), start=False, stop=(t == NT - 2))
            for t in range(NT):
                last = nc.tensor.matmul(pcnt[:, 0:E], cst["ones"][:], mask[:, t, :], start=(t == 0), stop=(t == NT - 1))
            last.then_inc(ranked, 1)

            def slots(it, u, first, last):
                pe.wait_ge(picked, it * 3 + 3)
                nc.tensor.matmul(pslot[:, 0:2 * MAXB], pick[u][:], place[:, u].rearrange("p a b -> p (a b)"),
                                 start=first, stop=last).then_inc(slotted, 1)
            N = TOPK * NT
            for it in range(2):
                slots(it, it, it == 0, False)
            with pe.Fori(1, N // 2 - 1) as i:
                for u in range(2):
                    slots(2 * i + u, u, False, False)
            for it in range(N - 2, N):
                slots(it, it % 2, False, it == N - 1)


def experts(nc, sem, cst, io, tab, w, hn2_dram, yslot_dram, g2row):
    ctx = ExitStack()
    with ctx:
        sb = lambda n, s, d=F32: ctx.enter_context(nc.sbuf_tensor(n, s, d))
        ps = lambda n, s: ctx.enter_context(nc.psum_tensor(n, s, F32))
        xg = sb("e_xg", [P, D])
        xh, xl = sb("e_xh", [P, D], F32R), sb("e_xl", [P, D], F32R)
        ah, al = sb("e_ah", [P, FE], F32R), sb("e_al", [P, FE], F32R)
        th, av = sb("e_th", [P, FE]), sb("e_av", [P, FE])
        ysb = sb("e_y", [P, D])
        idx = sb("e_idx", [P, 1], I32)
        gu, tp, pa, pd = ps("e_gu", [P, NB]), ps("e_tp", [P, D]), ps("e_pa", [P, NB]), ps("e_pd", [P, D])

        idx_ready, filled = sem("idx_ready"), sem("e_filled")
        gathered, turned, xh_ready, xl_ready = sem("gathered"), sem("e_turned"), sem("xh_ready"), sem("xl_ready")
        gu_mm, th_ready, tmp_ready, av_ready = sem("gu_mm"), sem("th_ready"), sem("tmp_ready"), sem("av_ready")
        av_turned, ah_ready, al_ready = sem("av_turned"), sem("ah_ready"), sem("al_ready")
        d_mm, y_ready, y_out = sem("d_mm"), sem("ey_ready"), sem("ey_out")
        KF = FE // P
        HX = D // 2
        block = ctx.enter_context(nc.Block())
        blocks_less = lambda eng: eng.value_load(tab["blocks_less"][0:1, 0:1], min_val=E - LEAD, max_val=MAXB - LEAD)

        def per_block(eng, name, b, lo, hi):
            return eng.value_load(tab[name][0:1, ds(b, 1)], min_val=lo, max_val=hi)

        @block.sync
        def _(sp):
            for q in range(2):
                sp.wait_ge(w["lo_done"], q + 3)
                load_quarter(sp, io, w, 1, q)
            used = sp.value_load(tab["ends"][0:1, E - 1:E], min_val=E, max_val=MAXB)
            unused = sp.value_load(tab["unused"][0:1, 0:1], min_val=1, max_val=MAXB + 1)
            with sp.Fori(used, MAXB + 1) as b:
                sp.dma_start(yslot_dram[ds(b * P, P), :], g2row[:]).then_inc(filled, 16)
            for q in range(2, NQ):
                sp.wait_ge(w["lo_done"], NQ + q - 1)
                load_quarter(sp, io, w, 1, q)
            with sp.Fori(2, E) as e:
                for q in range(NQ):
                    sp.wait_ge(w["lo_done"], NQ * e + (q - 1))
                    load_quarter(sp, io, w, e, q)
            sp.wait_ge(filled, unused * 16)
            sp.nop(nofuse=True)

        @block.gpsimd
        def _(pool):
            nless = blocks_less(pool)

            def gather(b, first=False):
                if not first:
                    pool.wait_ge(turned, b)
                pool.nop(nofuse=True)
                nc.gpsimd.tensor_copy(idx[:], tab["slot_token"][:, ds(b, 1)]).then_inc(idx_ready, 1)
                pool.wait_ge(idx_ready, b + 1)
                pool.nop(nofuse=True)
                pool.indirect_dma_start(xg[:], None, hn2_dram, bass.IndirectOffsetOnAxis(ap=idx[:], axis=0))\
                    .then_inc(gathered, 16)
            gather(0, True)
            for b in range(1, LEAD):
                gather(b)
            with pool.Fori(0, nless) as i:
                gather(i + LEAD)

        @block.scalar
        def _(act):
            nless = blocks_less(act)

            def tanh(b):
                act.wait_ge(gu_mm, b + 1)
                nc.scalar.activation(th[:], gu[:, 0:FE], ACT.Tanh, scale=0.5).then_inc(th_ready, 1)

            def high_x(b):
                act.wait_ge(turned, b + 1)
                for h in range(2):
                    cols = slice(h * HX, (h + 1) * HX)
                    nc.scalar.activation(xh[:, cols], tp[:, cols], ACT.Copy).then_inc(xh_ready, 1)

            def high_a(b):
                act.wait_ge(av_turned, b + 1)
                nc.scalar.activation(ah[:], pa[:, 0:FE], ACT.Copy).then_inc(ah_ready, 1)

            def high_w(b, first=False):
                for part in range(2):
                    due = per_block(act, f"split{part}", b, 0, 1)
                    with act.If(due == 1):
                        e = per_block(act, "expert1", b, 1, E - 1)
                        off = per_block(act, "woff_next", b, 0, WE)
                        if not first:
                            before = per_block(act, "before", b, 1, MAXB)
                            act.wait_ge(d_mm, before)
                        for q in (2 * part, 2 * part + 1):
                            act.wait_ge(w["in"][q], (e + 1) * (16 * QLOADS[q]))
                            act.nop(nofuse=True)
                            nc.scalar.activation(w["hi"][:, ds(off + q * QW, QW)], w["raw"][:, q % 2],
                                                 ACT.Copy).then_inc(w["hi_done"], 1)

            def store(b):
                act.wait_ge(y_ready, b + 1)
                act.dma_start(yslot_dram[ds(b * P, P), :], ysb[:]).then_inc(y_out, 16)
            high_x(0)
            tanh(0)
            high_x(1)
            high_w(0, True)
            high_a(0)
            tanh(1)
            high_x(2)
            high_w(1)
            with act.Fori(0, nless) as i:
                high_a(i + 1)
                tanh(i + 2)
                store(i)
                high_x(i + 3)
                high_w(i + 2)
            high_a(nless + 1)
            tanh(nless + 2)
            store(nless)
            high_w(nless + 2)
            store(nless + 1)
            high_a(nless + 2)
            store(nless + 2)
            act.wait_ge(y_out, (nless + LEAD) * 16)
            act.nop(nofuse=True)

        @block.vector
        def _(dve):
            nless = blocks_less(dve)

            def act_product(b):
                dve.wait_ge(th_ready, b + 1)
                nc.vector.scalar_tensor_tensor(th[:], th[:], 1.0, gu[:, 0:FE], ALU.add, ALU.mult).then_inc(tmp_ready, 1)
                dve.wait_ge(tmp_ready, b + 1)
                nc.vector.tensor_tensor(av[:], th[:], gu[:, FE:2 * FE], ALU.mult).then_inc(av_ready, 1)

            def low_x(b):
                for h in range(2):
                    cols = slice(h * HX, (h + 1) * HX)
                    dve.wait_ge(xh_ready, 2 * b + h + 1)
                    nc.vector.tensor_tensor(xl[:, cols], tp[:, cols], xh[:, cols].bitcast(F32), ALU.subtract)\
                        .then_inc(xl_ready, 1)

            def low_a(b):
                dve.wait_ge(ah_ready, b + 1)
                nc.vector.tensor_tensor(al[:], pa[:, 0:FE], ah[:].bitcast(F32), ALU.subtract).then_inc(al_ready, 1)

            def low_w(b):
                for part in range(2):
                    due = per_block(dve, f"split{part}", b, 0, 1)
                    with dve.If(due == 1):
                        e = per_block(dve, "expert1", b, 1, E - 1)
                        off = per_block(dve, "woff_next", b, 0, WE)
                        for q in (2 * part, 2 * part + 1):
                            dve.wait_ge(w["hi_done"], NQ * e + (q + 1))
                            dve.nop(nofuse=True)
                            nc.vector.tensor_tensor(w["lo"][:, ds(off + q * QW, QW)], w["raw"][:, q % 2],
                                                    w["hi"][:, ds(off + q * QW, QW)].bitcast(F32),
                                                    ALU.subtract).then_inc(w["lo_done"], 1)

            def y_scaled(b, first=False):
                dve.wait_ge(d_mm, b + 1)
                if not first:
                    dve.wait_ge(y_out, b * 16)
                nc.vector.scalar_tensor_tensor(ysb[:], pd[:], tab["slot_gate"][:, ds(b, 1)], g2row[:],
                                               ALU.mult, ALU.mult).then_inc(y_ready, 1)
            low_x(0)
            act_product(0)
            low_x(1)
            low_w(0)
            low_a(0)
            act_product(1)
            low_x(2)
            low_w(1)
            y_scaled(0, True)
            with dve.Fori(0, nless) as i:
                low_a(i + 1)
                act_product(i + 2)
                low_x(i + 3)
                low_w(i + 2)
                y_scaled(i + 1)
            low_a(nless + 1)
            act_product(nless + 2)
            low_w(nless + 2)
            y_scaled(nless + 1)
            low_a(nless + 2)
            y_scaled(nless + 2)

        @block.tensor
        def _(pe):
            nless = blocks_less(pe)

            def turn(b):
                pe.wait_ge(gathered, (b + 1) * 16)
                for k in range(KD):
                    last = nc.tensor.transpose(tp[:, k * P:(k + 1) * P], xg[:, k * P:(k + 1) * P], cst["ident"][:])
                last.then_inc(turned, 1)

            def gate_up(b, first=False):
                e = per_block(pe, "expert", b, 0, E - 1)
                off = per_block(pe, "woff", b, 0, WE)
                if not first:
                    pe.wait_ge(av_ready, b)
                for k in range(KD):
                    if k * 2 * FE % QW == 0:
                        pe.wait_ge(w["lo_done"], e * NQ + (k * 2 * FE // QW + 1))
                    if k % (KD // 2) == 0:
                        pe.wait_ge(xl_ready, 2 * b + 2 * k // KD + 1)
                    tok = slice(k * P, (k + 1) * P)
                    hi, lo = [w[n][:, ds(off + k * 2 * FE, 2 * FE)] for n in ("hi", "lo")]
                    nc.tensor.matmul(gu[:], xh[:, tok], hi, start=(k == 0), stop=False)
                    nc.tensor.matmul(gu[:], xh[:, tok], lo, start=False, stop=False)
                    last = nc.tensor.matmul(gu[:], xl[:, tok], hi, start=False, stop=(k == KD - 1))
                last.then_inc(gu_mm, 1)

            def turn_act(b):
                pe.wait_ge(av_ready, b + 1)
                for k in range(KF):
                    last = nc.tensor.transpose(pa[:, k * P:(k + 1) * P], av[:, k * P:(k + 1) * P], cst["ident"][:])
                last.then_inc(av_turned, 1)

            def down(b, first=False):
                e = per_block(pe, "expert", b, 0, E - 1)
                off = per_block(pe, "woff", b, 0, WE)
                pe.wait_ge(w["lo_done"], e * NQ + NQ)
                pe.wait_ge(al_ready, b + 1)
                if not first:
                    pe.wait_ge(y_ready, b)
                for half in range(D // NB):
                    dst = pd[:, half * NB:(half + 1) * NB]
                    for k in range(KF):
                        tok = slice(k * P, (k + 1) * P)
                        hi, lo = [w[n][:, ds(off + (DOWN + k * D + half * NB), NB)] for n in ("hi", "lo")]
                        nc.tensor.matmul(dst, ah[:, tok], hi, start=(k == 0), stop=False)
                        nc.tensor.matmul(dst, ah[:, tok], lo, start=False, stop=False)
                        last = nc.tensor.matmul(dst, al[:, tok], hi, start=False, stop=(k == KF - 1))
                last.then_inc(d_mm, 1)
            turn(0)
            gate_up(0, True)
            turn(1)
            gate_up(1)
            turn_act(0)
            turn(2)
            down(0, True)
            with pe.Fori(0, nless) as i:
                gate_up(i + 2)
                turn_act(i + 1)
                turn(i + 3)
                down(i + 1)
            gate_up(nless + 2)
            turn_act(nless + 1)
            down(nless + 1)
            turn_act(nless + 2)
            down(nless + 2)


def combine(nc, sem, cst, io, tab, x2, yslot_dram, out):
    ctx = ExitStack()
    with ctx:
        sb = lambda n, s, d=F32: ctx.enter_context(nc.sbuf_tensor(n, s, d))
        ps = lambda n, s: ctx.enter_context(nc.psum_tensor(n, s, F32))
        ya, yb, ob = sb("f_ya", [P, 2, D]), sb("f_yb", [P, 2, D]), sb("f_ob", [P, 2, D])
        fg = sb("f_g", [P, D])
        ssq, std, rstd = sb("f_ssq", [P, 2]), sb("f_std", [P, 2]), sb("f_rstd", [P, 2])
        junk = ps("f_junk", [P, D])
        idx = [sb(f"f_idx{u}", [P, TOPK], I32) for u in range(2)]
        fg_in, idx_ready = sem("f_in"), sem("f_idx_ready")
        ya_in, yb_in, stored = [[sem(f"f_{n}{u}") for u in range(2)] for n in ("ya", "yb", "st")]
        pair, summed, sqd, stdd, rec, normed = [sem("f_" + n) for n in ("pair", "summed", "sqd", "stdd", "rec", "normed")]
        block = ctx.enter_context(nc.Block())
        tile = lambda it: x2[:, ds(it, 1)].rearrange("p o n -> p (o n)")

        @block.gpsimd
        def _(pool):
            def gather(it, u):
                if at_least(it, 2):
                    pool.wait_ge(summed, it - 1)
                pool.nop(nofuse=True)
                nc.gpsimd.tensor_copy(idx[u][:].rearrange("p (c o) -> p c o", o=1), tab["pos"][:, :, ds(it, 1)])\
                    .then_inc(idx_ready, 1)
                pool.wait_ge(idx_ready, it + 1)
                pool.nop(nofuse=True)
                for c, (buf, s) in enumerate(((ya, ya_in), (yb, yb_in))):
                    pool.indirect_dma_start(buf[:, u], None, yslot_dram,
                                            bass.IndirectOffsetOnAxis(ap=idx[u][:, c:c + 1], axis=0)).then_inc(s[u], 16)
            pipelined(pool, NT, 2, [(gather, 0)])

        @block.sync
        def _(sp):
            sp.dma_start(fg[:], io["final_norm_g"].partition_broadcast(P)).then_inc(fg_in, 16)

            def store(it, u):
                sp.wait_ge(normed, it + 1)
                sp.dma_start(out[0, ds(it * P, P), :], ob[:, u]).then_inc(stored[u], 16)
            pipelined(sp, NT, 2, [(store, 0)])
            for u in range(2):
                sp.wait_ge(stored[u], NT // 2 * 16)

        @block.scalar
        def _(act):
            def squares(it, u):
                act.wait_ge(summed, it + 1)
                if at_least(it, 2):
                    act.wait_ge(rec, it - 1)
                act.nop(nofuse=True)
                nc.scalar.activation(junk[:], tile(it), ACT.Square, accum_out=ssq[:, u:u + 1]).then_inc(sqd, 1)
                act.wait_ge(sqd, it + 1)
                nc.scalar.activation(std[:, u:u + 1], ssq[:, u:u + 1], ACT.Sqrt, scale=1.0 / D,
                                     bias=cst["eps"][:]).then_inc(stdd, 1)
            pipelined(act, NT, 2, [(squares, 0)])

        @block.vector
        def _(dve):
            def add(it, u):
                dve.wait_ge(ya_in[u], it * 8 + 16 - u * 8)
                dve.wait_ge(yb_in[u], it * 8 + 16 - u * 8)
                nc.vector.tensor_tensor(ya[:, u], ya[:, u], yb[:, u], ALU.add).then_inc(pair, 1)
                dve.wait_ge(pair, it + 1)
                nc.vector.tensor_tensor(tile(it), tile(it), ya[:, u], ALU.add).then_inc(summed, 1)

            def norm(it, u):
                dve.wait_ge(stdd, it + 1)
                nc.vector.reciprocal(rstd[:, u:u + 1], std[:, u:u + 1]).then_inc(rec, 1)
                dve.wait_ge(rec, it + 1)
                if at_least(it, 2):
                    dve.wait_ge(stored[u], it * 8 - u * 8)
                nc.vector.scalar_tensor_tensor(ob[:, u], tile(it), rstd[:, u:u + 1], fg[:], ALU.mult, ALU.mult)\
                    .then_inc(normed, 1)
            dve.wait_ge(fg_in, 16)
            pipelined(dve, NT, 4, [(add, 0), (norm, 1)])


def build(nc, io, out):
    ctx = ExitStack()
    with ctx:
        sb = lambda n, s, d=F32: ctx.enter_context(nc.sbuf_tensor(n, s, d))
        sem = lambda n: ctx.enter_context(nc.semaphore(n))
        cst = {"ident": sb("ident", [P, P]), "ones": sb("ones", [P, P]), "eps": sb("eps", [P, 1])}
        cond = sb("cond", [P, KD])
        y_dram = nc.dram_tensor("y_scratch", (NT, P, KD, P), F32, kind="Internal").ap()
        mod_dram = nc.dram_tensor("mod_scratch", (P, 4 * D), F32, kind="Internal").ap()
        hn2_dram = nc.dram_tensor("hn2_scratch", (S, D), F32, kind="Internal").ap()
        made, cleared = sem("const_made"), sem("ident_cleared")
        with nc.Block() as block:
            @block.gpsimd
            def _(pool):
                nc.gpsimd.memset(cst["ident"][:], 0.0).then_inc(cleared, 1)
                nc.gpsimd.memset(cst["ones"][:], 1.0).then_inc(made, 1)
                nc.gpsimd.memset(cst["eps"][:], EPS).then_inc(made, 1)
                pool.wait_ge(cleared, 1)
                nc.gpsimd.affine_select(out=cst["ident"][:], in_=cst["ident"][:], compare_op=ALU.not_equal, fill=1.0,
                                        base=0, pattern=[[-1, P]], channel_multiplier=1).then_inc(made, 1)
                pool.wait_ge(made, 3)
        with nc.sbuf_tensor("hT_hi", [P, KD, S], F32R) as hT_hi, nc.sbuf_tensor("hT_lo", [P, KD, S], F32R) as hT_lo:
            norm_and_transpose(nc, sem, cst, io, hT_hi, hT_lo, cond)
            lru(nc, sem, cst, io, hT_hi, hT_lo, cond, y_dram, mod_dram)
        x2 = sb("x2", [P, NT, D])
        g2row = sb("g2row", [P, D])
        logits = sb("logits", [P, NT, E])
        out_and_norm(nc, sem, cst, io, x2, y_dram, mod_dram, hn2_dram, g2row, logits)
        tab = {"blocks_less": sb("t_blocks_less", [P, 1], I32), "unused": sb("t_unused", [P, 1], I32), "ends": sb("t_ends", [P, E], I32), "pos": sb("t_pos", [P, TOPK, NT], I32),
               "expert": sb("t_expert", [P, MAXB], I32), "expert1": sb("t_expert1", [P, MAXB], I32), "woff": sb("t_woff", [P, MAXB], I32),
               "woff_next": sb("t_woff_next", [P, MAXB], I32),
               "before": sb("t_before", [P, MAXB], I32), "split0": sb("t_split0", [P, MAXB], I32), "split1": sb("t_split1", [P, MAXB], I32),
               "slot_token": sb("t_slot_token", [P, MAXB], I32), "slot_gate": sb("t_slot_gate", [P, MAXB])}
        yslot_dram = nc.dram_tensor("yslot_scratch", ((MAXB + 1) * P, D), F32, kind="Internal").ap()
        with nc.sbuf_tensor("w_hi", [P, 2 * WE], F32R) as w_hi, nc.sbuf_tensor("w_lo", [P, 2 * WE], F32R) as w_lo, \
                nc.sbuf_tensor("w_raw", [P, 2, QW], F32) as w_raw:
            w = {"hi": w_hi, "lo": w_lo, "raw": w_raw, "in": [sem(f"raw_in{q}") for q in range(NQ)],
                 "hi_done": sem("w_hi_done"), "lo_done": sem("w_lo_done")}
            dispatch(nc, sem, cst, io, logits, tab, w)
            experts(nc, sem, cst, io, tab, w, hn2_dram, yslot_dram, g2row)
        combine(nc, sem, cst, io, tab, x2, yslot_dram, out)


_INS = ["x", "c", "ada_w", "ada_b", "norm1_g", "norm2_g", "lru_w_in", "lru_conv_w", "lru_conv_b", "lru_wa", "lru_ba",
        "lru_wx", "lru_bx", "lru_lambda", "lru_w_out", "router_w", "router_b", "moe_w_gate", "moe_w_up", "moe_w_down",
        "final_norm_g"]


def kernel(**inputs):
    import numpy as _np
    import concourse.bacc as _bacc
    from concourse import mybir as _mybir
    from concourse.bass_utils import run_bass_kernel_spmd as _run

    nc = _bacc.Bacc("TRN2", target_bir_lowering=False, num_devices=1)
    arrays, io = {}, {}
    for name in _INS:
        a = _np.ascontiguousarray(inputs[name])
        arrays[f"in_{name}_dram"] = a
        io[name] = nc.dram_tensor(f"in_{name}_dram", a.shape, _mybir.dt.from_np(a.dtype), kind="ExternalInput").ap()
    out = nc.dram_tensor("out_0_dram", (1, S, D), _mybir.dt.float32, kind="ExternalOutput").ap()
    build(nc, io, out)
    r = _run(nc, [arrays], core_ids=[0])
    return r.results[0]["out_0_dram"]
```

```python
import concourse.bass as bass
from concourse import mybir
from contextlib import ExitStack

F32 = mybir.dt.float32
F32R = mybir.dt.float32r
I32 = mybir.dt.int32
ALU = mybir.AluOpType
ACT = mybir.ActivationFunctionType
AX = mybir.AxisListType
ds = bass.ds

P = 128
D = 1024
S = 2048
KD = D // P
NT = S // P
NB = 512
EPS = 1e-6
LRU_C = 8.0
CONV = 4
HALF = S // 2
E = 16
G = 4
PER = E // G
FE = 256
TOPK = 2
MAXB = S * TOPK // P + E
LEAD = 3
WE = KD * 2 * FE + FE // P * D


def at_least(it, k):
    return not isinstance(it, int) or it >= k


def pipelined(eng, n, ramp, stages, bufs=2):
    assert (n - ramp) % bufs == 0 and ramp % bufs == 0
    def step(s):
        for stage, lag in stages:
            if 0 <= s - lag < n:
                stage(s - lag, (s - lag) % bufs)
    for s in range(ramp):
        step(s)
    with eng.Fori(0, (n - ramp) // bufs) as i:
        for u in range(bufs):
            for stage, lag in stages:
                stage(bufs * i + (ramp + u - lag), (u - lag) % bufs)
    for s in range(n, n + max(lag for _, lag in stages)):
        step(s)


def norm_and_transpose(nc, sem, cst, io, hT_hi, hT_lo, cond, pre):
    ctx = ExitStack()
    with ctx:
        sb = lambda n, s, d=F32: ctx.enter_context(nc.sbuf_tensor(n, s, d))
        ps = lambda n, s: ctx.enter_context(nc.psum_tensor(n, s, F32))
        KQ, AB, XB = 2, 4, 4
        ada = sb("n_ada", [P, AB, KQ, NB])
        acc = sb("n_acc", [P, 2, NB])
        brow = sb("n_brow", [P, 2, D])
        gain = sb("n_gain", [P, D])
        ct = sb("n_c", [P, KD])
        cth = sb("n_cth", [P, KD])
        xt = sb("n_x", [P, XB, D])
        hn = sb("n_hn", [P, XB, D])
        ssq, std, rstd = sb("n_ssq", [P, XB]), sb("n_std", [P, XB]), sb("n_rstd", [P, XB])
        pm = [ps("n_pm0", [P, NB]), ps("n_pm1", [P, NB])]
        pt = [ps("n_pt0", [P, D]), ps("n_pt1", [P, D])]
        junk = ps("n_junk", [P, D])

        c_in, rows_in = sem("c_in"), sem("rows_in")
        ada_in = [sem(f"ada_in{u}") for u in range(AB)]
        x_in = [sem(f"x_in{u}") for u in range(XB)]
        vec_in = pre["vec_in"]
        cth_ready, cond_ready = sem("cth_ready"), sem("cond_ready")
        acc_step, summed, row_ready = sem("acc_step"), sem("summed"), sem("row_ready")
        ssq_ready, std_ready, rstd_ready = sem("ssq_ready"), sem("std_ready"), sem("rstd_ready")
        scaled, shifted, turned = sem("scaled"), sem("shifted"), sem("turned")
        hi_ready, lo_ready = sem("hi_ready"), sem("lo_ready")

        ada_v = io["ada_w"][0].rearrange("(p k) n -> p k n", k=KD)
        NCH = 2 * D // NB
        block = ctx.enter_context(nc.Block())

        @block.sync
        def _(sp):
            sp.dma_start(ct[:], io["c"][0].rearrange("(p k) -> p k", k=KD)).then_inc(c_in, 16)
            for i in range(NCH * KD // KQ):
                n, k = i * KQ // KD, i * KQ % KD
                if i >= AB:
                    sp.wait_ge(acc_step, KQ * (i - AB + 1))
                sp.dma_start(ada[:, i % AB], ada_v[:, k:k + KQ, n * NB:(n + 1) * NB]).then_inc(ada_in[i % AB], 16)
                if i == AB - 1:
                    sp.dma_start(xt[:, 0], io["x"][0, 0:P, :]).then_inc(x_in[0], 16)
                    sp.dma_start(brow[:], io["ada_b"][0, 0:2 * D].partition_broadcast(P)
                                 .rearrange("p (a n) -> p a n", a=2)).then_inc(rows_in, 16)
                    sp.dma_start(gain[:], io["norm1_g"][0].partition_broadcast(P)).then_inc(rows_in, 16)

            def load(it, u):
                if not at_least(it, 1):
                    return
                if at_least(it, XB):
                    sp.wait_ge(scaled, it - (XB - 1))
                sp.dma_start(xt[:, u], io["x"][0, ds(it * P, P), :]).then_inc(x_in[u], 16)
            pipelined(sp, NT, XB, [(load, 0)], XB)
            col = lambda a: a.rearrange("(j p) -> p j", p=P)
            with nc.allow_non_contiguous_dma(reason="small vectors by channel"):
                for dst, src in ((pre["lam"][:], "lru_lambda"), (pre["cb"][:], "lru_conv_b"),
                                 (pre["gb"][:, 0], "lru_ba"), (pre["gb"][:, 1], "lru_bx")):
                    sp.dma_start(dst, col(io[src][0]), allow_slow_non_contiguous=True).then_inc(vec_in, 16)
                for w in range(CONV):
                    sp.dma_start(pre["cw"][:, :, w], col(io["lru_conv_w"][0, w]), allow_slow_non_contiguous=True)\
                        .then_inc(vec_in, 16)
            w_v = io["lru_w_in"][0].rearrange("(k p) n -> p k n", p=P)
            sp.dma_start(pre["raw_x"][:], w_v[:, :, D:D + P]).then_inc(pre["raw_x_in"], 16)

        @block.scalar
        def _(act):
            act.wait_ge(c_in, 16)
            nc.scalar.activation(cth[:], ct[:], ACT.Tanh, scale=0.5).then_inc(cth_ready, 1)

            def squares(it, u):
                act.wait_ge(x_in[u], it * 4 + 16 - u * 4)
                if at_least(it, XB):
                    act.wait_ge(rstd_ready, it - (XB - 1))
                nc.scalar.activation(junk[:], xt[:, u], ACT.Square, accum_out=ssq[:, u:u + 1]).then_inc(ssq_ready, 1)
                act.wait_ge(ssq_ready, it + 1)
                nc.scalar.activation(std[:, u:u + 1], ssq[:, u:u + 1], ACT.Sqrt, scale=1.0 / D,
                                     bias=cst["eps"][:]).then_inc(std_ready, 1)

            def high(it, u):
                act.wait_ge(turned, it + 1)
                act.nop(nofuse=True)
                nc.scalar.activation(hT_hi[:, :, ds(it * P, P)], pt[u % 2][:].rearrange("p (k n) -> p k n", k=KD),
                                     ACT.Copy).then_inc(hi_ready, 1)
            pipelined(act, NT, XB, [(squares, 0), (high, 3)], XB)

        @block.vector
        def _(dve):
            dve.wait_ge(cth_ready, 1)
            nc.vector.scalar_tensor_tensor(cond[:], cth[:], 1.0, ct[:], ALU.add, ALU.mult).then_inc(cond_ready, 1)
            dve.wait_ge(cond_ready, 1)
            nc.vector.tensor_scalar(cond[:], cond[:], 0.5, None, ALU.mult).then_inc(cond_ready, 1)
            dve.wait_ge(cond_ready, 2)
            def finish_row(n):
                row, cols = n * NB // D, ds(n * NB % D, NB)
                dve.wait_ge(summed, n + 1)
                if row == 0:
                    nc.vector.tensor_tensor(brow[:, 0, cols], pm[n % 2][:], brow[:, 0, cols], ALU.add).then_inc(row_ready, 1)
                else:
                    nc.vector.tensor_tensor(brow[:, 1, cols], pm[n % 2][:], brow[:, 1, cols], ALU.add).then_inc(cond_ready, 1)
                    dve.wait_ge(cond_ready, 1 + n)
                    nc.vector.scalar_tensor_tensor(brow[:, 1, cols], brow[:, 1, cols], 1.0, gain[:, cols],
                                                   ALU.add, ALU.mult).then_inc(row_ready, 1)
            for n in range(NCH):
                a = acc[:, n % 2, :]
                i = n * KD // KQ
                dve.wait_ge(ada_in[i % AB], 16 * (i // AB + 1))
                if n >= 2:
                    dve.wait_ge(summed, n - 1)
                nc.vector.tensor_scalar(a, ada[:, i % AB, 0, :], cond[:, 0:1], None, ALU.mult).then_inc(acc_step, 1)
                for k in range(1, KD):
                    dve.wait_ge(acc_step, KD * n + k)
                    i = (n * KD + k) // KQ
                    if k % KQ == 0:
                        dve.wait_ge(ada_in[i % AB], 16 * (i // AB + 1))
                    nc.vector.scalar_tensor_tensor(a, ada[:, i % AB, k % KQ, :], cond[:, k:k + 1], a,
                                                   ALU.mult, ALU.add).then_inc(acc_step, 1)
                if n == 0:
                    dve.wait_ge(rows_in, 32)
                else:
                    finish_row(n - 1)
            finish_row(NCH - 1)
            dve.wait_ge(row_ready, NCH)

            def scale(it, u):
                dve.wait_ge(std_ready, it + 1)
                if at_least(it, XB):
                    dve.wait_ge(turned, it - (XB - 1))
                nc.vector.reciprocal(rstd[:, u:u + 1], std[:, u:u + 1]).then_inc(rstd_ready, 1)
                dve.wait_ge(rstd_ready, it + 1)
                nc.vector.scalar_tensor_tensor(hn[:, u], xt[:, u], rstd[:, u:u + 1], brow[:, 1], ALU.mult,
                                               ALU.mult).then_inc(scaled, 1)

            def low(it, u):
                dve.wait_ge(hi_ready, it + 1)
                nc.vector.tensor_tensor(hT_lo[:, :, ds(it * P, P)], pt[u % 2][:].rearrange("p (k n) -> p k n", k=KD),
                                        hT_hi[:, :, ds(it * P, P)].bitcast(F32), ALU.subtract).then_inc(lo_ready, 1)
            pipelined(dve, NT, XB, [(scale, 0), (low, 3)], XB)

        @block.gpsimd
        def _(pool):
            pool.wait_ge(row_ready, NCH)

            def shift(it, u):
                pool.wait_ge(scaled, it + 1)
                nc.gpsimd.tensor_tensor(hn[:, u], hn[:, u], brow[:, 0], ALU.add).then_inc(shifted, 1)
            pipelined(pool, NT, XB, [(shift, 0)], XB)

        @block.tensor
        def _(pe):
            for n in range(NCH):
                pe.wait_ge(acc_step, KD * (n + 1))
                if n >= 2:
                    pe.wait_ge(row_ready, n - 1)
                nc.tensor.matmul(pm[n % 2][:], cst["ones"][:], acc[:, n % 2, :], start=True, stop=True).then_inc(summed, 1)

            def turn(it, u):
                pe.wait_ge(shifted, it + 1)
                if at_least(it, 2):
                    pe.wait_ge(lo_ready, it - 1)
                for k in range(KD):
                    last = nc.tensor.transpose(pt[u % 2][:, k * P:(k + 1) * P], hn[:, u, k * P:(k + 1) * P], cst["ident"][:])
                last.then_inc(turned, 1)
            pipelined(pe, NT, XB, [(turn, 0)], XB)


def lru(nc, sem, cst, io, hT_hi, hT_lo, cond, pre, y_dram, mod_dram):
    ctx = ExitStack()
    with ctx:
        sb = lambda n, s, d=F32: ctx.enter_context(nc.sbuf_tensor(n, s, d))
        ps = lambda n, s: ctx.enter_context(nc.psum_tensor(n, s, F32))
        raw = {"x": pre["raw_x"], "g": sb("raw_g", [P, KD, P])}
        whi = {"x": sb("wx_hi", [P, KD, P], F32R), "g": sb("wg_hi", [P, KD, P], F32R)}
        wlo = {"x": sb("wx_lo", [P, KD, P], F32R), "g": sb("wg_lo", [P, KD, P], F32R)}
        gw = sb("gate_w", [P, 2, P])
        gwh, gwl = sb("gate_w_hi", [P, 2, P], F32R), sb("gate_w_lo", [P, 2, P], F32R)
        cw, cb, gb, dec = [pre[n] for n in ("cw", "cb", "gb", "dec")]
        sp_t = sb("sp_t", [P, 6, KD])
        xu = sb("xu", [P, 2, CONV - 1 + NB])
        zero = sb("zero3", [P, CONV - 1])
        XB, TR, TI, A, T, M, GE = [sb(n, [P, HALF]) for n in ("XB", "TR", "TI", "A", "T", "M", "GE")]
        XBh, XBl = sb("XBh", [P, NB], F32R), sb("XBl", [P, NB], F32R)
        carry = sb("carry", [P, 1])
        stg = sb("stg", [P, 2, KD // 4, NB])
        mtmp = sb("mtmp", [P, NB])
        macc = sb("macc", [P, NB])
        px = [ps("px0", [P, NB]), ps("px1", [P, NB])]
        pg = [ps("pg0", [P, NB]), ps("pg1", [P, NB])]
        pr, pi = ps("pr", [P, NB]), ps("pi", [P, NB])
        pmod = ps("pmod", [P, NB])
        mrow = sb("mod_row", [1, NB])

        raw_in = {"x": pre["raw_x_in"], "g": sem("raw_g_in")}
        hi_done = {"x": sem("wx_hi_done"), "g": sem("wg_hi_done")}
        lo_done = {"x": sem("wx_lo_done"), "g": sem("wg_lo_done")}
        gw_in = sem("gw_in")
        vec_in, s_a, s_b = pre["vec_in"], sem("sp_a"), sem("sp_b")
        gw_hi_done, gw_lo_done, xbh_done, xbl_done = [sem(n) for n in ("gw_hi_done", "gw_lo_done", "xbh_done", "xbl_done")]
        x_mm, g_mm, gate_mm = sem("x_mm"), sem("g_mm"), sem("gate_mm")
        xu_ready, halo_ready, tap0, tap1, tap2, conv = [sem(n) for n in
                                                       ("xu_ready", "halo_ready", "tap0", "tap1", "tap2", "conv")]
        tr_ready, ti_ready, a_ready, sq_ready, m_ready = [sem(n) for n in
                                                          ("tr_ready", "ti_ready", "a_ready", "sq_ready", "m_ready")]
        root_ready, ix_ready, b_ready, scan_ready, carried, gelu, y_ready, y_out = [sem(n) for n in
                          ("root_ready", "ix_ready", "b_ready", "scan_ready", "carried", "gelu", "y_ready", "y_out")]
        stg_in = [sem("stg_in0"), sem("stg_in1")]
        mt, ma, mo = sem("mod_tmp"), sem("mod_acc"), sem("mod_out")
        msum, bias_in, mrow_ready = sem("mod_sum"), sem("mod_bias_in"), sem("mod_row_ready")
        zeroed = sem("zeroed")

        w_v = io["lru_w_in"][0].rearrange("(k p) n -> p k n", p=P)
        OFF = {"g": 0, "x": D}
        y_v = y_dram.rearrange("t p j n -> p j t n")
        NH = HALF // NB
        TH = HALF // P
        block = ctx.enter_context(nc.Block())

        def channels(eng, body):
            body(0, False)
            with eng.Fori(1, KD - 1) as j:
                body(j, False)
            body(KD - 1, True)

        @block.sync
        def _(sp):
            def load_gate(j):
                sp.nop(nofuse=True)
                sp.dma_start(raw["g"][:], w_v[:, :, ds(j * P, P)]).then_inc(raw_in["g"], 16)

            def load_gw(j):
                sp.nop(nofuse=True)
                sp.dma_start(gw[:, 0], io["lru_wa"][0, ds(j, 1)].rearrange("o i q -> (o i) q")).then_inc(gw_in, 16)
                sp.dma_start(gw[:, 1], io["lru_wx"][0, ds(j, 1)].rearrange("o i q -> (o i) q")).then_inc(gw_in, 16)

            def store_y(j, h):
                sp.wait_ge(y_ready, 2 * j + h + 1)
                sp.nop(nofuse=True)
                sp.dma_start(y_v[:, ds(j, 1), h * TH:(h + 1) * TH, :].rearrange("p o t n -> p (o t) n"),
                             M[:].rearrange("p (t n) -> p t n", n=P)).then_inc(y_out, 16)

            def body(j, last):
                if not last:
                    sp.wait_ge(lo_done["x"], j + 1)
                    sp.dma_start(raw["x"][:], w_v[:, :, ds(j * P + (D + P), P)]).then_inc(raw_in["x"], 16)
                    sp.wait_ge(lo_done["g"], j + 1)
                    load_gate(j + 1)
                    sp.wait_ge(gw_lo_done, j + 1)
                    load_gw(j + 1)
                if at_least(j, 1):
                    store_y(j - 1, 1)
                    store_mod(j - 1)
                    load_bias(j)
                store_y(j, 0)
            assert KD == 4 * D // NB

            def load_bias(m):
                sp.nop(nofuse=True)
                sp.dma_start(mrow[:], io["ada_b"][0:1, ds(m * NB + 2 * D, NB)]).then_inc(bias_in, 16)

            def store_mod(m):
                sp.wait_ge(mrow_ready, m + 1)
                sp.nop(nofuse=True)
                sp.dma_start(mod_dram[0:1, ds(m * NB, NB)], mrow[:]).then_inc(mo, 16)
                sp.wait_ge(mo, m * 16 + 16)
            load_gate(0)
            load_gw(0)
            load_bias(0)
            channels(sp, body)
            store_y(KD - 1, 1)
            store_mod(KD - 1)
            sp.wait_ge(y_out, 16 * 2 * KD)

        @block.scalar
        def _(act):
            act.wait_ge(raw_in["x"], 16)
            nc.scalar.activation(whi["x"][:], raw["x"][:], ACT.Copy).then_inc(hi_done["x"], 1)
            act.wait_ge(vec_in, 16 * (4 + CONV))
            nc.scalar.activation(sp_t[:, 0], pre["lam"][:], ACT.Abs).then_inc(s_a, 1)
            act.wait_ge(s_a, 1)
            nc.scalar.activation(sp_t[:, 1], sp_t[:, 0], ACT.Exp, scale=-1.0).then_inc(s_a, 1)
            act.wait_ge(s_b, 1)
            nc.scalar.activation(sp_t[:, 3], sp_t[:, 2], ACT.Ln).then_inc(s_a, 1)
            act.wait_ge(zeroed, 1)
            nc.scalar.activation(xu[:, 0, 0:CONV - 1], zero[:], ACT.Copy).then_inc(halo_ready, 1)

            def body(j, last):
                for h in range(2):
                    hh = 2 * j + h
                    for n in range(NH):
                        c = hh * NH + n
                        act.wait_ge(x_mm, c + 1)
                        if at_least(j, 1) or c >= 2:
                            act.wait_ge(conv, c - 1)
                        nc.scalar.activation(xu[:, n, CONV - 1:], px[n][:], ACT.Copy).then_inc(xu_ready, 1)
                        act.wait_ge(xu_ready, c + 1)
                        act.wait_ge(halo_ready, c + 1)
                        if n == 0 and (at_least(j, 1) or h):
                            act.wait_ge(ix_ready, hh)
                        act.nop(nofuse=True)
                        nc.scalar.activation(XB[:, n * NB:(n + 1) * NB], xu[:, n, 0:NB], ACT.Identity,
                                             scale=cw[:, ds(j, 1), 0], bias=cb[:, ds(j, 1)]).then_inc(tap0, 1)
                        if at_least(j, 1) or c >= 1:
                            act.wait_ge(conv, c)
                        tail = zero[:] if h == 1 and n == NH - 1 else xu[:, n, NB:]
                        if not (last and h == 1 and n == NH - 1):
                            nc.scalar.activation(xu[:, 1 - n, 0:CONV - 1], tail, ACT.Copy).then_inc(halo_ready, 1)
                        if h == 0 and n == 0:
                            act.wait_ge(raw_in["g"], 16 * (j + 1))
                            if at_least(j, 1):
                                act.wait_ge(g_mm, 4 * j)
                            nc.scalar.activation(whi["g"][:], raw["g"][:], ACT.Copy).then_inc(hi_done["g"], 1)
                            act.wait_ge(gw_in, 32 * (j + 1))
                            if at_least(j, 1):
                                act.wait_ge(gate_mm, 4 * j)
                            nc.scalar.activation(gwh[:], gw[:], ACT.Copy).then_inc(gw_hi_done, 1)
                        if h == 1 and n == NH - 1 and not last:
                            act.wait_ge(raw_in["x"], 16 * (j + 2))
                            nc.scalar.activation(whi["x"][:], raw["x"][:], ACT.Copy).then_inc(hi_done["x"], 1)
                        act.wait_ge(conv, c + 1)
                        if at_least(j, 1) or c >= 1:
                            act.wait_ge(gate_mm, c)
                        nc.scalar.activation(XBh[:], XB[:, n * NB:(n + 1) * NB], ACT.Copy).then_inc(xbh_done, 1)
                    if h == 0 and not at_least(j, 1):
                        act.wait_ge(s_b, 13)
                    for n in range(NH):
                        c = hh * NH + n
                        act.wait_ge(gate_mm, c + 1)
                        if n == 0 and (at_least(j, 1) or h):
                            act.wait_ge(b_ready, hh)
                        act.nop(nofuse=True)
                        nc.scalar.activation(TR[:, n * NB:(n + 1) * NB], pr[:], ACT.Tanh, scale=0.5,
                                             bias=gb[:, 0, ds(j, 1)]).then_inc(tr_ready, 1)
                        act.nop(nofuse=True)
                        nc.scalar.activation(TI[:, n * NB:(n + 1) * NB], pi[:], ACT.Tanh, scale=0.5,
                                             bias=gb[:, 1, ds(j, 1)]).then_inc(ti_ready, 1)
                    act.wait_ge(tr_ready, (hh + 1) * NH)
                    if at_least(j, 1) or h:
                        act.wait_ge(scan_ready, hh)
                        act.wait_ge(y_out, 16 * hh)
                    act.nop(nofuse=True)
                    nc.scalar.activation(T[:], TR[:], ACT.Tanh, scale=dec[:, 0, ds(j, 1)], bias=dec[:, 0, ds(j, 1)])
                    act.nop(nofuse=True)
                    nc.scalar.activation(A[:], TR[:], ACT.Exp, scale=dec[:, 1, ds(j, 1)], bias=dec[:, 1, ds(j, 1)])\
                        .then_inc(a_ready, 1)
                    act.wait_ge(a_ready, hh + 1)
                    nc.scalar.activation(M[:], A[:], ACT.Square).then_inc(sq_ready, 1)
                    act.wait_ge(m_ready, hh + 1)
                    nc.scalar.activation(M[:], T[:], ACT.Sqrt, scale=0.25).then_inc(root_ready, 1)
                    for n in range(NH):
                        act.wait_ge(g_mm, hh * NH + n + 1)
                        if n == 0 and (at_least(j, 1) or h):
                            act.wait_ge(y_ready, hh)
                        nc.scalar.activation(GE[:, n * NB:(n + 1) * NB], pg[n][:], ACT.Gelu_apprx_tanh).then_inc(gelu, 1)
            channels(act, body)

        @block.vector
        def _(dve):
            nc.vector.memset(zero[:], 0.0).then_inc(zeroed, 1)
            dve.wait_ge(hi_done["x"], 1)
            nc.vector.tensor_tensor(wlo["x"][:], raw["x"][:], whi["x"][:].bitcast(F32), ALU.subtract).then_inc(lo_done["x"], 1)
            dve.wait_ge(s_a, 2)
            nc.vector.tensor_scalar(sp_t[:, 2], sp_t[:, 1], 1.0, None, ALU.add).then_inc(s_b, 1)
            dve.wait_ge(s_b, 1)
            nc.vector.tensor_scalar(sp_t[:, 4], sp_t[:, 2], -1.0, None, ALU.add).then_inc(s_b, 1)
            dve.wait_ge(s_b, 2)
            nc.vector.tensor_scalar(sp_t[:, 5], sp_t[:, 4], 0.0, None, ALU.is_equal).then_inc(s_b, 1)
            dve.wait_ge(s_b, 3)
            dve.wait_ge(s_a, 3)
            nc.vector.tensor_tensor(sp_t[:, 3], sp_t[:, 3], sp_t[:, 5], ALU.add).then_inc(s_b, 1)
            nc.vector.tensor_tensor(sp_t[:, 4], sp_t[:, 4], sp_t[:, 5], ALU.add).then_inc(s_b, 1)
            dve.wait_ge(s_b, 5)
            nc.vector.tensor_tensor(sp_t[:, 3], sp_t[:, 3], sp_t[:, 1], ALU.mult).then_inc(s_b, 1)
            nc.vector.reciprocal(sp_t[:, 5], sp_t[:, 4]).then_inc(s_b, 1)
            dve.wait_ge(s_b, 7)
            nc.vector.tensor_tensor(sp_t[:, 3], sp_t[:, 3], sp_t[:, 5], ALU.mult).then_inc(s_b, 1)
            nc.vector.tensor_scalar(sp_t[:, 0], pre["lam"][:], -1.0, 0.0, ALU.mult, ALU.max).then_inc(s_b, 1)
            dve.wait_ge(s_b, 9)
            nc.vector.tensor_tensor(sp_t[:, 3], sp_t[:, 3], sp_t[:, 0], ALU.add).then_inc(s_b, 1)
            dve.wait_ge(s_b, 10)
            nc.vector.tensor_scalar(pre["dec"][:, 0], sp_t[:, 3], LRU_C / 2, None, ALU.mult).then_inc(s_b, 1)
            nc.vector.tensor_scalar(pre["dec"][:, 1], sp_t[:, 3], -LRU_C / 2, None, ALU.mult).then_inc(s_b, 1)
            nc.vector.tensor_scalar(pre["gb"][:], pre["gb"][:], 0.5, None, ALU.mult).then_inc(s_b, 1)

            def finish(hh):
                dve.wait_ge(carried, hh)
                dve.wait_ge(gelu, hh * NH)
                nc.vector.tensor_tensor(M[:], M[:], GE[:], ALU.mult).then_inc(y_ready, 1)

            def mod_row(m):
                dve.wait_ge(msum, m + 1)
                dve.wait_ge(bias_in, m * 16 + 16)
                nc.vector.tensor_tensor(mrow[:], pmod[0:1, :], mrow[:], ALU.add).then_inc(mrow_ready, 1)

            def body(j, last):
                for h in range(2):
                    hh = 2 * j + h
                    for n in range(NH):
                        c = hh * NH + n
                        xb = XB[:, n * NB:(n + 1) * NB]
                        dve.wait_ge(tap0, c + 1)
                        for w, before, done in ((1, None, tap1), (2, tap1, tap2), (3, tap2, conv)):
                            if before is not None:
                                dve.wait_ge(before, c + 1)
                            nc.vector.scalar_tensor_tensor(xb, xu[:, n, w:w + NB], cw[:, ds(j, 1), w], xb,
                                                           ALU.mult, ALU.add).then_inc(done, 1)
                        if h == 0 and n == 0:
                            dve.wait_ge(hi_done["g"], j + 1)
                            nc.vector.tensor_tensor(wlo["g"][:], raw["g"][:], whi["g"][:].bitcast(F32), ALU.subtract)\
                                .then_inc(lo_done["g"], 1)
                            dve.wait_ge(gw_hi_done, j + 1)
                            nc.vector.tensor_tensor(gwl[:], gw[:], gwh[:].bitcast(F32), ALU.subtract).then_inc(gw_lo_done, 1)
                        if h == 1 and n == NH - 1 and not last:
                            dve.wait_ge(hi_done["x"], j + 2)
                            nc.vector.tensor_tensor(wlo["x"][:], raw["x"][:], whi["x"][:].bitcast(F32), ALU.subtract)\
                                .then_inc(lo_done["x"], 1)
                        dve.wait_ge(xbh_done, c + 1)
                        if at_least(j, 1) or c >= 1:
                            dve.wait_ge(gate_mm, c)
                        nc.vector.tensor_tensor(XBl[:], xb, XBh[:].bitcast(F32), ALU.subtract).then_inc(xbl_done, 1)
                        if n == 0 and (at_least(j, 1) or h):
                            finish(hh)
                        if n == 0 and h == 0 and at_least(j, 1):
                            mod_row(j - 1)
                    dve.wait_ge(ti_ready, (hh + 1) * NH)
                    dve.wait_ge(conv, (hh + 1) * NH)
                    nc.vector.scalar_tensor_tensor(TI[:], TI[:], 1.0, XB[:], ALU.add, ALU.mult).then_inc(ix_ready, 1)
                    dve.wait_ge(sq_ready, hh + 1)
                    nc.vector.scalar_tensor_tensor(T[:], M[:], 1.0, T[:], ALU.add, ALU.mult).then_inc(m_ready, 1)
                    dve.wait_ge(root_ready, hh + 1)
                    dve.wait_ge(ix_ready, hh + 1)
                    nc.vector.tensor_tensor(TI[:], TI[:], M[:], ALU.mult).then_inc(b_ready, 1)
                    dve.wait_ge(b_ready, hh + 1)
                    if at_least(j, 1) or h:
                        dve.wait_ge(carried, hh)
                    nc.vector.tensor_tensor_scan(M[:], A[:], TI[:], 0.0 if h == 0 else carry[:], ALU.mult, ALU.add)\
                        .then_inc(scan_ready, 1)
                    dve.wait_ge(scan_ready, hh + 1)
                    nc.vector.tensor_copy(carry[:], M[:, HALF - 1:HALF]).then_inc(carried, 1)
            channels(dve, body)
            finish(2 * KD)
            mod_row(KD - 1)

        @block.gpsimd
        def _(pool):
            ada_v = io["ada_w"][0].rearrange("(p k) n -> p k n", k=KD)
            KH = KD // 4
            NM = 4 * D // NB
            def load(m, q):
                pool.dma_start(stg[:, q % 2], ada_v[:, q * KH:(q + 1) * KH, ds(m * NB + 2 * D, NB)])\
                    .then_inc(stg_in[q % 2], 16)
            load(0, 0)
            load(0, 1)
            def body(m, last):
                for k in range(KD):
                    q = k // KH
                    if k % KH == 0:
                        pool.wait_ge(stg_in[q % 2], m * 32 + 16 * (q // 2 + 1))
                    if k == 0:
                        if at_least(m, 1):
                            pool.wait_ge(msum, m)
                        pool.nop(nofuse=True)
                        nc.gpsimd.tensor_scalar(macc[:], stg[:, q % 2, k % KH], cond[:, k:k + 1], 0.0, ALU.mult, ALU.add).then_inc(ma, 1)
                        continue
                    pool.wait_ge(ma, m * KD + k)
                    pool.nop(nofuse=True)
                    nc.gpsimd.tensor_scalar(mtmp[:], stg[:, q % 2, k % KH], cond[:, k:k + 1], 0.0, ALU.mult, ALU.add).then_inc(mt, 1)
                    pool.wait_ge(mt, m * (KD - 1) + k)
                    nc.gpsimd.tensor_tensor(macc[:], macc[:], mtmp[:], ALU.add).then_inc(ma, 1)
                    if k % KH == KH - 1:
                        pool.wait_ge(ma, m * KD + k + 1)
                        if q < 2:
                            load(m, q + 2)
                        elif not last:
                            load(m + 1, q - 2)
            body(0, False)
            with pool.Fori(1, NM - 1) as m:
                body(m, False)
            body(NM - 1, True)

        @block.tensor
        def _(pe):
            def project(br, dst, tok, ks=range(KD)):
                for k in ks:
                    cols = slice(tok, tok + NB)
                    nc.tensor.matmul(dst[:], whi[br][:, k], hT_hi[:, k, cols], start=(k == 0), stop=False)
                    nc.tensor.matmul(dst[:], whi[br][:, k], hT_lo[:, k, cols], start=False, stop=False)
                    last = nc.tensor.matmul(dst[:], wlo[br][:, k], hT_hi[:, k, cols], start=False, stop=(k == KD - 1))
                return last

            def body(j, last):
                def gates(h, n):
                    c = (2 * j + h) * NH + n
                    if h == 0 and n == 0:
                        pe.wait_ge(gw_lo_done, j + 1)
                    pe.wait_ge(xbl_done, c + 1)
                    if at_least(j, 1) or c >= 1:
                        pe.wait_ge(ti_ready, c)
                    for g, dst in ((0, pr), (1, pi)):
                        nc.tensor.matmul(dst[:], gwh[:, g], XBh[:], start=True, stop=False)
                        nc.tensor.matmul(dst[:], gwh[:, g], XBl[:], start=False, stop=False)
                        last_mm = nc.tensor.matmul(dst[:], gwl[:, g], XBh[:], start=False, stop=True)
                    last_mm.then_inc(gate_mm, 1)

                for h in range(2):
                    hh = 2 * j + h
                    if h == 0:
                        pe.wait_ge(lo_done["x"], j + 1)
                    for n in range(NH):
                        if at_least(j, 1) or h:
                            pe.wait_ge(xu_ready, hh * NH + n - 1)
                        project("x", px[n], (h * NH + n) * NB).then_inc(x_mm, 1)
                    if h == 0:
                        pe.wait_ge(lo_done["g"], j + 1)
                    for n in range(NH):
                        if at_least(j, 1) or h:
                            pe.wait_ge(gelu, hh * NH + n - 1)
                        if n == 0:
                            project("g", pg[n], (h * NH + n) * NB, range(KD // 2))
                            gates(h, 0)
                            project("g", pg[n], (h * NH + n) * NB, range(KD // 2, KD)).then_inc(g_mm, 1)
                            gates(h, 1)
                        else:
                            project("g", pg[n], (h * NH + n) * NB).then_inc(g_mm, 1)
                pe.wait_ge(ma, KD * j + KD)
                if at_least(j, 1):
                    pe.wait_ge(mrow_ready, j)
                nc.tensor.matmul(pmod[:], cst["ones"][:], macc[:], start=True, stop=True).then_inc(msum, 1)
            channels(pe, body)


def out_and_norm(nc, sem, cst, io, x2, y_dram, mod_dram, hn2_dram, g2row, logits):
    ctx = ExitStack()
    with ctx:
        sb = lambda n, s, d=F32: ctx.enter_context(nc.sbuf_tensor(n, s, d))
        ps = lambda n, s: ctx.enter_context(nc.psum_tensor(n, s, F32))
        wr = x2[:, NT - KD:NT, :]
        g1row, sh2, sc2 = sb("g1row", [P, D]), sb("sh2", [P, D]), sb("sc2", [P, D])
        rw = sb("router_w", [P, KD, E])
        rb = sb("router_b", [P, E])
        wo_hi, wo_lo = sb("wo_hi", [P, KD, D], F32R), sb("wo_lo", [P, KD, D], F32R)
        yt, xr = sb("b_yt", [P, 2, D]), sb("b_xr", [P, 2, D])
        yh = [sb(f"b_yh{u}", [P, D], F32R) for u in range(2)]
        yl = [sb(f"b_yl{u}", [P, D], F32R) for u in range(2)]
        hn = sb("b_hn", [P, 2, D])
        hT = sb("b_hT", [P, D])
        gain = hT
        ssq, std, rstd = sb("b_ssq", [P, 2]), sb("b_std", [P, 2]), sb("b_rstd", [P, 2])
        po = [ps("po0", [P, D]), ps("po1", [P, D])]
        pt = ps("b_pt", [P, D])
        pl = ps("pl", [P, NB])
        junk = pt[:]

        g1_in, rows_in, sc2_ready = sem("g1_in"), sem("b_rows_in"), sem("sc2_ready")
        wr_in = [sem(f"wr_in{k}") for k in range(KD)]
        wo_h, wo_l = sem("wo_h"), sem("wo_l")
        y_in = [sem("by_in0"), sem("by_in1")]
        x_in = [sem("bx_in0"), sem("bx_in1")]
        yhi, ylo, mm, gated, resid = sem("b_yhi"), sem("b_ylo"), sem("b_mm"), sem("b_gated"), sem("b_resid")
        sqd, stdd, rec, scaled, shifted = sem("b_sq"), sem("b_std_s"), sem("b_rec"), sem("b_scaled"), sem("b_shifted")
        turned, hT_ready, routed, logit = sem("b_turned"), sem("b_hT_s"), sem("b_routed"), sem("b_logit")
        stored = [sem("b_stored0"), sem("b_stored1")]
        last_tile = lambda it: isinstance(it, int) and it == NT - 1
        w_v = io["lru_w_out"][0].rearrange("(k p) n -> k p n", p=P)
        y_v = y_dram.rearrange("t p j n -> t p (j n)")
        block = ctx.enter_context(nc.Block())

        @block.sync
        def _(sp):
            def load(it, u):
                if at_least(it, 2):
                    sp.wait_ge(ylo, it - 1)
                sp.dma_start(yt[:, u], y_v[ds(it, 1)].rearrange("o p n -> (o p) n")).then_inc(y_in[u], 16)
                if not at_least(it, 1):
                    for k in range(KD):
                        sp.dma_start(wr[:, k], w_v[k]).then_inc(wr_in[k], 16)
                if at_least(it, 2):
                    sp.wait_ge(resid, it - 1)
                sp.dma_start(xr[:, u], io["x"][0, ds(it * P, P), :]).then_inc(x_in[u], 16)
                if at_least(it, 1) and not at_least(it, 2):
                    for q, dst in enumerate((g1row, sh2, sc2, g2row)):
                        sp.dma_start(dst[:], mod_dram[0, q * D:(q + 1) * D].partition_broadcast(P))\
                            .then_inc(g1_in if q == 0 else rows_in, 16)
                    sp.dma_start(gain[:], io["norm2_g"][0].partition_broadcast(P)).then_inc(rows_in, 16)
                    sp.dma_start(rw[:], io["router_w"].rearrange("(k p) e -> p k e", p=P)).then_inc(rows_in, 16)
                    sp.dma_start(rb[:], io["router_b"].partition_broadcast(P)).then_inc(rows_in, 16)

            def store(it, u):
                sp.wait_ge(shifted, it + 1)
                sp.dma_start(hn2_dram[ds(it * P, P), :], hn[:, u]).then_inc(stored[u], 16)
            pipelined(sp, NT, 6, [(load, 0), (store, 4)])
            for u in range(2):
                sp.wait_ge(stored[u], 16 * NT // 2)

        @block.scalar
        def _(act):
            def high(it, u):
                act.wait_ge(y_in[u], it * 8 + 16 - u * 8)
                if at_least(it, 2):
                    act.wait_ge(mm, it - 1)
                nc.scalar.activation(yh[u][:], yt[:, u], ACT.Copy).then_inc(yhi, 1)
                if not at_least(it, 1):
                    for k in range(KD):
                        act.wait_ge(wr_in[k], 16)
                        nc.scalar.activation(wo_hi[:, k], wr[:, k], ACT.Copy).then_inc(wo_h, 1)

            def squares(it, u):
                act.wait_ge(resid, it + 1)
                if at_least(it, 2):
                    act.wait_ge(rec, it - 1)
                act.nop(nofuse=True)
                nc.scalar.activation(hn[:, u], x2[:, ds(it, 1)].rearrange("p o n -> p (o n)"), ACT.Square,
                                     accum_out=ssq[:, u:u + 1]).then_inc(sqd, 1)
                act.wait_ge(sqd, it + 1)
                nc.scalar.activation(std[:, u:u + 1], ssq[:, u:u + 1], ACT.Sqrt, scale=1.0 / D,
                                     bias=cst["eps"][:]).then_inc(stdd, 1)

            def squares_free(it, u):
                if at_least(it, 2):
                    act.wait_ge(turned, it - 1)
                    act.wait_ge(stored[u], it * 8 - u * 8)
                squares(it, u)

            def evacuate(it, u):
                act.wait_ge(turned, it + 1)
                if at_least(it, 1):
                    act.wait_ge(routed, it)
                nc.scalar.activation(hT[:], pt[:], ACT.Copy).then_inc(hT_ready, 1)
            pipelined(act, NT, 6, [(high, 0), (squares_free, 2), (evacuate, 4)])

        @block.vector
        def _(dve):
            def low(it, u):
                dve.wait_ge(yhi, it + 1)
                if at_least(it, 2):
                    dve.wait_ge(mm, it - 1)
                nc.vector.tensor_tensor(yl[u][:], yt[:, u], yh[u][:].bitcast(F32), ALU.subtract).then_inc(ylo, 1)
                if not at_least(it, 1):
                    for k in range(KD):
                        dve.wait_ge(wo_h, k + 1)
                        nc.vector.tensor_tensor(wo_lo[:, k], wr[:, k], wo_hi[:, k].bitcast(F32), ALU.subtract)\
                            .then_inc(wo_l, 1)

            def gate(it, u):
                dve.wait_ge(mm, it + 1)
                if not at_least(it, 1):
                    dve.wait_ge(g1_in, 16)
                x2t = x2[:, ds(it, 1)].rearrange("p o n -> p (o n)")
                nc.vector.tensor_tensor(x2t, po[u][:], g1row[:], ALU.mult).then_inc(gated, 1)
                if last_tile(it):
                    dve.wait_ge(gated, it + 1)
                    dve.wait_ge(x_in[u], 16 * NT // 2)
                    dve.wait_ge(resid, it)
                    nc.vector.tensor_tensor(x2t, x2t, xr[:, u], ALU.add).then_inc(resid, 1)

            def norm(it, u):
                if not at_least(it, 1):
                    dve.wait_ge(rows_in, 16 * 6)
                    nc.vector.scalar_tensor_tensor(sc2[:], sc2[:], 1.0, gain[:], ALU.add, ALU.mult).then_inc(sc2_ready, 1)
                    dve.wait_ge(sc2_ready, 1)
                dve.wait_ge(stdd, it + 1)
                nc.vector.reciprocal(rstd[:, u:u + 1], std[:, u:u + 1]).then_inc(rec, 1)
                dve.wait_ge(rec, it + 1)
                nc.vector.scalar_tensor_tensor(hn[:, u], x2[:, ds(it, 1)].rearrange("p o n -> p (o n)"),
                                               rstd[:, u:u + 1], sc2[:], ALU.mult, ALU.mult).then_inc(scaled, 1)
                if last_tile(it):
                    dve.wait_ge(scaled, it + 1)
                    dve.wait_ge(shifted, it)
                    nc.vector.tensor_tensor(hn[:, u], hn[:, u], sh2[:], ALU.add).then_inc(shifted, 1)

            def bias(it, u):
                dve.wait_ge(routed, it + 1)
                nc.vector.tensor_tensor(logits[:, ds(it, 1)].rearrange("p o n -> p (o n)"), pl[:, 0:E], rb[:],
                                        ALU.add).then_inc(logit, 1)
            pipelined(dve, NT, 6, [(low, 0), (gate, 1), (norm, 2), (bias, 4)])

        @block.gpsimd
        def _(pool):
            def add_x(it, u):
                if last_tile(it):
                    return
                pool.wait_ge(gated, it + 1)
                pool.wait_ge(x_in[u], it * 8 + 16 - u * 8)
                x2t = x2[:, ds(it, 1)].rearrange("p o n -> p (o n)")
                nc.gpsimd.tensor_tensor(x2t, x2t, xr[:, u], ALU.add).then_inc(resid, 1)

            def shift(it, u):
                if last_tile(it):
                    return
                pool.wait_ge(scaled, it + 1)
                nc.gpsimd.tensor_tensor(hn[:, u], hn[:, u], sh2[:], ALU.add).then_inc(shifted, 1)
            pipelined(pool, NT, 4, [(add_x, 1), (shift, 2)])

        @block.tensor
        def _(pe):
            def main(it, u, half):
                if half == 0:
                    pe.wait_ge(ylo, it + 1)
                    if at_least(it, 2):
                        pe.wait_ge(gated, it - 1)
                if at_least(it, 1):
                    products = [(k, half) for k in range(KD)]
                elif half == 0:
                    products = [(k, h) for k in range(KD) for h in range(2)]
                else:
                    return
                for k, h in products:
                    tok, cols = slice(k * P, (k + 1) * P), slice(h * NB, (h + 1) * NB)
                    if not at_least(it, 1):
                        pe.wait_ge(wo_l, k + 1)
                    nc.tensor.matmul(po[u][:, cols], yh[u][:, tok], wo_hi[:, k, cols], start=(k == 0), stop=False)
                    nc.tensor.matmul(po[u][:, cols], yh[u][:, tok], wo_lo[:, k, cols], start=False, stop=False)
                    last = nc.tensor.matmul(po[u][:, cols], yl[u][:, tok], wo_hi[:, k, cols], start=False, stop=(k == KD - 1))
                if half == 1 or not at_least(it, 1):
                    last.then_inc(mm, 1)

            def turn(it, u):
                pe.wait_ge(shifted, it + 1)
                if at_least(it, 1):
                    pe.wait_ge(hT_ready, it)
                for k in range(KD):
                    last = nc.tensor.transpose(pt[:, k * P:(k + 1) * P], hn[:, u, k * P:(k + 1) * P], cst["ident"][:])
                last.then_inc(turned, 1)

            def route(it, u):
                pe.wait_ge(hT_ready, it + 1)
                if at_least(it, 1):
                    pe.wait_ge(logit, it)
                for k in range(KD):
                    last = nc.tensor.matmul(pl[:, 0:E], hT[:, k * P:(k + 1) * P], rw[:, k], start=(k == 0), stop=(k == KD - 1))
                last.then_inc(routed, 1)
            pipelined(pe, NT, 4, [(lambda it, u: main(it, u, 0), 0), (turn, 3),
                                  (lambda it, u: main(it, u, 1), 0), (route, 3)])


DOWN = KD * 2 * FE
NQ = 4
QW = WE // NQ
QLOADS = (2, 2, 3, 2)


def load_quarter(sp, io, w, e, q):
    raw, arrived = w["raw"][:, q % 2, :], w["in"][q]
    KQ = QW // (2 * FE)
    src = lambda t: io[t][0, ds(e, 1)].rearrange("o (k p) f -> p (o k) f", p=P)
    if q < 3:
        ks = slice(q * KQ, min((q + 1) * KQ, KD))
        nk = ks.stop - ks.start
        dst = raw[:, 0:nk * 2 * FE].rearrange("p (k a f) -> p k a f", k=nk, a=2)
        sp.dma_start(dst[:, :, 0], src("moe_w_gate")[:, ks]).then_inc(arrived, 16)
        sp.dma_start(dst[:, :, 1], src("moe_w_up")[:, ks]).then_inc(arrived, 16)
    down = src("moe_w_down")
    if q == 2:
        sp.dma_start(raw[:, nk * 2 * FE:], down[:, 0, 0:QW - nk * 2 * FE]).then_inc(arrived, 16)
    if q == 3:
        sp.dma_start(raw[:, 0:NB], down[:, 0, NB:D]).then_inc(arrived, 16)
        sp.dma_start(raw[:, NB:], down[:, 1]).then_inc(arrived, 16)


def dispatch(nc, sem, cst, io, logits, tab, w, yslot_dram, g2row):
    ctx = ExitStack()
    with ctx:
        sb = lambda n, s, d=F32: ctx.enter_context(nc.sbuf_tensor(n, s, d))
        ps = lambda n, s: ctx.enter_context(nc.psum_tensor(n, s, F32))
        prob, work, work2 = [sb(n, [P, NT, E]) for n in ("prob", "work", "work2")]
        chosen = sb("chosen", [P, 3, NT, E])
        oh1, oh2, mask = [chosen[:, i] for i in range(3)]
        mx, m1, m2, vm = [sb(n, [P, NT]) for n in ("d_mx", "d_m1", "d_m2", "d_vm")]
        gs, gq = sb("d_gs", [P, NT, G]), sb("d_gq", [P, NT, G])
        larger, smaller = sb("larger", [P, NT * G, 2]), sb("smaller", [P, NT * G, 2])
        gates = sb("d_gates", [P, TOPK, NT])
        below = sb("below", [P, P])
        slot_no, block_no = sb("slot_no", [P, P]), sb("block_no", [P, MAXB])
        rank_w, thresh = sb("rank_w", [P, E]), sb("thresh", [P, E])
        cnt, nblk, ends, start, ones_e = [sb(n, [P, E]) for n in ("cnt", "nblk", "ends", "start", "ones_e")]
        first, sole, second, flag = [sb(n, [P, MAXB]) for n in ("d_first", "d_sole", "d_second", "d_flag")]
        ones_b = sb("ones_b", [P, MAXB])
        cmp = sb("cmp", [P, E, E])
        upto, keep = sb("upto", [P, E, NT]), sb("keep", [P, E, NT])
        assert 3 * NT == MAXB
        cmpb = chosen[:].rearrange("p i t e -> p (i t) e")
        eb, par = sb("eb", [P, MAXB]), sb("par", [P, MAXB])
        pari = sb("pari", [P, MAXB], I32)
        posf = sb("posf", [P, TOPK, NT])
        ri, bi = sb("ri", [P, TOPK * NT], I32), sb("bi", [P, TOPK * NT], I32)
        rf, bf = sb("rf", [P, TOPK * NT]), sb("bf", [P, TOPK * NT])
        tok2 = sb("tok2", [P, TOPK * NT])
        NP, PB = 4, 3
        pick = [sb(f"pick{u}", [P, NP, P]) for u in range(PB)]
        place = sb("place", [P, PB, NP, 2, MAXB])
        prank, ptot, pslot = ps("prank", [P, NB]), ps("ptot", [P, NB]), ps("pslot", [P, NB])

        consts, dve_done, exp_in, exp_out = sem("d_consts"), sem("d_step"), sem("exp_in"), sem("exp_out")
        mask_ready, ranked, picked, slotted = sem("mask_ready"), sem("ranked"), sem("picked"), sem("slotted")
        CONSTS = 9
        block_hot, placed = sem("block_hot"), sem("placed")
        below_set, keep_set = sem("below_set"), sem("keep_set")
        ends_ready, filled = sem("ends_ready"), sem("yslot_filled")
        gate2 = gates[:].rearrange("p c t -> p (c t)")
        wide = lambda a, k: a.unsqueeze(2).to_broadcast([a.shape[0], a.shape[1], k])
        row = lambda a, k: a.unsqueeze(1).to_broadcast([P, k, a.shape[-1]])
        block = ctx.enter_context(nc.Block())

        @block.gpsimd
        def _(pool):
            nc.gpsimd.memset(below[:], 1.0).then_inc(below_set, 1)
            nc.gpsimd.memset(ones_e[:], 1.0).then_inc(consts, 1)
            nc.gpsimd.memset(ones_b[:], 1.0).then_inc(consts, 1)
            nc.gpsimd.memset(keep[:], 1.0).then_inc(keep_set, 1)
            pool.wait_ge(keep_set, 1)
            nc.gpsimd.memset(keep[:, :, 0:1], 0.0).then_inc(consts, 1)
            pool.wait_ge(below_set, 1)
            nc.gpsimd.affine_select(out=below[:], in_=below[:], compare_op=ALU.is_gt, fill=0.0, base=0,
                                    pattern=[[1, P]], channel_multiplier=-1).then_inc(consts, 1)
            io_ = lambda t, pat, base, cm: nc.gpsimd.iota(t, pat, base=base, channel_multiplier=cm,
                                                          allow_small_or_imprecise_dtypes=True).then_inc(consts, 1)
            io_(slot_no[:], [[1, P]], 0, 0)
            io_(block_no[:], [[1, MAXB]], 0, 0)
            io_(rank_w[:], [[-1, E]], E, 0)
            io_(thresh[:], [[P, E]], 0, 0)
            io_(tok2[:], [[0, TOPK], [P, NT]], 0, 1)
            for q in range(NQ):
                cols = slice(q * QW, (q + 1) * QW)
                pool.wait_ge(w["hi_done"], q + 1)
                nc.gpsimd.tensor_tensor(w["lo"][:, cols], w["raw"][:, q % 2], w["hi"][:, cols].bitcast(F32),
                                        ALU.subtract).then_inc(w["lo_done"][q % 2], 1)
            for b in range(TOPK * NT // NP):
                cols, u = slice(b * NP, (b + 1) * NP), b % PB
                pool.wait_ge(block_hot, b + 1)
                nc.gpsimd.tensor_tensor(place[:, u, :, 0], place[:, u, :, 1], wide(tok2[:, cols], MAXB),
                                        ALU.mult).then_inc(placed, 1)
                pool.wait_ge(placed, 2 * b + 1)
                nc.gpsimd.tensor_tensor(place[:, u, :, 1], place[:, u, :, 1], wide(gate2[:, cols], MAXB),
                                        ALU.mult).then_inc(placed, 1)

        @block.sync
        def _(sp):
            for q in range(NQ):
                if q >= 2:
                    sp.wait_ge(w["lo_done"][q % 2], q // 2)
                load_quarter(sp, io, w, 0, q)
            for q in range(2):
                sp.wait_ge(w["lo_done"][q % 2], 2)
                load_quarter(sp, io, w, 1, q)
            sp.wait_ge(ends_ready, 1)
            used = sp.value_load(tab["ends"][0:1, E - 1:E], min_val=E, max_val=MAXB)
            unused = sp.value_load(tab["unused"][0:1, 0:1], min_val=1, max_val=MAXB + 1)
            with sp.Fori(used, MAXB + 1) as b:
                sp.dma_start(yslot_dram[ds(b * P, P), :], g2row[:]).then_inc(filled, 16)
            sp.wait_ge(filled, unused * 16)
            sp.nop(nofuse=True)

        @block.scalar
        def _(act):
            act.wait_ge(exp_in, 1)
            nc.scalar.activation(prob[:], work[:], ACT.Exp).then_inc(exp_out, 1)
            for q in range(NQ):
                cols = slice(q * QW, (q + 1) * QW)
                act.wait_ge(w["in"][q], 16 * QLOADS[q])
                nc.scalar.activation(w["hi"][:, cols], w["raw"][:, q % 2], ACT.Copy).then_inc(w["hi_done"], 1)

        @block.vector
        def _(dve):
            n = [0]
            v = nc.vector

            def done(ins):
                n[0] += 1
                ins.then_inc(dve_done, 1)
                dve.wait_ge(dve_done, n[0])

            done(v.tensor_reduce(mx[:], logits[:], AX.X, ALU.max))
            v.tensor_tensor(work[:], logits[:], wide(mx[:], E), ALU.subtract).then_inc(exp_in, 1)
            dve.wait_ge(exp_out, 1)
            done(v.tensor_reduce(mx[:], prob[:], AX.X, ALU.add))
            done(v.reciprocal(vm[:], mx[:]))
            done(v.tensor_tensor(prob[:], prob[:], wide(vm[:], E), ALU.mult))
            assert PER == 4
            pairs = prob[:].rearrange("p t (g c m) -> p (t g) c m", c=2, m=2)
            done(v.tensor_tensor(larger[:], pairs[:, :, :, 0], pairs[:, :, :, 1], ALU.max))
            v.tensor_tensor(smaller[:], pairs[:, :, :, 0], pairs[:, :, :, 1], ALU.min).then_inc(dve_done, 1)
            n[0] += 1
            tg = lambda a: a.rearrange("p t g -> p (t g)")
            done(v.tensor_tensor(tg(gs[:]), larger[:, :, 0], larger[:, :, 1], ALU.max))
            done(v.tensor_tensor(tg(gq[:]), larger[:, :, 0], larger[:, :, 1], ALU.min))
            done(v.tensor_tensor(larger[:, :, 0], smaller[:, :, 0], smaller[:, :, 1], ALU.max))
            done(v.tensor_tensor(tg(gq[:]), tg(gq[:]), larger[:, :, 0], ALU.max))
            done(v.tensor_tensor(gs[:], gs[:], gq[:], ALU.add))
            dve.wait_ge(consts, CONSTS)

            def first_of(out, vals, top, k):
                done(v.tensor_reduce(top, vals, AX.X, ALU.max))
                done(v.tensor_tensor(out, vals, wide(top, k), ALU.is_equal))
                done(v.tensor_tensor(out, out, row(rank_w[:, 0:k], NT), ALU.mult))
                done(v.tensor_reduce(vm[:], out, AX.X, ALU.max))
                done(v.tensor_tensor(out, out, wide(vm[:], k), ALU.is_equal))
            first_of(gq[:], gs[:], mx[:], G)
            inb = gq[:].rearrange("p t g -> p (t g)")
            w3 = work[:].rearrange("p t (g m) -> p (t g) m", m=PER)
            p3 = prob[:].rearrange("p t (g m) -> p (t g) m", m=PER)
            done(v.tensor_tensor(w3, p3, wide(inb, PER), ALU.mult))
            done(v.tensor_scalar(gq[:], gq[:], -1.0, None, ALU.add))
            done(v.tensor_tensor(w3, w3, wide(inb, PER), ALU.add))
            first_of(oh1, work[:], m1[:], E)
            done(v.scalar_tensor_tensor(work2[:], oh1, -4.0, work[:], ALU.mult, ALU.add))
            first_of(oh2, work2[:], m2[:], E)
            v.tensor_tensor(mask, oh1, oh2, ALU.add).then_inc(mask_ready, 1)
            done(v.tensor_tensor(mx[:], m1[:], m2[:], ALU.add))
            done(v.reciprocal(vm[:], mx[:]))
            done(v.tensor_tensor(gates[:, 0], m1[:], vm[:], ALU.mult))
            done(v.tensor_tensor(gates[:, 1], m2[:], vm[:], ALU.mult))
            done(v.memset(thresh[:, 0:1], -1.0))
            dve.wait_ge(ranked, 1)
            tot = ptot[:, 0:NT * E].rearrange("p (t e) -> p e t", e=E)
            by_expert = work2[:].rearrange("p t e -> p (t e)")
            done(v.tensor_copy(by_expert.rearrange("p (e t) -> p e t", t=NT), tot))
            done(v.tensor_tensor_scan(upto[:].rearrange("p e t -> p (e t)"), keep[:].rearrange("p e t -> p (e t)"),
                                      by_expert, 0.0, ALU.mult, ALU.add))
            done(v.tensor_tensor(cmp[:], upto[:, :, NT - 1:NT].to_broadcast([P, E, E]), row(thresh[:], E), ALU.is_gt))
            done(v.tensor_reduce(nblk[:], cmp[:], AX.X, ALU.add))
            done(v.tensor_tensor_scan(ends[:], ones_e[:], nblk[:], 0.0, ALU.mult, ALU.add))
            done(v.tensor_tensor(start[:], ends[:], nblk[:], ALU.subtract))
            done(v.scalar_tensor_tensor(upto[:], wide(start[:], NT), float(P), upto[:], ALU.mult, ALU.add))
            done(v.tensor_tensor(upto[:], upto[:], by_expert.rearrange("p (e t) -> p e t", t=NT), ALU.subtract))
            done(v.tensor_tensor(work[:], upto[:].rearrange("p e t -> p t e"),
                                 prank[:, 0:NT * E].rearrange("p (t e) -> p t e", e=E), ALU.add))
            for c, oh in enumerate((oh1, oh2)):
                done(v.tensor_tensor(work2[:], work[:], oh, ALU.mult))
                done(v.tensor_reduce(posf[:, c], work2[:], AX.X, ALU.add))
            pos_i = tab["pos"][:].rearrange("p c t -> p (c t)")
            done(v.tensor_copy(pos_i, posf[:].rearrange("p c t -> p (c t)")))
            done(v.tensor_scalar(ri[:], pos_i, P - 1, None, ALU.bitwise_and))
            done(v.tensor_scalar(bi[:], pos_i, P.bit_length() - 1, None, ALU.logical_shift_right))
            done(v.tensor_copy(bf[:], bi[:]))
            done(v.tensor_copy(rf[:], ri[:]))

            done(v.tensor_copy(tab["ends"][:], ends[:]))
            done(v.tensor_scalar(tab["unused"][:], ends[:, E - 1:E], -1.0, float(MAXB + 1), ALU.mult, ALU.add))
            v.tensor_scalar(tab["blocks_less"][:], ends[:, E - 1:E], -float(LEAD), None, ALU.add).then_inc(ends_ready, 1)

            def factors(b):
                cols = slice(b * NP, (b + 1) * NP)
                if b >= PB:
                    dve.wait_ge(slotted, (b - PB + 1) * NP)
                v.tensor_tensor(place[:, b % PB, :, 1], row(block_no[:], NP), wide(bf[:, cols], MAXB),
                                ALU.is_equal).then_inc(block_hot, 1)
                v.tensor_tensor(pick[b % PB][:], row(slot_no[:], NP), wide(rf[:, cols], P),
                                ALU.is_equal).then_inc(picked, 1)
            assert TOPK * NT // NP == 8
            factors(0)
            factors(1)
            factors(2)
            done(v.tensor_tensor(cmpb, wide(block_no[:], E), row(ends[:], MAXB), ALU.is_ge))
            done(v.tensor_reduce(eb[:], cmpb, AX.X, ALU.add))
            factors(3)
            done(v.tensor_copy(tab["expert"][:], eb[:]))
            done(v.tensor_scalar(pari[:], tab["expert"][:], 1, None, ALU.bitwise_and))
            done(v.tensor_scalar(tab["woff"][:], pari[:], float(WE), None, ALU.mult))
            done(v.tensor_scalar(tab["woff_next"][:], pari[:], -float(WE), float(WE), ALU.mult, ALU.add))
            factors(4)
            v.memset(first[:, 0:1], 1.0).then_inc(dve_done, 1)
            v.memset(second[:], 0.0).then_inc(dve_done, 1)
            n[0] += 2
            done(v.tensor_tensor(first[:, 1:], eb[:, 1:], eb[:, 0:MAXB - 1], ALU.subtract))
            done(v.tensor_scalar(flag[:], eb[:], float(E - 1), None, ALU.is_lt))
            done(v.tensor_tensor(sole[:, 0:MAXB - 1], first[:, 0:MAXB - 1], first[:, 1:], ALU.mult))
            factors(5)
            done(v.tensor_scalar(par[:], first[:], -1.0, 1.0, ALU.mult, ALU.add))
            done(v.tensor_tensor(second[:, 1:], first[:, 0:MAXB - 1], par[:, 1:], ALU.mult))
            done(v.tensor_tensor(second[:, 0:MAXB - 1], second[:, 0:MAXB - 1], sole[:, 0:MAXB - 1], ALU.add))
            done(v.tensor_tensor(tab["split1"][:], second[:], flag[:], ALU.mult))
            factors(6)
            done(v.tensor_tensor(tab["split0"][:], first[:], flag[:], ALU.mult))
            done(v.tensor_tensor(par[:], first[:], block_no[:], ALU.mult))
            factors(7)
            done(v.tensor_tensor_scan(sole[:], ones_b[:], par[:], 1.0, ALU.mult, ALU.max))
            done(v.tensor_copy(tab["before"][:], sole[:]))
            done(v.tensor_scalar(tab["expert1"][:], eb[:], 1.0, None, ALU.add))
            dve.wait_ge(slotted, TOPK * NT)
            done(v.tensor_copy(tab["slot_token"][:], pslot[:, 0:MAXB]))
            done(v.tensor_scalar(tab["slot_gate"][:], pslot[:, MAXB:2 * MAXB], 0.5, None, ALU.mult))

        @block.tensor
        def _(pe):
            pe.wait_ge(consts, CONSTS)
            pe.wait_ge(mask_ready, 1)
            m2d = mask.rearrange("p t e -> p (t e)")
            nc.tensor.matmul(prank[:, 0:NT * E], below[:], m2d, start=True, stop=True)
            nc.tensor.matmul(ptot[:, 0:NT * E], cst["ones"][:], m2d, start=True, stop=True).then_inc(ranked, 1)

            N = TOPK * NT
            for it in range(N):
                if it % NP == 0:
                    pe.wait_ge(picked, it // NP + 1)
                    pe.wait_ge(placed, 2 * (it // NP) + 2)
                nc.tensor.matmul(pslot[:, 0:2 * MAXB], pick[it // NP % PB][:, it % NP],
                                 place[:, it // NP % PB, it % NP].rearrange("p a b -> p (a b)"),
                                 start=(it == 0), stop=(it == N - 1)).then_inc(slotted, 1)


def experts(nc, sem, cst, io, tab, w, hn2_dram, yslot_dram, g2row):
    ctx = ExitStack()
    with ctx:
        sb = lambda n, s, d=F32: ctx.enter_context(nc.sbuf_tensor(n, s, d))
        ps = lambda n, s: ctx.enter_context(nc.psum_tensor(n, s, F32))
        xg = sb("e_xg", [P, D])
        xh, xl = sb("e_xh", [P, D], F32R), sb("e_xl", [P, D], F32R)
        ah, al = sb("e_ah", [P, FE], F32R), sb("e_al", [P, FE], F32R)
        th, av = sb("e_th", [P, FE]), sb("e_av", [P, FE])
        ysb = sb("e_y", [P, D])
        idx = sb("e_idx", [P, 1], I32)
        gu, tp, pa, pd = ps("e_gu", [P, NB]), ps("e_tp", [P, D]), ps("e_pa", [P, NB]), ps("e_pd", [P, D])

        idx_ready = sem("idx_ready")
        gathered, turned, xh_ready, xl_ready = sem("gathered"), sem("e_turned"), sem("xh_ready"), sem("xl_ready")
        gu_mm, th_ready, tmp_ready, av_ready = sem("gu_mm"), sem("th_ready"), sem("tmp_ready"), sem("av_ready")
        av_turned, ah_ready, al_ready = sem("av_turned"), sem("ah_ready"), sem("al_ready")
        d_mm, y_ready, y_out = sem("d_mm"), sem("ey_ready"), sem("ey_out")
        KF = FE // P
        HX = D // 2
        block = ctx.enter_context(nc.Block())
        blocks_less = lambda eng: eng.value_load(tab["blocks_less"][0:1, 0:1], min_val=E - LEAD, max_val=MAXB - LEAD)

        def per_block(eng, name, b, lo, hi):
            return eng.value_load(tab[name][0:1, ds(b, 1)], min_val=lo, max_val=hi)

        @block.sync
        def _(sp):
            for q in range(2, NQ):
                sp.wait_ge(w["lo_done"][q % 2], 3)
                load_quarter(sp, io, w, 1, q)
            with sp.Fori(2, E) as e:
                for q in range(NQ):
                    sp.wait_ge(w["lo_done"][q % 2], 2 * e + q // 2)
                    load_quarter(sp, io, w, e, q)

        def low_w(eng, tensor_tensor, b, odd, dues=None):
            for part in range(2):
                due = dues[part] if dues else per_block(eng, f"split{part}", b, 0, 1)
                with eng.If(due == 1):
                    e = per_block(eng, "expert1", b, 1, E - 1)
                    off = per_block(eng, "woff_next", b, 0, WE)
                    q = 2 * part + odd
                    eng.wait_ge(w["hi_done"], NQ * e + (q + 1))
                    eng.nop(nofuse=True)
                    tensor_tensor(w["lo"][:, ds(off + q * QW, QW)], w["raw"][:, q % 2],
                                  w["hi"][:, ds(off + q * QW, QW)].bitcast(F32),
                                  ALU.subtract).then_inc(w["lo_done"][odd], 1)

        @block.gpsimd
        def _(pool):
            nless = blocks_less(pool)

            def gather(b, first=False):
                if not first:
                    pool.wait_ge(turned, b)
                pool.nop(nofuse=True)
                nc.gpsimd.tensor_copy(idx[:], tab["slot_token"][:, ds(b, 1)]).then_inc(idx_ready, 1)
                pool.wait_ge(idx_ready, b + 1)
                pool.nop(nofuse=True)
                pool.indirect_dma_start(xg[:], None, hn2_dram, bass.IndirectOffsetOnAxis(ap=idx[:], axis=0))\
                    .then_inc(gathered, 16)
            gather(0, True)
            gather(1)
            gather(2)
            low_w(pool, nc.gpsimd.tensor_tensor, 0, 1)
            with pool.Fori(0, nless) as i:
                gather(i + LEAD)
                low_w(pool, nc.gpsimd.tensor_tensor, i + 1, 1)
            low_w(pool, nc.gpsimd.tensor_tensor, nless + 1, 1)
            low_w(pool, nc.gpsimd.tensor_tensor, nless + 2, 1)

        @block.scalar
        def _(act):
            nless = blocks_less(act)

            def tanh(b):
                act.wait_ge(gu_mm, b + 1)
                nc.scalar.activation(th[:], gu[:, 0:FE], ACT.Tanh, scale=0.5).then_inc(th_ready, 1)

            def high_x(b):
                act.wait_ge(turned, b + 1)
                for h in range(2):
                    cols = slice(h * HX, (h + 1) * HX)
                    nc.scalar.activation(xh[:, cols], tp[:, cols], ACT.Copy).then_inc(xh_ready, 1)

            def high_a(b):
                act.wait_ge(av_turned, b + 1)
                nc.scalar.activation(ah[:], pa[:, 0:FE], ACT.Copy).then_inc(ah_ready, 1)

            def high_w(b, first=False):
                for part in range(2):
                    due = per_block(act, f"split{part}", b, 0, 1)
                    with act.If(due == 1):
                        e = per_block(act, "expert1", b, 1, E - 1)
                        off = per_block(act, "woff_next", b, 0, WE)
                        if not first:
                            before = per_block(act, "before", b, 1, MAXB)
                            act.wait_ge(d_mm, before)
                        for q in (2 * part, 2 * part + 1):
                            act.wait_ge(w["in"][q], (e + 1) * (16 * QLOADS[q]))
                            act.nop(nofuse=True)
                            nc.scalar.activation(w["hi"][:, ds(off + q * QW, QW)], w["raw"][:, q % 2],
                                                 ACT.Copy).then_inc(w["hi_done"], 1)

            def store(b):
                act.wait_ge(y_ready, b + 1)
                act.dma_start(yslot_dram[ds(b * P, P), :], ysb[:]).then_inc(y_out, 16)
            high_x(0)
            tanh(0)
            high_x(1)
            high_w(0, True)
            high_a(0)
            tanh(1)
            high_x(2)
            high_w(1)
            with act.Fori(0, nless) as i:
                high_a(i + 1)
                tanh(i + 2)
                store(i)
                high_x(i + 3)
                high_w(i + 2)
            high_a(nless + 1)
            tanh(nless + 2)
            store(nless)
            high_w(nless + 2)
            store(nless + 1)
            high_a(nless + 2)
            store(nless + 2)
            act.wait_ge(y_out, (nless + LEAD) * 16)
            act.nop(nofuse=True)

        @block.vector
        def _(dve):
            nless = blocks_less(dve)

            def act_product(b):
                dve.wait_ge(th_ready, b + 1)
                nc.vector.scalar_tensor_tensor(th[:], th[:], 1.0, gu[:, 0:FE], ALU.add, ALU.mult).then_inc(tmp_ready, 1)
                dve.wait_ge(tmp_ready, b + 1)
                nc.vector.tensor_tensor(av[:], th[:], gu[:, FE:2 * FE], ALU.mult).then_inc(av_ready, 1)

            def low_x(b):
                for h in range(2):
                    cols = slice(h * HX, (h + 1) * HX)
                    dve.wait_ge(xh_ready, 2 * b + h + 1)
                    nc.vector.tensor_tensor(xl[:, cols], tp[:, cols], xh[:, cols].bitcast(F32), ALU.subtract)\
                        .then_inc(xl_ready, 1)

            def low_a(b):
                dve.wait_ge(ah_ready, b + 1)
                nc.vector.tensor_tensor(al[:], pa[:, 0:FE], ah[:].bitcast(F32), ALU.subtract).then_inc(al_ready, 1)

            def y_scaled(b, first=False):
                dve.wait_ge(d_mm, b + 1)
                if not first:
                    dve.wait_ge(y_out, b * 16)
                nc.vector.scalar_tensor_tensor(ysb[:], pd[:], tab["slot_gate"][:, ds(b, 1)], g2row[:],
                                               ALU.mult, ALU.mult).then_inc(y_ready, 1)
            low_x(0)
            act_product(0)
            low_x(1)
            low_w(dve, nc.vector.tensor_tensor, 0, 0)
            low_a(0)
            act_product(1)
            low_x(2)
            y_scaled(0, True)
            low_w(dve, nc.vector.tensor_tensor, 1, 0)
            with dve.Fori(0, nless) as i:
                low_a(i + 1)
                act_product(i + 2)
                low_x(i + 3)
                dues = [per_block(dve, f"split{part}", i + 2, 0, 1) for part in range(2)]
                y_scaled(i + 1)
                low_w(dve, nc.vector.tensor_tensor, i + 2, 0, dues)
            low_a(nless + 1)
            act_product(nless + 2)
            y_scaled(nless + 1)
            low_w(dve, nc.vector.tensor_tensor, nless + 2, 0)
            low_a(nless + 2)
            y_scaled(nless + 2)

        @block.tensor
        def _(pe):
            nless = blocks_less(pe)

            def turn(b):
                pe.wait_ge(gathered, (b + 1) * 16)
                for k in range(KD):
                    last = nc.tensor.transpose(tp[:, k * P:(k + 1) * P], xg[:, k * P:(k + 1) * P], cst["ident"][:])
                last.then_inc(turned, 1)

            def gate_up(b, first=False, turn_before=False):
                e = per_block(pe, "expert", b, 0, E - 1)
                off = per_block(pe, "woff", b, 0, WE)
                if not first:
                    pe.wait_ge(av_ready, b)
                for k in range(KD):
                    if k * 2 * FE % QW == 0:
                        q = k * 2 * FE // QW
                        pe.wait_ge(w["lo_done"][q % 2], e * 2 + (q // 2 + 1))
                    if k % (KD // 2) == 0:
                        pe.wait_ge(xl_ready, 2 * b + 2 * k // KD + 1)
                    tok = slice(k * P, (k + 1) * P)
                    hi, lo = [w[n][:, ds(off + k * 2 * FE, 2 * FE)] for n in ("hi", "lo")]
                    if k == KD - 2 and turn_before:
                        turn_act(b - 1)
                    nc.tensor.matmul(gu[:], xh[:, tok], hi, start=(k == 0), stop=False)
                    nc.tensor.matmul(gu[:], xh[:, tok], lo, start=False, stop=False)
                    last = nc.tensor.matmul(gu[:], xl[:, tok], hi, start=False, stop=(k == KD - 1))
                last.then_inc(gu_mm, 1)

            def turn_act(b):
                pe.wait_ge(av_ready, b + 1)
                for k in range(KF):
                    last = nc.tensor.transpose(pa[:, k * P:(k + 1) * P], av[:, k * P:(k + 1) * P], cst["ident"][:])
                last.then_inc(av_turned, 1)

            def down(b, first=False):
                e = per_block(pe, "expert", b, 0, E - 1)
                off = per_block(pe, "woff", b, 0, WE)
                pe.wait_ge(w["lo_done"][1], e * 2 + 2)
                pe.wait_ge(al_ready, b + 1)
                if not first:
                    pe.wait_ge(y_ready, b)
                for half in range(D // NB):
                    dst = pd[:, half * NB:(half + 1) * NB]
                    for k in range(KF):
                        tok = slice(k * P, (k + 1) * P)
                        hi, lo = [w[n][:, ds(off + (DOWN + k * D + half * NB), NB)] for n in ("hi", "lo")]
                        nc.tensor.matmul(dst, ah[:, tok], hi, start=(k == 0), stop=False)
                        nc.tensor.matmul(dst, ah[:, tok], lo, start=False, stop=False)
                        last = nc.tensor.matmul(dst, al[:, tok], hi, start=False, stop=(k == KF - 1))
                last.then_inc(d_mm, 1)
            turn(0)
            gate_up(0, True)
            turn(1)
            gate_up(1)
            turn_act(0)
            turn(2)
            down(0, True)
            with pe.Fori(0, nless) as i:
                gate_up(i + 2, turn_before=True)
                turn(i + 3)
                down(i + 1)
            gate_up(nless + 2)
            turn_act(nless + 1)
            down(nless + 1)
            turn_act(nless + 2)
            down(nless + 2)


def combine(nc, sem, cst, io, tab, x2, yslot_dram, out):
    ctx = ExitStack()
    with ctx:
        sb = lambda n, s, d=F32: ctx.enter_context(nc.sbuf_tensor(n, s, d))
        ps = lambda n, s: ctx.enter_context(nc.psum_tensor(n, s, F32))
        B = 4
        ya, yb, ob = sb("f_ya", [P, B, D]), sb("f_yb", [P, B, D]), sb("f_ob", [P, B, D])
        fg = sb("f_g", [P, D])
        ssq, std, rstd = sb("f_ssq", [P, B]), sb("f_std", [P, B]), sb("f_rstd", [P, B])
        junk = ps("f_junk", [P, D])
        idx = [sb(f"f_idx{u}", [P, TOPK], I32) for u in range(B)]
        fg_in, idx_ready = sem("f_in"), sem("f_idx_ready")
        pair_in, stored = [[sem(f"f_{n}{u}") for u in range(B)] for n in ("pair_in", "st")]
        pair, summed, sqd, stdd, rec, normed = [sem("f_" + n) for n in ("pair", "summed", "sqd", "stdd", "rec", "normed")]
        block = ctx.enter_context(nc.Block())
        tile = lambda it: x2[:, ds(it, 1)].rearrange("p o n -> p (o n)")

        @block.gpsimd
        def _(pool):
            def gather(it, u):
                if at_least(it, B):
                    pool.wait_ge(summed, it - (B - 1))
                pool.nop(nofuse=True)
                nc.gpsimd.tensor_copy(idx[u][:].rearrange("p (c o) -> p c o", o=1), tab["pos"][:, :, ds(it, 1)])\
                    .then_inc(idx_ready, 1)
                pool.wait_ge(idx_ready, it + 1)
                pool.nop(nofuse=True)
                for c, buf in enumerate((ya, yb)):
                    pool.indirect_dma_start(buf[:, u], None, yslot_dram,
                                            bass.IndirectOffsetOnAxis(ap=idx[u][:, c:c + 1], axis=0)).then_inc(pair_in[u], 16)
            pipelined(pool, NT, B, [(gather, 0)], B)

        @block.sync
        def _(sp):
            sp.dma_start(fg[:], io["final_norm_g"].partition_broadcast(P)).then_inc(fg_in, 16)

            def store(it, u):
                sp.wait_ge(normed, it + 1)
                sp.dma_start(out[0, ds(it * P, P), :], ob[:, u]).then_inc(stored[u], 16)
            pipelined(sp, NT, B, [(store, 0)], B)
            for u in range(B):
                sp.wait_ge(stored[u], NT // B * 16)

        @block.scalar
        def _(act):
            def squares(it, u):
                act.wait_ge(summed, it + 1)
                if at_least(it, B):
                    act.wait_ge(rec, it - (B - 1))
                act.nop(nofuse=True)
                nc.scalar.activation(junk[:], tile(it), ACT.Square, accum_out=ssq[:, u:u + 1]).then_inc(sqd, 1)
                act.wait_ge(sqd, it + 1)
                nc.scalar.activation(std[:, u:u + 1], ssq[:, u:u + 1], ACT.Sqrt, scale=1.0 / D,
                                     bias=cst["eps"][:]).then_inc(stdd, 1)
            pipelined(act, NT, B, [(squares, 0)], B)

        @block.vector
        def _(dve):
            def add(it, u):
                dve.wait_ge(pair_in[u], it * 8 + 32 - u * 8)
                nc.vector.tensor_tensor(ya[:, u], ya[:, u], yb[:, u], ALU.add).then_inc(pair, 1)
                dve.wait_ge(pair, it + 1)
                nc.vector.tensor_tensor(tile(it), tile(it), ya[:, u], ALU.add).then_inc(summed, 1)

            def norm(it, u):
                dve.wait_ge(stdd, it + 1)
                nc.vector.reciprocal(rstd[:, u:u + 1], std[:, u:u + 1]).then_inc(rec, 1)
                dve.wait_ge(rec, it + 1)
                if at_least(it, B):
                    dve.wait_ge(stored[u], it * 4 - u * 4)
                nc.vector.scalar_tensor_tensor(ob[:, u], tile(it), rstd[:, u:u + 1], fg[:], ALU.mult, ALU.mult)\
                    .then_inc(normed, 1)
            dve.wait_ge(fg_in, 16)
            pipelined(dve, NT, B, [(add, 0), (norm, 1)], B)


def build(nc, io, out):
    ctx = ExitStack()
    with ctx:
        sb = lambda n, s, d=F32: ctx.enter_context(nc.sbuf_tensor(n, s, d))
        sem = lambda n: ctx.enter_context(nc.semaphore(n))
        cst = {"ident": sb("ident", [P, P]), "ones": sb("ones", [P, P]), "eps": sb("eps", [P, 1])}
        cond = sb("cond", [P, KD])
        y_dram = nc.dram_tensor("y_scratch", (NT, P, KD, P), F32, kind="Internal").ap()
        mod_dram = nc.dram_tensor("mod_scratch", (1, 4 * D), F32, kind="Internal").ap()
        hn2_dram = nc.dram_tensor("hn2_scratch", (S, D), F32, kind="Internal").ap()
        made, cleared = sem("const_made"), sem("ident_cleared")
        with nc.Block() as block:
            @block.gpsimd
            def _(pool):
                nc.gpsimd.memset(cst["ident"][:], 0.0).then_inc(cleared, 1)
                nc.gpsimd.memset(cst["ones"][:], 1.0).then_inc(made, 1)
                nc.gpsimd.memset(cst["eps"][:], EPS).then_inc(made, 1)
                pool.wait_ge(cleared, 1)
                nc.gpsimd.affine_select(out=cst["ident"][:], in_=cst["ident"][:], compare_op=ALU.not_equal, fill=1.0,
                                        base=0, pattern=[[-1, P]], channel_multiplier=1).then_inc(made, 1)
                pool.wait_ge(made, 3)
        with nc.sbuf_tensor("hT_hi", [P, KD, S], F32R) as hT_hi, nc.sbuf_tensor("hT_lo", [P, KD, S], F32R) as hT_lo:
            with nc.sbuf_tensor("raw_x", [P, KD, P], F32) as raw_x, nc.sbuf_tensor("conv_w", [P, KD, CONV], F32) as cw, \
                    nc.sbuf_tensor("conv_b", [P, KD], F32) as cb, nc.sbuf_tensor("gate_b", [P, 2, KD], F32) as gb, \
                    nc.sbuf_tensor("lam", [P, KD], F32) as lam, nc.sbuf_tensor("decay", [P, 2, KD], F32) as dec:
                pre = {"vec_in": sem("vec_in"), "raw_x": raw_x, "raw_x_in": sem("raw_x_in"), "cw": cw, "cb": cb, "gb": gb, "lam": lam, "dec": dec}
                norm_and_transpose(nc, sem, cst, io, hT_hi, hT_lo, cond, pre)
                lru(nc, sem, cst, io, hT_hi, hT_lo, cond, pre, y_dram, mod_dram)
        x2 = sb("x2", [P, NT, D])
        g2row = sb("g2row", [P, D])
        logits = sb("logits", [P, NT, E])
        out_and_norm(nc, sem, cst, io, x2, y_dram, mod_dram, hn2_dram, g2row, logits)
        tab = {"blocks_less": sb("t_blocks_less", [P, 1], I32), "unused": sb("t_unused", [P, 1], I32), "ends": sb("t_ends", [P, E], I32), "pos": sb("t_pos", [P, TOPK, NT], I32),
               "expert": sb("t_expert", [P, MAXB], I32), "expert1": sb("t_expert1", [P, MAXB], I32), "woff": sb("t_woff", [P, MAXB], I32),
               "woff_next": sb("t_woff_next", [P, MAXB], I32),
               "before": sb("t_before", [P, MAXB], I32), "split0": sb("t_split0", [P, MAXB], I32), "split1": sb("t_split1", [P, MAXB], I32),
               "slot_token": sb("t_slot_token", [P, MAXB], I32), "slot_gate": sb("t_slot_gate", [P, MAXB])}
        yslot_dram = nc.dram_tensor("yslot_scratch", ((MAXB + 1) * P, D), F32, kind="Internal").ap()
        with nc.sbuf_tensor("w_hi", [P, 2 * WE], F32R) as w_hi, nc.sbuf_tensor("w_lo", [P, 2 * WE], F32R) as w_lo, \
                nc.sbuf_tensor("w_raw", [P, 2, QW], F32) as w_raw:
            w = {"hi": w_hi, "lo": w_lo, "raw": w_raw, "in": [sem(f"raw_in{q}") for q in range(NQ)],
                 "hi_done": sem("w_hi_done"), "lo_done": [sem("w_lo_done0"), sem("w_lo_done1")]}
            dispatch(nc, sem, cst, io, logits, tab, w, yslot_dram, g2row)
            experts(nc, sem, cst, io, tab, w, hn2_dram, yslot_dram, g2row)
        combine(nc, sem, cst, io, tab, x2, yslot_dram, out)


_INS = ["x", "c", "ada_w", "ada_b", "norm1_g", "norm2_g", "lru_w_in", "lru_conv_w", "lru_conv_b", "lru_wa", "lru_ba",
        "lru_wx", "lru_bx", "lru_lambda", "lru_w_out", "router_w", "router_b", "moe_w_gate", "moe_w_up", "moe_w_down",
        "final_norm_g"]


def kernel(**inputs):
    import numpy as _np
    import concourse.bacc as _bacc
    from concourse import mybir as _mybir
    from concourse.bass_utils import run_bass_kernel_spmd as _run

    nc = _bacc.Bacc("TRN2", target_bir_lowering=False, num_devices=1)
    arrays, io = {}, {}
    for name in _INS:
        a = _np.ascontiguousarray(inputs[name])
        arrays[f"in_{name}_dram"] = a
        io[name] = nc.dram_tensor(f"in_{name}_dram", a.shape, _mybir.dt.from_np(a.dtype), kind="ExternalInput").ap()
    out = nc.dram_tensor("out_0_dram", (1, S, D), _mybir.dt.float32, kind="ExternalOutput").ap()
    build(nc, io, out)
    r = _run(nc, [arrays], core_ids=[0])
    return r.results[0]["out_0_dram"]
```
